# Optimizing a Trainium2 kernel written in Bass

```python
import jax, jax.numpy as jnp
from jax import lax
import numpy as np
import math

D_MODEL = 1024
BATCH = 1
SEQ = 1024
DEPTH = 1

CTX_LEN = 256
GRID_W = 64
D_MIX = D_MODEL
D_GMLP = D_MIX // 2
G_A = 4
GA_DIM = D_GMLP // G_A
CHUNK_A = 2 * GRID_W
D_MLSTM = D_MIX - D_GMLP
H_B = 4
HV = D_MLSTM // H_B
HK = HV // 2
D_QK = H_B * HK
CONV_W = 3
CHUNK_B = 128
N_GATES = 4 * H_B
D_IN = 2 * D_GMLP + 2 * D_QK + 2 * D_MLSTM + N_GATES
D_FF = 4 * D_MODEL
ALPHA = (2 * DEPTH) ** 0.25
BETA = (8 * DEPTH) ** -0.25
LN_EPS = 1e-5


def _ln_stats(x):
    xf = x.astype(jnp.float32)
    mu = jnp.mean(xf, axis=-1, keepdims=True)
    var = jnp.mean(jnp.square(xf - mu), axis=-1, keepdims=True)
    return (xf - mu) * lax.rsqrt(var + LN_EPS)

def layer_norm(x, g, b):
    return (_ln_stats(x) * g + b).astype(x.dtype)

def modulate(x, shift, scale):
    return _ln_stats(x).astype(x.dtype) * (1 + scale) + shift

def ada_split(cond, w_ada, b_ada):
    return jnp.split(jax.nn.silu(cond) @ w_ada + b_ada, 6, axis=-1)

def split_proj(p):
    bounds = [D_GMLP, 2 * D_GMLP, 2 * D_GMLP + D_QK, 2 * D_GMLP + 2 * D_QK,
              2 * D_GMLP + 2 * D_QK + D_MLSTM, 2 * D_GMLP + 2 * D_QK + 2 * D_MLSTM]
    return jnp.split(p, bounds, axis=-1)

def spatial_gating(u, v, w_s, b_s, g_v, b_v):
    bsz, s, _ = v.shape
    vc = layer_norm(v, g_v, b_v).reshape(bsz, s // CHUNK_A, CHUNK_A, G_A, GA_DIM)
    mixed = jnp.einsum('gts,bnsgd->bntgd', w_s, vc) + b_s.T[:, :, None]
    return u * mixed.reshape(bsz, s, D_GMLP)

def short_conv(x, w):
    pad = CONV_W // 2
    return lax.conv_general_dilated(
        x, w[:, None, :], window_strides=(1,), padding=[(pad, pad)],
        dimension_numbers=('NWC', 'WIO', 'NWC'), feature_group_count=x.shape[-1])

def mlstm_inputs(q, k, vv, gates, conv_w, b_gates):
    bsz, s, _ = q.shape
    qk = jax.nn.silu(short_conv(jnp.concatenate([q, k], axis=-1), conv_w))
    q, k = jnp.split(qk, 2, axis=-1)
    heads = lambda a, d: a.reshape(bsz, s, H_B, d).transpose(0, 2, 1, 3)
    g = (gates + b_gates).reshape(bsz, s, 4, H_B).transpose(2, 0, 3, 1)
    return heads(q, HK), heads(k, HK), heads(vv, HV), g

def mlstm_chunkwise(q, k, v, ig, fg, state):
    bsz, nh, s, _ = q.shape
    nc = s // CHUNK_B
    f32 = jnp.float32
    q = q.astype(f32) * (HK ** -0.5)
    k = k.astype(f32)
    v = v.astype(f32)
    ig = ig.astype(f32)
    logf = jax.nn.log_sigmoid(fg.astype(f32))

    def to_chunks(a):
        return jnp.moveaxis(a.reshape(bsz, nh, nc, CHUNK_B, *a.shape[3:]), 2, 0)

    tri = jnp.tril(jnp.ones((CHUNK_B, CHUNK_B), dtype=bool))

    def step(carry, xs_c):
        c0, n0, m0 = carry
        qc, kc, vc, ic, lfc = xs_c
        b = jnp.cumsum(lfc, axis=-1)
        dmat = jnp.where(tri, b[..., :, None] - b[..., None, :] + ic[..., None, :], -jnp.inf)
        inter = b + m0[..., None]
        m = jnp.maximum(inter, jnp.max(dmat, axis=-1))
        w_intra = jnp.exp(dmat - m[..., None])
        w_inter = jnp.exp(inter - m)
        scores = jnp.einsum('bhtk,bhsk->bhts', qc, kc) * w_intra
        num = (jnp.einsum('bhts,bhsv->bhtv', scores, vc)
               + w_inter[..., None] * jnp.einsum('bhtk,bhkv->bhtv', qc, c0))
        den = jnp.sum(scores, axis=-1) + w_inter * jnp.einsum('bhtk,bhk->bht', qc, n0)
        h = num / jnp.maximum(jnp.abs(den), jnp.exp(-m))[..., None]
        b_last = b[..., -1]
        dec = b_last[..., None] - b + ic
        m_new = jnp.maximum(b_last + m0, jnp.max(dec, axis=-1))
        w_s = jnp.exp(dec - m_new[..., None])
        carry_w = jnp.exp(b_last + m0 - m_new)
        c_new = carry_w[..., None, None] * c0 + jnp.einsum('bhs,bhsk,bhsv->bhkv', w_s, kc, vc)
        n_new = carry_w[..., None] * n0 + jnp.einsum('bhs,bhsk->bhk', w_s, kc)
        return (c_new, n_new, m_new), h

    xs = (to_chunks(q), to_chunks(k), to_chunks(v), to_chunks(ig), to_chunks(logf))
    state, hs = lax.scan(step, state, xs)
    h = jnp.moveaxis(hs, 0, 2).reshape(bsz, nh, s, HV)
    return h, state

def mlstm_bidirectional(ctx_in, lat_in):
    qc, kc, vc, gc = ctx_in
    ql, kl, vl, gl = lat_in
    bsz = ql.shape[0]
    f32 = jnp.float32
    zero = (jnp.zeros((bsz, H_B, HK, HV), f32), jnp.zeros((bsz, H_B, HK), f32), jnp.zeros((bsz, H_B), f32))
    flip = lambda a: jnp.flip(a, axis=2)
    hc_f, st_f = mlstm_chunkwise(qc, kc, vc, gc[0], gc[1], zero)
    hl_f, _ = mlstm_chunkwise(ql, kl, vl, gl[0], gl[1], st_f)
    hc_b, st_b = mlstm_chunkwise(flip(qc), flip(kc), flip(vc), flip(gc[2]), flip(gc[3]), zero)
    hl_b, _ = mlstm_chunkwise(flip(ql), flip(kl), flip(vl), flip(gl[2]), flip(gl[3]), st_b)
    return hc_f + flip(hc_b), hl_f + flip(hl_b)

def head_norm(h, g):
    bsz, nh, s, dv = h.shape
    y = _ln_stats(h).transpose(0, 2, 1, 3).reshape(bsz, s, nh * dv)
    return y * g

def mixer_output(u, v, h_b, o, w_s, b_s, ln_v_g, ln_v_b, hn_g, w_out):
    y_a = spatial_gating(u, v, w_s, b_s, ln_v_g, ln_v_b)
    y_b = head_norm(h_b, hn_g).astype(o.dtype) * jax.nn.sigmoid(o)
    return jnp.concatenate([y_a, y_b], axis=-1) @ w_out

def channel_mlp(h, w1, b1, w2, b2):
    return jnp.square(jax.nn.relu(h @ w1 + b1)) @ w2 + b2

def deepnorm_update(x, y, gate, g, b):
    return layer_norm(ALPHA * x + gate * y, g, b)

def first_inputs(seed: int = 0) -> dict:
    key = jax.random.key(seed)
    ks = jax.random.split(key, 28)
    nrm = lambda k, shape, s: jax.random.normal(k, shape, jnp.float32) * s
    L = DEPTH
    f_bias = jnp.linspace(3.0, 6.0, H_B, dtype=jnp.float32)
    b_gates = jnp.concatenate([
        nrm(ks[10], (L, H_B), 0.1), f_bias + nrm(ks[11], (L, H_B), 0.1),
        nrm(ks[12], (L, H_B), 0.1), f_bias + nrm(ks[13], (L, H_B), 0.1)], axis=-1)
    return {
        "x": nrm(ks[0], (BATCH, SEQ, D_MODEL), 1.0),
        "c": nrm(ks[1], (BATCH, D_MODEL), 1.0),
        "ctx": nrm(ks[2], (BATCH, CTX_LEN, D_MODEL), 1.0),
        "c_ctx": nrm(ks[3], (D_MODEL,), 1.0),
        "w_ada": nrm(ks[4], (L, D_MODEL, 6 * D_MODEL), D_MODEL ** -0.5),
        "b_ada": nrm(ks[5], (L, 6 * D_MODEL), 0.01),
        "w_in": nrm(ks[6], (L, D_MODEL, D_IN), D_MODEL ** -0.5),
        "w_s": nrm(ks[7], (L, G_A, CHUNK_A, CHUNK_A), CHUNK_A ** -0.5),
        "b_s": 1.0 + nrm(ks[8], (L, G_A, CHUNK_A), 0.01),
        "ln_v_g": 1.0 + nrm(ks[9], (L, D_GMLP), 0.01),
        "ln_v_b": nrm(ks[14], (L, D_GMLP), 0.01),
        "conv_qk": nrm(ks[15], (L, CONV_W, 2 * D_QK), CONV_W ** -0.5),
        "b_gates": b_gates,
        "hn_g": 1.0 + nrm(ks[16], (L, D_MLSTM), 0.01),
        "w_out": nrm(ks[17], (L, D_MIX, D_MODEL), BETA * D_MIX ** -0.5),
        "ln1_g": 1.0 + nrm(ks[18], (L, D_MODEL), 0.01),
        "ln1_b": nrm(ks[19], (L, D_MODEL), 0.01),
        "w1": nrm(ks[20], (L, D_MODEL, D_FF), D_MODEL ** -0.5),
        "b1": nrm(ks[21], (L, D_FF), 0.01),
        "w2": nrm(ks[22], (L, D_FF, D_MODEL), BETA * D_FF ** -0.5),
        "b2": nrm(ks[23], (L, D_MODEL), 0.01),
        "ln2_g": 1.0 + nrm(ks[24], (L, D_MODEL), 0.01),
        "ln2_b": nrm(ks[25], (L, D_MODEL), 0.01),
    }

def first_block(x, c, ctx, c_ctx, w_ada, b_ada, w_in, w_s, b_s, ln_v_g, ln_v_b, conv_qk, b_gates, hn_g,
              w_out, ln1_g, ln1_b, w1, b1, w2, b2, ln2_g, ln2_b):
    xc = ctx
    for l in range(DEPTH):
        sh1, sc1, g1, sh2, sc2, g2 = [m[:, None, :] for m in ada_split(c, w_ada[l], b_ada[l])]
        csh1, csc1, cg1, csh2, csc2, cg2 = ada_split(c_ctx, w_ada[l], b_ada[l])

        u_l, v_l, q_l, k_l, vv_l, o_l, gt_l = split_proj(modulate(x, sh1, sc1) @ w_in[l])
        u_c, v_c, q_c, k_c, vv_c, o_c, gt_c = split_proj(modulate(xc, csh1, csc1) @ w_in[l])

        hb_c, hb_l = mlstm_bidirectional(
            mlstm_inputs(q_c, k_c, vv_c, gt_c, conv_qk[l], b_gates[l]),
            mlstm_inputs(q_l, k_l, vv_l, gt_l, conv_qk[l], b_gates[l]))

        y_l = mixer_output(u_l, v_l, hb_l, o_l, w_s[l], b_s[l], ln_v_g[l], ln_v_b[l], hn_g[l], w_out[l])
        x_new = deepnorm_update(x, y_l, g1, ln1_g[l], ln1_b[l])
        x_new = deepnorm_update(x_new, channel_mlp(modulate(x_new, sh2, sc2), w1[l], b1[l], w2[l], b2[l]),
                                g2, ln2_g[l], ln2_b[l])

        if l < DEPTH - 1:
            y_c = mixer_output(u_c, v_c, hb_c, o_c, w_s[l], b_s[l], ln_v_g[l], ln_v_b[l], hn_g[l], w_out[l])
            xc = deepnorm_update(xc, y_c, cg1, ln1_g[l], ln1_b[l])
            xc = deepnorm_update(xc, channel_mlp(modulate(xc, csh2, csc2), w1[l], b1[l], w2[l], b2[l]),
                                 cg2, ln2_g[l], ln2_b[l])
        x = x_new
    return x


_first_inputs = first_inputs


def first_inputs(seed=0):
    import zlib

    import numpy as np

    out = dict(_first_inputs(seed))
    spreads = {}
    factors = {'ctx': 5.289,
     'b_ada': 3.928,
     'b_s': 8.0,
     'ln_v_g': 8.0,
     'ln_v_b': 8.0,
     'hn_g': 8.0,
     'ln1_g': 5.768,
     'ln1_b': 5.735,
     'b1': 8.0,
     'b2': 8.0,
     'ln2_g': 5.662,
     'ln2_b': 5.61}
    for name, (base, spread) in spreads.items():
        noise = np.random.default_rng([zlib.crc32(name.encode()), seed]).standard_normal(out[name].shape)
        drawn = base * np.exp(spread * noise) if base else spread * noise
        out[name] = __import__('jax').numpy.asarray(drawn.astype(out[name].dtype))
    for name, factor in factors.items():
        out[name] = (out[name] * factor).astype(out[name].dtype)
    return out


_narrow_inputs = first_inputs


def first_inputs(seed=0):

    out = dict(_narrow_inputs(seed))
    wider = {'b_s': 10.87,
     'ln_v_g': 9.87,
     'ln_v_b': 10.3,
     'hn_g': 12.0,
     'ln1_g': 6.68,
     'ln1_b': 6.46,
     'b1': 7.36,
     'b2': 8.34,
     'ln2_g': 6.3,
     'ln2_b': 6.37}
    for name, times in wider.items():
        mean = out[name].mean()
        out[name] = (mean + times * (out[name] - mean)).astype(out[name].dtype)
    return out


DEPTH_2 = 2

HEAD_DIM = 64
ROT_DIM = HEAD_DIM // 4
ROPE_THETA = 500000.0
BLOCK = 128
NORM_EPS = 1e-6

RWKV_HEADS = 6
RWKV_WIDTH = RWKV_HEADS * HEAD_DIM
DECAY_RANK = 64
ICL_RANK = 64
GN_EPS = 64e-5
DECAY_SCALE = math.exp(-0.5)

DSA_HEADS = 4
DSA_WIDTH = DSA_HEADS * HEAD_DIM
IDX_HEADS = 8
IDX_DIM = 32
IDX_ROT_DIM = IDX_DIM // 4
DSA_TOPK = 256

DIL_WINDOWS = (128, 512, 2048)
DIL_RATES = (1, 4, 16)
DIL_GROUPS = 3
DIL_HEADS_PER_GROUP = 2
DIL_HEADS = DIL_GROUPS * DIL_HEADS_PER_GROUP
DIL_WIDTH = DIL_HEADS * HEAD_DIM

MIX_WIDTH = RWKV_WIDTH + DSA_WIDTH + DIL_WIDTH
PLE_DIM = 256

RWKV_COLS = (RWKV_WIDTH, RWKV_WIDTH, RWKV_WIDTH, RWKV_WIDTH, DECAY_RANK, ICL_RANK)
RWKV_IN_WIDTH = 4 * RWKV_WIDTH + DECAY_RANK + ICL_RANK
DSA_COLS = (DSA_WIDTH, HEAD_DIM, HEAD_DIM, IDX_HEADS * IDX_DIM, IDX_DIM, IDX_HEADS, DSA_WIDTH)
DSA_IN_WIDTH = 2 * DSA_WIDTH + 2 * HEAD_DIM + IDX_HEADS * IDX_DIM + IDX_DIM + IDX_HEADS
DIL_COLS = (DIL_WIDTH, DIL_WIDTH, DIL_WIDTH, DIL_WIDTH)
DIL_IN_WIDTH = 4 * DIL_WIDTH
IN_COLS = RWKV_IN_WIDTH + DSA_IN_WIDTH + DIL_IN_WIDTH


def rms_norm(x, g):
    xf = x.astype(jnp.float32)
    y = xf * lax.rsqrt(jnp.mean(xf * xf, axis=-1, keepdims=True) + NORM_EPS)
    return (y * g.astype(jnp.float32)).astype(x.dtype)

def split_cols(z, widths):
    out, off = [], 0
    for w in widths:
        out.append(z[..., off:off + w])
        off += w
    return out

def rope_tables(seq, rot_dim):
    half = rot_dim // 2
    inv = ROPE_THETA ** (-jnp.arange(half, dtype=jnp.float32) / half)
    ang = jnp.arange(seq, dtype=jnp.float32)[:, None] * inv[None, :]
    return jnp.cos(ang), jnp.sin(ang)

def partial_rope(x, cos, sin):
    half = cos.shape[-1]
    c = cos[None, :, None, :].astype(x.dtype)
    s = sin[None, :, None, :].astype(x.dtype)
    x1, x2, rest = x[..., :half], x[..., half:2 * half], x[..., 2 * half:]
    return jnp.concatenate([x1 * c - x2 * s, x2 * c + x1 * s, rest], axis=-1)

def token_shift_mix(z, mu):
    prev = jnp.pad(z, ((0, 0), (1, 0), (0, 0)))[:, :-1]
    return z + (prev - z) * mu

def rwkv7_branch(z, mu, w0, w_up, a0, a_up, k_k, k_a, r_k, ln_g, ln_b):
    B, S, _ = z.shape
    f32 = jnp.float32
    z = token_shift_mix(z, mu)
    r, k, v, g, wd, ad = split_cols(z, RWKV_COLS)
    heads = lambda t: t.astype(f32).reshape(B, S, RWKV_HEADS, HEAD_DIM)
    per_head = lambda t: t.astype(f32).reshape(RWKV_HEADS, HEAD_DIM)
    w = jnp.exp(-DECAY_SCALE * jax.nn.sigmoid((w0 + jnp.tanh(wd) @ w_up).astype(f32)))
    a = jax.nn.sigmoid((a0 + ad @ a_up).astype(f32))
    r, k, v, w, a = heads(r), heads(k), heads(v), heads(w), heads(a)
    kk = k * per_head(k_k)
    kk = kk / jnp.maximum(jnp.linalg.norm(kk, axis=-1, keepdims=True), 1e-12)
    k = k * (1.0 + (a - 1.0) * per_head(k_a))

    def step(state, inp):
        r_t, w_t, k_t, v_t, kk_t, a_t = inp
        sa = jnp.einsum('bhvk,bhk->bhv', state, -kk_t)
        state = (state * w_t[:, :, None, :]
                 + sa[..., None] * (kk_t * a_t)[:, :, None, :]
                 + v_t[..., None] * k_t[:, :, None, :])
        return state, jnp.einsum('bhvk,bhk->bhv', state, r_t)

    seq_first = lambda t: jnp.moveaxis(t, 1, 0)
    s0 = jnp.zeros((B, RWKV_HEADS, HEAD_DIM, HEAD_DIM), f32)
    _, y = lax.scan(step, s0, (seq_first(r), seq_first(w), seq_first(k), seq_first(v), seq_first(kk), seq_first(a)))
    y = jnp.moveaxis(y, 0, 1)
    mean = jnp.mean(y, axis=-1, keepdims=True)
    var = jnp.mean(jnp.square(y - mean), axis=-1, keepdims=True)
    y = ((y - mean) * lax.rsqrt(var + GN_EPS)).reshape(B, S, RWKV_WIDTH) * ln_g.astype(f32) + ln_b.astype(f32)
    bonus = jnp.sum(r * k * r_k.astype(f32), axis=-1, keepdims=True) * v
    y = y + bonus.reshape(B, S, RWKV_WIDTH)
    return (y * jax.nn.silu(g.astype(f32))).astype(z.dtype)

def dsa_branch(z, cos, sin, icos, isin):
    B, S, _ = z.shape
    f32 = jnp.float32
    q, k, v, iq, ik, iw, g = split_cols(z, DSA_COLS)
    q = partial_rope(q.reshape(B, S, DSA_HEADS, HEAD_DIM), cos, sin)
    k = partial_rope(k[:, :, None, :], cos, sin)[:, :, 0]
    iq = partial_rope(iq.reshape(B, S, IDX_HEADS, IDX_DIM), icos, isin)
    ik = partial_rope(ik[:, :, None, :], icos, isin)[:, :, 0]
    iw = iw * (IDX_HEADS ** -0.5)
    topk = min(DSA_TOPK, S // 4)
    nb = S // BLOCK
    key_pos = jnp.arange(S)
    gather = jax.vmap(lambda table, idx: table[idx])

    def block_fn(args):
        qb, iqb, iwb, start = args
        qpos = start + jnp.arange(BLOCK)
        sc = jnp.einsum('bqhd,bsd->bqhs', iqb, ik).astype(f32) * (IDX_DIM ** -0.5)
        sc = jnp.einsum('bqhs,bqh->bqs', jax.nn.relu(sc), iwb.astype(f32))
        sc = jnp.where((key_pos[None, :] <= qpos[:, None])[None], sc, -jnp.inf)
        _, idx = lax.top_k(sc, topk)
        valid = idx <= qpos[None, :, None]
        ks = gather(k, idx)
        vs = gather(v, idx)
        att = jnp.einsum('bqhd,bqkd->bqhk', qb, ks).astype(f32) * (HEAD_DIM ** -0.5)
        att = jnp.where(valid[:, :, None, :], att, -jnp.inf)
        probs = jax.nn.softmax(att, axis=-1).astype(vs.dtype)
        return jnp.einsum('bqhk,bqkd->bqhd', probs, vs)

    blocks = lambda t: jnp.moveaxis(t.reshape(B, nb, BLOCK, *t.shape[2:]), 1, 0)
    out = lax.map(block_fn, (blocks(q), blocks(iq), blocks(iw), jnp.arange(nb) * BLOCK))
    out = jnp.moveaxis(out, 0, 1).reshape(B, S, DSA_WIDTH)
    return out * jax.nn.silu(g)

def banded_attention(q, k, v, max_steps):
    N, n, H, dh = q.shape
    nb = -(-n // BLOCK)
    pad = nb * BLOCK - n
    to_blocks = lambda t: jnp.pad(t, ((0, 0), (0, pad), (0, 0), (0, 0))).reshape(N, nb, BLOCK, H, dh)
    qb, kb, vb = to_blocks(q), to_blocks(k), to_blocks(v)
    prev = lambda t: jnp.concatenate([jnp.zeros_like(t[:, :1]), t[:, :-1]], axis=1)
    kc = jnp.concatenate([prev(kb), kb], axis=2)
    vc = jnp.concatenate([prev(vb), vb], axis=2)
    s = jnp.einsum('nbqhd,nbkhd->nbhqk', qb, kc).astype(jnp.float32) * (HEAD_DIM ** -0.5)
    qi = jnp.arange(BLOCK)[:, None] + BLOCK
    kj = jnp.arange(2 * BLOCK)[None, :]
    dist = qi - kj
    band = (dist >= 0) & (dist <= max_steps)
    has_prev = (jnp.arange(nb)[:, None, None] > 0) | (kj[None] >= BLOCK)
    mask = band[None] & has_prev
    s = jnp.where(mask[None, :, None], s, -jnp.inf)
    m = jnp.max(s, axis=-1, keepdims=True)
    e = jnp.exp(s - m)
    l = jnp.sum(e, axis=-1, keepdims=True)
    o = jnp.einsum('nbhqk,nbkhd->nbqhd', (e / l).astype(v.dtype), vc)
    lse = (m + jnp.log(l))[..., 0]
    o = o.reshape(N, nb * BLOCK, H, dh)[:, :n]
    lse = jnp.moveaxis(lse, 2, 3).reshape(N, nb * BLOCK, H)[:, :n]
    return o, lse

def dilated_group(q, k, v, rate, steps):
    B, S, H, dh = q.shape
    n = S // rate
    to_res = lambda t: jnp.swapaxes(t.reshape(B, n, rate, H, dh), 1, 2).reshape(B * rate, n, H, dh)
    o, lse = banded_attention(to_res(q), to_res(k), to_res(v), steps)
    o = jnp.swapaxes(o.reshape(B, rate, n, H, dh), 1, 2).reshape(B, S, H, dh)
    lse = jnp.swapaxes(lse.reshape(B, rate, n, H), 1, 2).reshape(B, S, H)
    return o, lse

def dilated_branch(z, cos, sin):
    B, S, _ = z.shape
    q, k, v, g = split_cols(z, DIL_COLS)
    heads = lambda t: t.reshape(B, S, DIL_HEADS, HEAD_DIM)
    q = partial_rope(heads(q), cos, sin)
    k = partial_rope(heads(k), cos, sin)
    v = heads(v)
    outs, lses = [], []
    for gi in range(DIL_GROUPS):
        hs = slice(gi * DIL_HEADS_PER_GROUP, (gi + 1) * DIL_HEADS_PER_GROUP)
        o, lse = dilated_group(q[:, :, hs], k[:, :, hs], v[:, :, hs], DIL_RATES[gi], DIL_WINDOWS[gi] // DIL_RATES[gi])
        outs.append(o)
        lses.append(lse)
    o = jnp.stack(outs, axis=2)
    alpha = jax.nn.softmax(jnp.stack(lses, axis=2), axis=2)
    o = (o * alpha[..., None].astype(o.dtype)).reshape(B, S, DIL_WIDTH)
    return o * jax.nn.silu(g)

def second_inputs(seed: int = 0) -> dict:
    key = jax.random.key(seed)
    ks = jax.random.split(key, 20)
    f32 = jnp.float32
    nrm = lambda kk, shape, scale: scale * jax.random.normal(kk, shape, f32)
    L = DEPTH_2
    return {
        'x': nrm(ks[0], (BATCH, SEQ, D_MODEL), 1.0),
        'p': nrm(ks[1], (DEPTH_2, BATCH, SEQ, PLE_DIM), 1.0),
        'norm_g': 1.0 + nrm(ks[2], (L, D_MODEL), 0.05),
        'w_in': nrm(ks[3], (L, D_MODEL, IN_COLS), D_MODEL ** -0.5),
        'tshift_mu': jax.random.uniform(ks[4], (L, RWKV_IN_WIDTH), f32),
        'rwkv_w0': jax.random.uniform(ks[5], (L, RWKV_WIDTH), f32, -6.0, 1.0),
        'rwkv_w_up': nrm(ks[6], (L, DECAY_RANK, RWKV_WIDTH), DECAY_RANK ** -0.5),
        'rwkv_a0': nrm(ks[7], (L, RWKV_WIDTH), 0.5),
        'rwkv_a_up': nrm(ks[8], (L, ICL_RANK, RWKV_WIDTH), ICL_RANK ** -0.5),
        'rwkv_k_k': 0.85 + nrm(ks[9], (L, RWKV_WIDTH), 0.05),
        'rwkv_k_a': 1.0 + nrm(ks[10], (L, RWKV_WIDTH), 0.05),
        'rwkv_r_k': nrm(ks[11], (L, RWKV_HEADS, HEAD_DIM), 0.1),
        'rwkv_ln_g': 1.0 + nrm(ks[12], (L, RWKV_WIDTH), 0.05),
        'rwkv_ln_b': nrm(ks[13], (L, RWKV_WIDTH), 0.01),
        'w_out': nrm(ks[14], (L, MIX_WIDTH, D_MODEL), 0.5 * MIX_WIDTH ** -0.5),
        'ple_norm_g': 1.0 + nrm(ks[15], (L, D_MODEL), 0.05),
        'ple_w_gate': nrm(ks[16], (L, D_MODEL, D_MODEL), D_MODEL ** -0.5),
        'ple_w_proj': nrm(ks[17], (L, PLE_DIM, D_MODEL), 0.5 * PLE_DIM ** -0.5),
        'final_norm_g': 1.0 + nrm(ks[18], (D_MODEL,), 0.05),
    }

def second_block(x, p, norm_g, w_in, tshift_mu, rwkv_w0, rwkv_w_up, rwkv_a0, rwkv_a_up, rwkv_k_k, rwkv_k_a,
              rwkv_r_k, rwkv_ln_g, rwkv_ln_b, w_out, ple_norm_g, ple_w_gate, ple_w_proj, final_norm_g):
    S = x.shape[1]
    cos, sin = rope_tables(S, ROT_DIM)
    icos, isin = rope_tables(S, IDX_ROT_DIM)
    for i in range(DEPTH_2):
        h = rms_norm(x, norm_g[i])
        z = h @ w_in[i]
        z_a, z_b, z_c = split_cols(z, (RWKV_IN_WIDTH, DSA_IN_WIDTH, DIL_IN_WIDTH))
        y_a = rwkv7_branch(z_a, tshift_mu[i], rwkv_w0[i], rwkv_w_up[i], rwkv_a0[i], rwkv_a_up[i],
                           rwkv_k_k[i], rwkv_k_a[i], rwkv_r_k[i], rwkv_ln_g[i], rwkv_ln_b[i])
        y_b = dsa_branch(z_b, cos, sin, icos, isin)
        y_c = dilated_branch(z_c, cos, sin)
        y = jnp.concatenate([y_a, y_b, y_c], axis=-1)
        x = x + y @ w_out[i]
        gate = jax.nn.sigmoid(rms_norm(x, ple_norm_g[i]) @ ple_w_gate[i])
        x = x + gate * (p[i] @ ple_w_proj[i])
    return rms_norm(x, final_norm_g)


def setup_inputs(seed=0):
    out = dict(first_inputs(seed))
    for name, value in second_inputs(seed + 1).items():
        if name != "x":
            out[name + "_2"] = value
    return out


def reference(
    x, c, ctx, c_ctx, w_ada, b_ada, w_in, w_s, b_s, ln_v_g, ln_v_b, conv_qk, b_gates, hn_g,
    w_out, ln1_g, ln1_b, w1, b1, w2, b2, ln2_g, ln2_b, p_2, norm_g_2, w_in_2, tshift_mu_2,
    rwkv_w0_2, rwkv_w_up_2, rwkv_a0_2, rwkv_a_up_2, rwkv_k_k_2, rwkv_k_a_2, rwkv_r_k_2,
    rwkv_ln_g_2, rwkv_ln_b_2, w_out_2, ple_norm_g_2, ple_w_gate_2, ple_w_proj_2, final_norm_g_2,
):
    x = first_block(
        x, c, ctx, c_ctx, w_ada, b_ada, w_in, w_s, b_s, ln_v_g, ln_v_b, conv_qk, b_gates, hn_g,
        w_out, ln1_g, ln1_b, w1, b1, w2, b2, ln2_g, ln2_b,
    )
    return second_block(
        x, p_2, norm_g_2, w_in_2, tshift_mu_2, rwkv_w0_2, rwkv_w_up_2, rwkv_a0_2, rwkv_a_up_2,
        rwkv_k_k_2, rwkv_k_a_2, rwkv_r_k_2, rwkv_ln_g_2, rwkv_ln_b_2, w_out_2, ple_norm_g_2,
        ple_w_gate_2, ple_w_proj_2, final_norm_g_2,
    )


_drawn_inputs = setup_inputs


def setup_inputs(seed=0):
    import zlib

    import numpy as np

    out = dict(_drawn_inputs(seed))
    spreads = {}
    factors = {'norm_g_2': 8.0,
     'rwkv_w_up_2': 200.0,
     'rwkv_a0_2': 8.0,
     'rwkv_a_up_2': 4.734,
     'rwkv_k_k_2': 200.0,
     'rwkv_k_a_2': 8.0,
     'rwkv_r_k_2': 5.496,
     'rwkv_ln_g_2': 200.0,
     'rwkv_ln_b_2': 200.0,
     'ple_norm_g_2': 200.0,
     'p_2': 57.995,
     'rwkv_w0_2': 39.774,
     'ple_w_gate_2': 64.0,
     'ple_w_proj_2': 58.278}
    for name, (base, spread) in spreads.items():
        noise = np.random.default_rng([zlib.crc32(name.encode()), seed]).standard_normal(out[name].shape)
        drawn = base * np.exp(spread * noise) if base else spread * noise
        out[name] = __import__('jax').numpy.asarray(drawn.astype(out[name].dtype))
    for name, factor in factors.items():
        out[name] = (out[name] * factor).astype(out[name].dtype)
    return out
```

```python
from contextlib import ExitStack

import numpy as np
import concourse.bass as bass
from concourse import mybir

F32 = mybir.dt.float32
U8 = mybir.dt.uint8
ALU = mybir.AluOpType
ACT = mybir.ActivationFunctionType
X = mybir.AxisListType.X

P = 128
D = 1024
KC = D // P
SEQ = 1024
CTX = 256
NT = SEQ // P
NTC = CTX // P
DMA = 16
COL = 512

D_IN = 2576
H_B, HK, HV = 4, 64, 128
G_A, GA = 4, 128
D_FF = 4096
ALPHA = 2.0 ** 0.25
LN_EPS = 1e-5
VA = HV + 1
BIG = 1e30
ROW_CTX = 1
ROW_LAT = CTX + 3
ROWS_Z1 = CTX + SEQ + 4


START = 1


class Phase:

    def __init__(self, nc, name):
        self.nc, self.name, self.stack, self.sems = nc, name, ExitStack(), []

    def __enter__(self):
        return self

    def sb(self, name, shape, dt=F32):
        return self.stack.enter_context(self.nc.sbuf_tensor(f"{self.name}_{name}", shape, dt))

    def ps(self, name, shape, dt=F32):
        return self.stack.enter_context(self.nc.psum_tensor(f"{self.name}_{name}", shape, dt))

    def sem(self, name):
        s = self.stack.enter_context(self.nc.semaphore(f"{self.name}_{name}"))
        self.sems.append(s)
        self.nc.sync.sem_inc(s, START)
        return s

    def block(self):
        self.nc.all_engine_barrier()
        return self.nc.Block()

    def __exit__(self, *a):
        if a[0] is None:
            for s in self.sems:
                self.nc.sync.sem_clear(s)
        self.stack.close()


class Steps:

    def __init__(self, eng, sem, trip, per_trip):
        self.eng, self.sem, self.base, self.k, self.n = eng, sem, trip * per_trip, 0, per_trip

    def __call__(self, ins):
        self.k += 1
        ins.then_inc(self.sem, 1)
        self.eng.wait_ge(self.sem, START + self.base + self.k)

    def settle(self, passed):
        self.eng.sem_inc(passed, 1)

    def end(self):
        assert self.k == self.n, f"{self.k} steps in a trip, not {self.n}"


def rows_to_all(ap):
    return ap.partition_broadcast(P)


def columns(ap):
    return ap.rearrange("(k p) -> p k", p=P)


def bc_last(ap, n):
    return ap.unsqueeze(2).to_broadcast([ap.shape[0], ap.shape[1], n])


def bc_mid(ap, n):
    return ap.unsqueeze(1).to_broadcast([ap.shape[0], n, ap.shape[1]])


def ada_phase(nc, A, S):
    W = 6 * D
    NCH = W // COL
    with Phase(nc, "ada") as ph:
        cond = ph.sb("cond", [P, KC, 2])
        scond = ph.sb("scond", [P, KC, 2])
        bias = ph.sb("bias", [2, W])
        mod = ph.sb("mod", [2, W])
        w = ph.sb("w", [P, 2, KC, COL])
        acc = ph.ps("acc", [2, 2, COL])
        cond_in, cond_silu = ph.sem("cond_in"), ph.sem("cond_silu")
        w_in = [ph.sem("w_in0"), ph.sem("w_in1")]
        w_used = [ph.sem("w_used0"), ph.sem("w_used1")]
        summed = [ph.sem("summed0"), ph.sem("summed1")]
        stored = ph.sem("stored")
        w_v = A["w_ada"][0].rearrange("(k p) n -> p k n", p=P)
        with ph.block() as block:
            @block.sync
            def _(sp):
                sp.dma_start(cond[:, :, :], A["cond_cols"]).then_inc(cond_in, DMA)
                for r in range(2):
                    sp.dma_start(bias[r:r + 1, :], A["b_ada"]).then_inc(cond_in, DMA)
                with sp.Fori(0, NCH // 2) as i:
                    for j in range(2):
                        sp.wait_ge(w_used[j], START + i)
                        sp.dma_start(w[:, j, :, :], w_v[:, :, bass.ds((2 * i + j) * COL, COL)]).then_inc(w_in[j], DMA)
                for j in range(2):
                    sp.wait_ge(summed[j], START + NCH // 2)
                sp.dma_start(S["mod"], mod[:, :]).then_inc(stored, DMA)
                sp.wait_ge(stored, START + DMA)

            @block.scalar
            def _(act):
                act.wait_ge(cond_in, START + 3 * DMA)
                act.activation(scond[:, :, :], cond[:, :, :], ACT.Silu).then_inc(cond_silu, 1)

            @block.tensor
            def _(pe):
                pe.wait_ge(cond_silu, START + 1)
                with pe.Fori(0, NCH // 2) as i:
                    for j in range(2):
                        pe.wait_ge(w_in[j], START + DMA * i + DMA)
                        pe.wait_ge(summed[j], START + i)
                        for k in range(KC):
                            mm = pe.matmul(acc[:, j, :], scond[:, k, :], w[:, j, k, :], start=k == 0, stop=k == KC - 1)
                        mm.then_inc(w_used[j], 1)

            @block.vector
            def _(dve):
                dve.wait_ge(cond_in, START + 3 * DMA)
                with dve.Fori(0, NCH // 2) as i:
                    for j in range(2):
                        dve.wait_ge(w_used[j], START + i + 1)
                        cols = bass.ds((2 * i + j) * COL, COL)
                        dve.tensor_tensor(mod[:, cols], acc[:, j, :], bias[:, cols], ALU.add).then_inc(summed[j], 1)


def norm_transpose(nc, name, src, nt, hT, tok0, scale_row, shift_row, const, eps, center):
    with Phase(nc, name) as ph:
        ident = ph.sb("ident", [P, P])
        scale = ph.sb("scale", [P, KC])
        shift = ph.sb("shift", [P, KC])
        x = ph.sb("x", [P, 2, D])
        xn = ph.sb("xn", [P, 2, D])
        stats = ph.sb("stats", [P, 2, 6])
        mv = ph.sb("mv", [P, 2, 2])
        sd = ph.sb("sd", [P, 2])
        xT = ph.ps("xT", [P, 2, KC, P])
        const_in, x_in = ph.sem("const_in"), [ph.sem("x_in0"), ph.sem("x_in1")]
        step, var_ready, sd_ready = ph.sem("step"), ph.sem("var_ready"), ph.sem("sd_ready")
        normed, turned, placed = ph.sem("normed"), ph.sem("turned"), [ph.sem("placed0"), ph.sem("placed1")]
        scale_ready, passed = ph.sem("scale_ready"), ph.sem("passed")
        n_const = 1 + 1 + (shift_row is not None)
        with ph.block() as block:
            @block.sync
            def _(sp):
                sp.dma_start(ident[:, :], const["ident"]).then_inc(const_in, DMA)
                sp.dma_start(scale[:, :], columns(scale_row), allow_slow_non_contiguous=True).then_inc(const_in, DMA)
                if shift_row is not None:
                    sp.dma_start(shift[:, :], columns(shift_row), allow_slow_non_contiguous=True).then_inc(const_in, DMA)
                with sp.Fori(0, nt // 2) as i:
                    for j in range(2):
                        sp.wait_ge(placed[j], START + i)
                        sp.dma_start(x[:, j, :], src[bass.ds((2 * i + j) * P, P), :]).then_inc(x_in[j], DMA)

            @block.vector
            def _(dve):
                dve.wait_ge(const_in, START + n_const * DMA)
                if center:
                    dve.tensor_scalar(scale[:, :], scale[:, :], 1.0, None, ALU.add).then_inc(scale_ready, 1)
                with dve.Fori(0, nt // 2) as i:
                    for j in range(2):
                        s = Steps(dve, step, 2 * i + j, 5)
                        dve.wait_ge(x_in[j], START + DMA * i + DMA)
                        for q in range(2):
                            s(dve.bn_stats(stats[:, q, :], x[:, j, q * COL:(q + 1) * COL]))
                        s.settle(passed)
                        s(dve.bn_aggr(mv[:, j, :], stats[:, :, :]))
                        if center:
                            dve.tensor_scalar(sd[:, j:j + 1], mv[:, j, 1:2], eps, None, ALU.add).then_inc(var_ready, 1)
                        else:
                            s(dve.scalar_tensor_tensor(sd[:, j:j + 1], mv[:, j, 0:1], mv[:, j, 0:1], mv[:, j, 1:2], ALU.mult, ALU.add))
                            dve.tensor_scalar(sd[:, j:j + 1], sd[:, j:j + 1], eps, None, ALU.add).then_inc(var_ready, 1)
                        dve.wait_ge(sd_ready, START + 2 * i + j + 1)
                        s(dve.reciprocal(sd[:, j:j + 1], sd[:, j:j + 1]))
                        if center:
                            s(dve.tensor_scalar(xn[:, j, :], x[:, j, :], mv[:, j, 0:1], sd[:, j:j + 1], ALU.subtract, ALU.mult))
                            dve.sem_inc(normed, 1)
                        else:
                            dve.tensor_scalar(xn[:, j, :], x[:, j, :], sd[:, j:j + 1], None, ALU.mult).then_inc(normed, 1)
                        s.end()

            @block.scalar
            def _(act):
                if center:
                    act.wait_ge(scale_ready, START + 1)
                with act.Fori(0, nt // 2) as i:
                    for j in range(2):
                        act.wait_ge(var_ready, START + 2 * i + j + 1)
                        act.activation(sd[:, j:j + 1], sd[:, j:j + 1], ACT.Sqrt).then_inc(sd_ready, 1)
                        act.wait_ge(turned, START + 2 * i + j + 1)
                        for k in range(KC):
                            ins = act.activation(hT[:, k, bass.ds(tok0 + (2 * i + j) * P, P)], xT[:, j, k, :], ACT.Identity,
                                                 scale=scale[:, k:k + 1],
                                                 bias=shift[:, k:k + 1] if shift_row is not None else 0.0)
                        ins.then_inc(placed[j], 1)

            @block.tensor
            def _(pe):
                pe.wait_ge(const_in, START + n_const * DMA)
                with pe.Fori(0, nt // 2) as i:
                    for j in range(2):
                        pe.wait_ge(normed, START + 2 * i + j + 1)
                        for k in range(KC):
                            mm = pe.transpose(xT[:, j, k, :], xn[:, j, k * P:(k + 1) * P], ident[:, :])
                        mm.then_inc(turned, 1)


def product(nc, name, hT, nt, tok0, w, kc, chunks, looped):
    with Phase(nc, name) as ph:
        wt = ph.sb("wt", [P, 2, kc, COL])
        ot = ph.sb("ot", [P, 2, nt, COL])
        acc = ph.ps("acc", [P, 8, COL])
        w_in = [ph.sem("w_in0"), ph.sem("w_in1")]
        made = [ph.sem("made0"), ph.sem("made1")]
        out_v = [ph.sem("out_v0"), ph.sem("out_v1")]
        out_s = [ph.sem("out_s0"), ph.sem("out_s1")]
        stored = [ph.sem("stored0"), ph.sem("stored1")]
        w_v = w.rearrange("(k p) n -> p k n", p=P)
        half = (nt + 1) // 2
        bank = lambda j, t: (t if nt == 8 else j * nt + t)
        pairs = looped[0] if looped else 0
        tail = [(pairs + n // 2, n % 2) + c for n, c in enumerate(chunks)]

        def steps(eng, body):
            if pairs:
                with eng.Fori(0, pairs) as i:
                    for j in range(2):
                        body(i, j, looped[1](2 * i + j), COL, looped[2](2 * i + j))
            for trip, j, c, width, view in tail:
                body(trip, j, c, width, view)

        last = [0, 0]
        for j in range(2):
            last[j] = pairs + sum(1 for t in tail if t[1] == j)
        with ph.block() as block:
            @block.sync
            def _(sp):
                def load(trip, j, c, width, view):
                    sp.wait_ge(made[j], START + trip * nt)
                    sp.dma_start(wt[:, j, :, 0:width], w_v[:, :, bass.ds(c, width)]).then_inc(w_in[j], DMA)
                steps(sp, load)

            @block.tensor
            def _(pe):
                def body(trip, j, c, width, view):
                    pe.wait_ge(w_in[j], START + DMA * trip + DMA)
                    for t in range(nt):
                        out, n = (out_v, half) if t % 2 == 0 else (out_s, nt - half)
                        if nt == 8:
                            pe.wait_ge(out[1 - j], START + trip * n + (t // 2 + 1 if j else 0))
                        else:
                            pe.wait_ge(out[j], START + trip * n)
                        for k in range(kc):
                            mm = pe.matmul(acc[:, bank(j, t), 0:width], hT[:, k, (tok0 + t) * P:(tok0 + t + 1) * P],
                                           wt[:, j, k, 0:width], start=k == 0, stop=k == kc - 1)
                        mm.then_inc(made[j], 1)
                steps(pe, body)

            def copy_tiles(eng, copy, first, out_sem, trip, j, width):
                eng.wait_ge(stored[j], START + DMA * trip)
                for t in range(first, nt, 2):
                    eng.wait_ge(made[j], START + trip * nt + t + 1)
                    copy(ot[:, j, t, 0:width], acc[:, bank(j, t), 0:width]).then_inc(out_sem[j], 1)

            @block.vector
            def _(dve):
                def body(trip, j, c, width, view):
                    copy_tiles(dve, dve.tensor_copy, 0, out_v, trip, j, width)
                steps(dve, body)

            @block.scalar
            def _(act):
                def body(trip, j, c, width, view):
                    copy_tiles(act, act.copy, 1, out_s, trip, j, width)
                    act.wait_ge(out_v[j], START + (trip + 1) * half)
                    act.wait_ge(out_s[j], START + (trip + 1) * (nt - half))
                    act.dma_start(view, ot[:, j, :, 0:width]).then_inc(stored[j], DMA)
                steps(act, body)
                for j in range(2):
                    if last[j]:
                        act.wait_ge(stored[j], START + DMA * last[j])


def tiles(ap, cols):
    return ap[:, cols].rearrange("(t p) n -> p t n", p=P)


def mlstm_prep(nc, A, S, name, nt, row0, chunk0):
    z = S["z1"]
    NJ = 2 * H_B
    with Phase(nc, name) as ph:
        ident, ones = ph.sb("ident", [P, P]), ph.sb("ones", [P, P])
        upto, fromon = ph.sb("upto", [P, P]), ph.sb("fromon", [P, P])
        mask_ts, mask_st = ph.sb("mask_ts", [P, 2, P]), ph.sb("mask_st", [P, 2, P])
        cw = ph.sb("cw", [P, 3, 512])
        bg = ph.sb("bg", [P, 16])
        zq = ph.sb("zq", [P, 2, 3, 512])
        gt = ph.sb("gt", [P, 2, 16])
        va = ph.sb("va", [P, 2, H_B, VA])
        qk = ph.sb("qk", [P, 512])
        qkT = ph.sb("qkT", [P, 4, P])
        lf, lg = ph.sb("lf", [P, 16]), ph.sb("lg", [P, 16])
        sc = ph.sb("sc", [P, 4, NJ])
        a = ph.sb("a", [P, NJ])
        diag, am = ph.sb("diag", [P, NJ, P]), ph.sb("am", [P, NJ, P])
        wT = ph.sb("wT", [P, NJ, P])
        ea = ph.sb("ea", [P, NJ])
        kw = ph.sb("kw", [P, NJ, HK])
        num, own = ph.sb("num", [P, NJ, VA]), ph.sb("own", [P, H_B, VA])
        pT = ph.ps("pT", [P, 4, P])
        psmall = ph.ps("psmall", [P, 4 * NJ])
        pa = ph.ps("pa", [P, 3, 512])
        pb = ph.ps("pb", [P, 3, 512])
        const_in, in_ = ph.sem("const_in"), [ph.sem("in0"), ph.sem("in1")]
        step = ph.sem("step")
        conv, silu, qk_turned, qkT_ready = ph.sem("conv"), ph.sem("silu"), ph.sem("qk_turned"), ph.sem("qkT_ready")
        gated, absd, expd, logd = ph.sem("gated"), ph.sem("absd"), ph.sem("expd"), ph.sem("logd")
        lf_ready, b_made, diag_a, arow, diag_g, grow = (ph.sem(n) for n in ("lf_ready", "b_made", "diag_a", "arow", "diag_g", "grow"))
        gmask, wexp, ascale, eexp = ph.sem("gmask"), ph.sem("wexp"), ph.sem("ascale"), ph.sem("eexp")
        scores, weighted, kw_ready = ph.sem("scores"), ph.sem("weighted"), ph.sem("kw_ready")
        num_made, own_made, num_out, own_out = ph.sem("num_made"), ph.sem("own_made"), ph.sem("num_out"), ph.sem("own_out")
        stored, ones_set = ph.sem("stored"), ph.sem("ones_set")
        N_IN, N_OUT, DVE_STEPS = 5, 4, 26
        with ph.block() as block:
            @block.sync
            def _(sp):
                for dst, src in ((ident, "ident"), (ones, "ones"), (upto, "upto"), (fromon, "fromon")):
                    sp.dma_start(dst[:, :], A[src]).then_inc(const_in, DMA)
                sp.dma_start(mask_ts[:, :, :], A["mask_ts"]).then_inc(const_in, DMA)
                sp.dma_start(mask_st[:, :, :], A["mask_st"]).then_inc(const_in, DMA)
                for q in range(3):
                    sp.dma_start(cw[:, q, :], rows_to_all(A["conv_qk"][0, q])).then_inc(const_in, DMA)
                sp.dma_start(bg[:, :], rows_to_all(A["b_gates"][0])).then_inc(const_in, DMA)
                with sp.Fori(0, nt // 2) as i:
                    for j in range(2):
                        n = 2 * i + j
                        row = row0 + n * P
                        sp.wait_ge(stored, START + i * 2 * N_OUT * DMA)
                        for q in range(3):
                            sp.dma_start(zq[:, j, q, :], z[bass.ds(row + (q - 1), P), 1024:1536]).then_inc(in_[j], DMA)
                        sp.dma_start(va[:, j, :, 0:HV], z[bass.ds(row, P), 1536:2048].rearrange("p (h v) -> p h v", h=H_B)).then_inc(in_[j], DMA)
                        sp.dma_start(gt[:, j, :], z[bass.ds(row, P), 2560:2576]).then_inc(in_[j], DMA)

            @block.vector
            def _(dve):
                dve.memset(va[:, :, :, HV:VA], 1.0).then_inc(ones_set, 1)
                dve.wait_ge(const_in, START + 10 * DMA)
                with dve.Fori(0, nt // 2) as i:
                    for j in range(2):
                        n = 2 * i + j
                        s = Steps(dve, step, n, DVE_STEPS)
                        dve.wait_ge(in_[j], START + (i + 1) * N_IN * DMA)
                        dve.wait_ge(stored, START + n * N_OUT * DMA)
                        for q in range(3):
                            s(dve.tensor_tensor(zq[:, j, q, :], zq[:, j, q, :], cw[:, q, :], ALU.mult))
                        s(dve.tensor_tensor(qk[:, :], zq[:, j, 0, :], zq[:, j, 1, :], ALU.add))
                        dve.tensor_tensor(qk[:, :], qk[:, :], zq[:, j, 2, :], ALU.add).then_inc(conv, 1)
                        s(dve.tensor_tensor(gt[:, j, :], gt[:, j, :], bg[:, :], ALU.add))
                        s(dve.tensor_scalar(lf[:, :], gt[:, j, :], 0.0, None, ALU.min))
                        dve.scalar_tensor_tensor(lg[:, :], gt[:, j, :], -1.0, gt[:, j, :], ALU.mult, ALU.max).then_inc(gated, 1)
                        dve.wait_ge(logd, START + n + 1)
                        dve.tensor_tensor(lf[:, :], lf[:, :], lg[:, :], ALU.subtract).then_inc(lf_ready, 1)
                        dve.wait_ge(b_made, START + n + 1)
                        s(dve.tensor_copy(sc[:, 0, :], psmall[:, 0:NJ]))
                        s(dve.tensor_copy(sc[:, 3, :], psmall[:, NJ:2 * NJ]))
                        for d in range(2):
                            s(dve.tensor_tensor(a[:, 4 * d:4 * d + 4], gt[:, j, 8 * d:8 * d + 4], sc[:, 0, 4 * d:4 * d + 4], ALU.subtract))
                        dve.tensor_tensor(diag[:, :, :], bc_mid(ident[:, :], NJ), bc_last(a[:, :], P), ALU.mult).then_inc(diag_a, 1)
                        dve.wait_ge(arow, START + n + 1)
                        for d in range(2):
                            s(dve.tensor_tensor(am[:, 4 * d:4 * d + 4, :], pa[:, d, :].rearrange("p (h t) -> p h t", h=4),
                                                bc_mid(mask_ts[:, d, :], 4), ALU.add))
                        s(dve.tensor_reduce(sc[:, 1, :], am[:, :, :], X, ALU.max))
                        s(dve.tensor_reduce(sc[:, 2, :], pa[:, 0:2, :].rearrange("p d (h t) -> p (d h) t", h=4), X, ALU.max))
                        dve.tensor_tensor(diag[:, :, :], bc_mid(ident[:, :], NJ), bc_last(sc[:, 1, :], P), ALU.mult).then_inc(diag_g, 1)
                        s(dve.tensor_tensor(ea[:, :], a[:, :], sc[:, 2, :], ALU.subtract))
                        dve.sem_inc(ascale, 1)
                        dve.wait_ge(grow, START + n + 1)
                        for d in range(2):
                            s(dve.tensor_tensor(am[:, 4 * d:4 * d + 4, :], pb[:, d, :].rearrange("p (h t) -> p h t", h=4),
                                                bc_mid(mask_st[:, d, :], 4), ALU.add))
                        dve.sem_inc(gmask, 1)
                        dve.wait_ge(scores, START + n + 1)
                        dve.wait_ge(wexp, START + n + 1)
                        for d in range(2):
                            for b, sT in enumerate((pT[:, 0:2, :], pa[:, 2, 0:2 * P].rearrange("p (m t) -> p m t", m=2))):
                                s(dve.tensor_tensor(wT[:, 4 * d + b:4 * d + 4:2, :], sT, wT[:, 4 * d + b:4 * d + 4:2, :], ALU.mult))
                        dve.sem_inc(weighted, 1)
                        dve.wait_ge(eexp, START + n + 1)
                        kh = qk[:, 256:512].rearrange("p (h c) -> p h c", h=4)
                        for d in range(2):
                            s(dve.tensor_tensor(kw[:, 4 * d:4 * d + 4, :], kh, bc_last(ea[:, 4 * d:4 * d + 4], HK), ALU.mult))
                        dve.sem_inc(kw_ready, 1)
                        dve.wait_ge(num_made, START + n + 1)
                        for b in range(3):
                            m = min(3, NJ - 3 * b)
                            s(dve.tensor_copy(num[:, 3 * b:3 * b + m, :], pa[:, b, 0:m * VA].rearrange("p (m v) -> p m v", m=m)))
                        dve.sem_inc(num_out, 1)
                        s.end()

            @block.scalar
            def _(act):
                with act.Fori(0, nt // 2) as i:
                    for j in range(2):
                        n = 2 * i + j
                        act.wait_ge(gated, START + n + 1)
                        act.activation(lg[:, :], lg[:, :], ACT.Exp, scale=-1.0).then_inc(expd, 1)
                        act.wait_ge(expd, START + n + 1)
                        act.activation(lg[:, :], lg[:, :], ACT.Ln, bias=1.0).then_inc(logd, 1)
                        act.wait_ge(conv, START + n + 1)
                        act.activation(qk[:, :], qk[:, :], ACT.Silu).then_inc(silu, 1)
                        act.wait_ge(qk_turned, START + n + 1)
                        act.activation(qkT[:, 0:2, :], pT[:, 0:2, :], ACT.Copy, scale=float(HK) ** -0.5)
                        act.activation(qkT[:, 2:4, :], pT[:, 2:4, :], ACT.Copy).then_inc(qkT_ready, 1)
                        act.wait_ge(ascale, START + n + 1)
                        act.activation(ea[:, :], ea[:, :], ACT.Exp).then_inc(eexp, 1)
                        act.wait_ge(gmask, START + n + 1)
                        for m in range(NJ):
                            ins = act.activation(wT[:, m, :], am[:, m, :], ACT.Exp, scale=-1.0, bias=a[:, m:m + 1])
                        ins.then_inc(wexp, 1)
                        act.wait_ge(own_made, START + n + 1)
                        for d in range(2):
                            ins = act.activation(own[:, 2 * d:2 * d + 2, :], pb[:, d, 0:2 * VA].rearrange("p (m v) -> p m v", m=2), ACT.Copy)
                        ins.then_inc(own_out, 1)
                        c = chunk0 + n
                        act.wait_ge(num_out, START + n + 1)
                        act.dma_start(S["num"][c], num[:, :, :]).then_inc(stored, DMA)
                        act.dma_start(S["sc"][c], sc[:, :, :]).then_inc(stored, DMA)
                        act.dma_start(S["qT"][c], qkT[:, 0:2, :]).then_inc(stored, DMA)
                        act.wait_ge(own_out, START + n + 1)
                        act.dma_start(S["own"][c], own[:, :, :]).then_inc(stored, DMA)
                act.wait_ge(stored, START + nt * N_OUT * DMA)

            @block.tensor
            def _(pe):
                pe.wait_ge(const_in, START + 10 * DMA)
                pe.wait_ge(ones_set, START + 1)
                with pe.Fori(0, nt // 2) as i:
                    for j in range(2):
                        n = 2 * i + j
                        pe.wait_ge(lf_ready, START + n + 1)
                        pe.matmul(psmall[:, 0:4], upto[:, :], lf[:, 4:8], start=True, stop=True)
                        pe.matmul(psmall[:, 4:8], fromon[:, :], lf[:, 12:16], start=True, stop=True)
                        pe.matmul(psmall[:, 8:12], ones[:, :], lf[:, 4:8], start=True, stop=True)
                        pe.matmul(psmall[:, 12:16], ones[:, :], lf[:, 12:16], start=True, stop=True).then_inc(b_made, 1)
                        pe.wait_ge(silu, START + n + 1)
                        for q in range(4):
                            mm = pe.transpose(pT[:, q, :], qk[:, q * P:(q + 1) * P], ident[:, :])
                        mm.then_inc(qk_turned, 1)
                        pe.wait_ge(diag_a, START + n + 1)
                        for d in range(2):
                            mm = pe.matmul(pa[:, d, :], ones[:, :], diag[:, 4 * d:4 * d + 4, :], start=True, stop=True)
                        mm.then_inc(arow, 1)
                        pe.wait_ge(diag_g, START + n + 1)
                        for d in range(2):
                            mm = pe.matmul(pb[:, d, :], ones[:, :], diag[:, 4 * d:4 * d + 4, :], start=True, stop=True)
                        mm.then_inc(grow, 1)
                        pe.wait_ge(qkT_ready, START + n + 1)
                        for h in range(H_B):
                            b = 64 * (h % 2)
                            out = pa[:, 2, (h // 2) * P:(h // 2 + 1) * P] if b else pT[:, h // 2, :]
                            mm = pe.matmul(out, qkT[b:b + 64, 2 + h // 2, :], qkT[b:b + 64, h // 2, :], start=True, stop=True)
                        mm.then_inc(scores, 1)
                        pe.wait_ge(weighted, START + n + 1)
                        for m in range(NJ):
                            mm = pe.matmul(pa[:, m // 3, (m % 3) * VA:(m % 3 + 1) * VA], wT[:, m, :], va[:, j, m % 4, :], start=True, stop=True)
                        mm.then_inc(num_made, 1)
                        pe.wait_ge(kw_ready, START + n + 1)
                        for m in range(NJ):
                            d, h = m // 4, m % 4
                            b = 64 * (h % 2)
                            mm = pe.matmul(pb[b:b + 64, d, (h // 2) * VA:(h // 2 + 1) * VA], kw[:, m, :], va[:, j, h, :], start=True, stop=True)
                        mm.then_inc(own_made, 1)


def mlstm_chain(nc, A, S):
    NJ = 2 * H_B
    with Phase(nc, "chain") as ph:
        num = ph.sb("num", [P, 2, NJ, VA])
        own = ph.sb("own", [P, 2, H_B, VA])
        qT = ph.sb("qT", [P, 2, 2, 2, P])
        sc = ph.sb("sc", [P, 2, 4, NJ])
        C = ph.sb("C", [P, H_B, VA])
        m0 = ph.sb("m0", [P, NJ])
        G = ph.sb("G", [P, NJ])
        w = ph.sb("w", [P, 2, NJ])
        wh = ph.sb("wh", [P, 2, H_B])
        g = ph.sb("g", [P, NJ])
        e = ph.sb("e", [P, 3, NJ])
        t = ph.sb("t", [P, NJ, VA])
        h = ph.sb("h", [P, 2, NJ, HV])
        den = ph.sb("den", [P, NJ])
        inter = ph.ps("inter", [P, 4, 512])
        in_ = [ph.sem("in0"), ph.sem("in1")]
        zeroed, step, w_ready, w_exp = ph.sem("zeroed"), ph.sem("step"), ph.sem("w_ready"), ph.sem("w_exp")
        inter_made, h_ready = ph.sem("inter_made"), ph.sem("h_ready")
        C_ready = ph.sem("C_ready")
        stored = ph.sem("stored")

        def load(sp, j, cf, cb):
            for d, c in ((0, cf), (1, cb)):
                hs = slice(4 * d, 4 * d + 4)
                sp.dma_start(num[:, j, hs, :], S["num"][c][:, hs, :]).then_inc(in_[j], DMA)
                sp.dma_start(own[:, j, 2 * d:2 * d + 2, :], S["own"][c][:, 2 * d:2 * d + 2, :]).then_inc(in_[j], DMA)
                sp.dma_start(qT[:, j, d, :, :], S["qT"][c]).then_inc(in_[j], DMA)
                sp.dma_start(sc[:, j, :, hs], S["sc"][c][:, :, hs]).then_inc(in_[j], DMA)

        with ph.block() as block:
            @block.sync
            def _(sp):
                load(sp, 0, 0, 1)
                load(sp, 1, 1, 0)
                with sp.Fori(0, NT // 2) as i:
                    for j in range(2):
                        k = 2 * i + j
                        sp.wait_ge(C_ready, START + k + 1)
                        load(sp, j, k + 2, 9 - k)
            @block.vector
            def _(dve):
                dve.memset(C[:, :, :], 0.0).then_inc(zeroed, 1)
                dve.memset(m0[:, :], 0.0).then_inc(zeroed, 1)
                dve.wait_ge(zeroed, START + 2)

                def output(s, k, j):
                    dve.wait_ge(inter_made, START + k + 1)
                    for d in range(2):
                        for b in range(2):
                            hs = slice(4 * d + b, 4 * d + 4, 2)
                            s(dve.tensor_tensor(t[:, hs, :], inter[:, 2 * b + d, 0:2 * VA].rearrange("p (m v) -> p m v", m=2),
                                                bc_last(e[:, 1, hs], VA), ALU.mult))
                    s(dve.tensor_tensor(num[:, j, :, :], num[:, j, :, :], bc_last(e[:, 0, :], VA), ALU.mult))
                    s(dve.tensor_tensor(t[:, :, :], t[:, :, :], num[:, j, :, :], ALU.add))
                    s(dve.scalar_tensor_tensor(den[:, :], t[:, :, HV], -1.0, t[:, :, HV], ALU.mult, ALU.max))
                    s(dve.tensor_tensor(den[:, :], den[:, :], e[:, 2, :], ALU.max))
                    s(dve.reciprocal(den[:, :], den[:, :]))
                    dve.wait_ge(stored, START + k * 2 * DMA)
                    s(dve.tensor_tensor(h[:, j, :, :], t[:, :, 0:HV], bc_last(den[:, :], HV), ALU.mult))
                    dve.sem_inc(h_ready, 1)

                def weights(s, j):
                    s(dve.tensor_tensor(G[:, :], m0[:, :], sc[:, j, 2, :], ALU.max))
                    s(dve.tensor_tensor(w[:, 0, :], m0[:, :], G[:, :], ALU.subtract))
                    s(dve.tensor_tensor(w[:, 1, :], sc[:, j, 2, :], G[:, :], ALU.subtract))
                    s(dve.tensor_tensor(g[:, :], m0[:, :], sc[:, j, 1, :], ALU.max))
                    s(dve.tensor_tensor(e[:, 0, :], sc[:, j, 1, :], g[:, :], ALU.subtract))
                    s(dve.tensor_tensor(e[:, 1, :], m0[:, :], g[:, :], ALU.subtract))
                    s(dve.scalar_tensor_tensor(e[:, 2, :], sc[:, j, 0, :], -1.0, g[:, :], ALU.mult, ALU.subtract))
                    s(dve.tensor_tensor(m0[:, :], sc[:, j, 3, :], G[:, :], ALU.add))
                    dve.sem_inc(w_ready, 1)

                def state(s, k, j):
                    dve.wait_ge(w_exp, START + k + 1)
                    for b in range(2):
                        s(dve.tensor_copy(wh[64 * b:64 * b + 64, :, :], w[64 * b:64 * b + 64, :, b::2]))
                    s(dve.tensor_tensor(own[:, j, :, :], own[:, j, :, :], bc_last(wh[:, 1, :], VA), ALU.mult))
                    s(dve.tensor_tensor(C[:, :, :], C[:, :, :], bc_last(wh[:, 0, :], VA), ALU.mult))
                    s(dve.tensor_tensor(C[:, :, :], C[:, :, :], own[:, j, :, :], ALU.add))
                    dve.sem_inc(C_ready, 1)

                CTX_STEPS, LAT_STEPS = 13, 23
                for k in range(2):
                    s = Steps(dve, step, k, CTX_STEPS)
                    dve.wait_ge(in_[k], START + 8 * DMA)
                    weights(s, k)
                    state(s, k, k)
                    s.end()
                with dve.Fori(0, NT // 2) as i:
                    for j in range(2):
                        k = 2 * i + j
                        s = Steps(dve, step, 0, LAT_STEPS)
                        s.base = 2 * CTX_STEPS + k * LAT_STEPS
                        dve.wait_ge(in_[j], START + (i + 2) * 8 * DMA)
                        weights(s, j)
                        dve.wait_ge(w_exp, START + k + 3)
                        output(s, k, j)
                        state(s, k + 2, j)
                        s.end()

            @block.scalar
            def _(act):
                def exps(k):
                    act.wait_ge(w_ready, START + k + 1)
                    act.activation(w[:, :, :], w[:, :, :], ACT.Exp)
                    act.activation(e[:, :, :], e[:, :, :], ACT.Exp).then_inc(w_exp, 1)
                for k in range(2):
                    exps(k)
                with act.Fori(0, NT // 2) as i:
                    for j in range(2):
                        k = 2 * i + j
                        exps(k + 2)
                        act.wait_ge(h_ready, START + k + 1)
                        act.dma_start(S["h"][0, k], h[:, j, 0:4, :]).then_inc(stored, DMA)
                        act.dma_start(S["h"][1, 7 - k], h[:, j, 4:8, :]).then_inc(stored, DMA)
                act.wait_ge(stored, START + NT * 2 * DMA)

            @block.tensor
            def _(pe):
                with pe.Fori(0, NT // 2) as i:
                    for j in range(2):
                        k = 2 * i + j
                        pe.wait_ge(in_[j], START + (i + 2) * 8 * DMA)
                        pe.wait_ge(C_ready, START + k + 2)
                        pe.wait_ge(h_ready, START + k)
                        for m in range(NJ):
                            d, hd = m // 4, m % 4
                            b = 64 * (hd % 2)
                            mm = pe.matmul(inter[:, 2 * (hd % 2) + d, (hd // 2) * VA:(hd // 2 + 1) * VA], qT[b:b + 64, j, d, hd // 2, :],
                                           C[b:b + 64, 2 * d + hd // 2, :], start=True, stop=True)
                        mm.then_inc(inter_made, 1)


def mixer_rows(nc, A, S, yT):
    with Phase(nc, "mixer") as ph:
        ident = ph.sb("ident", [P, P])
        wsT = ph.sb("wsT", [P, G_A, P])
        bs = ph.sb("bs", [P, G_A])
        rows = ph.sb("rows", [P, 3, 512])
        uv = ph.sb("uv", [P, 2, 2, 512])
        hh = ph.sb("hh", [P, 2, 2, 512])
        o = ph.sb("o", [P, 2, 512])
        stats = ph.sb("stats", [P, 5, 6])
        mv = ph.sb("mv", [P, 5, 2])
        sd = ph.sb("sd", [P, 5])
        vn = ph.sb("vn", [P, 512])
        hs = ph.sb("hs", [P, 512])
        y = ph.sb("y", [P, D])
        mixed = ph.ps("mixed", [P, 512])
        tp = ph.ps("tp", [P, KC, P])
        const_in, in_ = ph.sem("const_in"), [ph.sem("in0"), ph.sem("in1")]
        step, var_ready, sd_ready = ph.sem("step"), ph.sem("var_ready"), ph.sem("sd_ready")
        vn_ready, mixed_ready, y_ready, turned = ph.sem("vn_ready"), ph.sem("mixed_ready"), ph.sem("y_ready"), ph.sem("turned")
        placed, passed = ph.sem("placed"), ph.sem("passed")
        N_IN, STEPS = 4, 24
        with ph.block() as block:
            @block.sync
            def _(sp):
                sp.dma_start(ident[:, :], A["ident"]).then_inc(const_in, DMA)
                sp.dma_start(wsT[:, :, :], A["w_sT"]).then_inc(const_in, DMA)
                sp.dma_start(bs[:, :], A["b_sT"]).then_inc(const_in, DMA)
                for q, n in enumerate(("ln_v_g", "ln_v_b", "hn_g")):
                    sp.dma_start(rows[:, q, :], rows_to_all(A[n][0])).then_inc(const_in, DMA)
                with sp.Fori(0, NT // 2) as i:
                    for j in range(2):
                        n = 2 * i + j
                        sp.wait_ge(placed, START + 2 * i)
                        z = S["z1"][bass.ds(ROW_LAT + n * P, P), :]
                        sp.dma_start(uv[:, j, :, :], z[:, 0:1024].rearrange("p (a n) -> p a n", a=2)).then_inc(in_[j], DMA)
                        sp.dma_start(o[:, j, :], z[:, 2048:2560]).then_inc(in_[j], DMA)
                        for d in range(2):
                            sp.dma_start(hh[:, j, d, :], S["h"][d, n].rearrange("p h v -> p (h v)")).then_inc(in_[j], DMA)

            @block.vector
            def _(dve):
                dve.wait_ge(const_in, START + 6 * DMA)
                with dve.Fori(0, NT // 2) as i:
                    for j in range(2):
                        n = 2 * i + j
                        s = Steps(dve, step, n, STEPS)
                        dve.wait_ge(in_[j], START + (i + 1) * N_IN * DMA)
                        s(dve.bn_stats(stats[:, 4, :], uv[:, j, 1, :]))
                        s(dve.tensor_tensor(hs[:, :], hh[:, j, 0, :], hh[:, j, 1, :], ALU.add))
                        for q in range(4):
                            s(dve.bn_stats(stats[:, q, :], hs[:, q * P:(q + 1) * P]))
                        for q in range(5):
                            s.settle(passed)
                            s(dve.bn_aggr(mv[:, q, :], stats[:, q, :]))
                        dve.tensor_scalar(sd[:, :], mv[:, :, 1], LN_EPS, None, ALU.add).then_inc(var_ready, 1)
                        dve.wait_ge(sd_ready, START + n + 1)
                        s(dve.reciprocal(sd[:, :], sd[:, :]))
                        s(dve.tensor_scalar(vn[:, :], uv[:, j, 1, :], mv[:, 4, 0:1], sd[:, 4:5], ALU.subtract, ALU.mult))
                        s(dve.tensor_tensor(vn[:, :], vn[:, :], rows[:, 0, :], ALU.mult))
                        dve.tensor_tensor(vn[:, :], vn[:, :], rows[:, 1, :], ALU.add).then_inc(vn_ready, 1)
                        for q in range(4):
                            s(dve.tensor_scalar(hs[:, q * P:(q + 1) * P], hs[:, q * P:(q + 1) * P], mv[:, q, 0:1], sd[:, q:q + 1], ALU.subtract, ALU.mult))
                        s(dve.tensor_tensor(hs[:, :], hs[:, :], rows[:, 2, :], ALU.mult))
                        dve.wait_ge(turned, START + n)
                        s(dve.tensor_tensor(y[:, 512:1024], hs[:, :], o[:, j, :], ALU.mult))
                        dve.wait_ge(mixed_ready, START + n + 1)
                        for q in range(4):
                            s(dve.scalar_tensor_tensor(y[:, q * P:(q + 1) * P], mixed[:, q * P:(q + 1) * P], bs[:, q:q + 1],
                                                       uv[:, j, 0, q * P:(q + 1) * P], ALU.add, ALU.mult))
                        dve.sem_inc(y_ready, 1)
                        s.end()

            @block.scalar
            def _(act):
                with act.Fori(0, NT // 2) as i:
                    for j in range(2):
                        n = 2 * i + j
                        act.wait_ge(var_ready, START + n + 1)
                        act.activation(o[:, j, :], o[:, j, :], ACT.Sigmoid)
                        act.activation(sd[:, :], sd[:, :], ACT.Sqrt).then_inc(sd_ready, 1)
                        act.wait_ge(turned, START + n + 1)
                        act.activation(yT[:, :, bass.ds(n * P, P)], tp[:, :, :], ACT.Copy).then_inc(placed, 1)

            @block.tensor
            def _(pe):
                pe.wait_ge(const_in, START + 6 * DMA)
                with pe.Fori(0, NT // 2) as i:
                    for j in range(2):
                        n = 2 * i + j
                        pe.wait_ge(vn_ready, START + n + 1)
                        for q in range(4):
                            mm = pe.matmul(mixed[:, q * P:(q + 1) * P], wsT[:, q, :], vn[:, q * P:(q + 1) * P], start=True, stop=True)
                        mm.then_inc(mixed_ready, 1)
                        pe.wait_ge(y_ready, START + n + 1)
                        pe.wait_ge(placed, START + n)
                        for k in range(KC):
                            mm = pe.transpose(tp[:, k, :], y[:, k * P:(k + 1) * P], ident[:, :])
                        mm.then_inc(turned, 1)


def deepnorm(nc, A, S, name, src, y, dst, gate_row, g_row, b_row, bias_row):
    n_rows = 3 + (bias_row is not None)
    with Phase(nc, name) as ph:
        rows = ph.sb("rows", [P, 4, D])
        x = ph.sb("x", [P, 2, D])
        t = ph.sb("t", [P, 2, D])
        stats, mv, sd = ph.sb("stats", [P, 2, 6]), ph.sb("mv", [P, 2]), ph.sb("sd", [P, 1])
        const_in, in_ = ph.sem("const_in"), [ph.sem("in0"), ph.sem("in1")]
        step, var_ready, sd_ready = ph.sem("step"), ph.sem("var_ready"), ph.sem("sd_ready")
        done, stored = ph.sem("done"), [ph.sem("stored0"), ph.sem("stored1")]
        passed = ph.sem("passed")
        STEPS = 9 + (bias_row is not None)
        with ph.block() as block:
            @block.sync
            def _(sp):
                rr = [gate_row, g_row, b_row] + ([bias_row] if bias_row is not None else [])
                for q, r in enumerate(rr):
                    sp.dma_start(rows[:, q, :], rows_to_all(r)).then_inc(const_in, DMA)
                with sp.Fori(0, NT // 2) as i:
                    for j in range(2):
                        n = 2 * i + j
                        sp.wait_ge(stored[j], START + i * DMA)
                        sp.dma_start(x[:, j, :], src[bass.ds(n * P, P), :]).then_inc(in_[j], DMA)
                        sp.dma_start(t[:, j, :], y[bass.ds(n * P, P), :]).then_inc(in_[j], DMA)

            @block.vector
            def _(dve):
                dve.wait_ge(const_in, START + n_rows * DMA)
                with dve.Fori(0, NT // 2) as i:
                    for j in range(2):
                        n = 2 * i + j
                        s = Steps(dve, step, n, STEPS)
                        dve.wait_ge(in_[j], START + (i + 1) * 2 * DMA)
                        if bias_row is not None:
                            s(dve.tensor_tensor(t[:, j, :], t[:, j, :], rows[:, 3, :], ALU.add))
                        s(dve.tensor_tensor(t[:, j, :], t[:, j, :], rows[:, 0, :], ALU.mult))
                        s(dve.scalar_tensor_tensor(t[:, j, :], x[:, j, :], ALPHA, t[:, j, :], ALU.mult, ALU.add))
                        for q in range(2):
                            s(dve.bn_stats(stats[:, q, :], t[:, j, q * COL:(q + 1) * COL]))
                        s.settle(passed)
                        s(dve.bn_aggr(mv[:, :], stats[:, :, :]))
                        dve.tensor_scalar(sd[:, :], mv[:, 1:2], LN_EPS, None, ALU.add).then_inc(var_ready, 1)
                        dve.wait_ge(sd_ready, START + n + 1)
                        s(dve.reciprocal(sd[:, :], sd[:, :]))
                        s(dve.tensor_scalar(t[:, j, :], t[:, j, :], mv[:, 0:1], sd[:, 0:1], ALU.subtract, ALU.mult))
                        s(dve.tensor_tensor(t[:, j, :], t[:, j, :], rows[:, 1, :], ALU.mult))
                        s(dve.tensor_tensor(t[:, j, :], t[:, j, :], rows[:, 2, :], ALU.add))
                        dve.sem_inc(done, 1)
                        s.end()

            @block.scalar
            def _(act):
                with act.Fori(0, NT // 2) as i:
                    for j in range(2):
                        n = 2 * i + j
                        act.wait_ge(var_ready, START + n + 1)
                        act.activation(sd[:, :], sd[:, :], ACT.Sqrt).then_inc(sd_ready, 1)
                        act.wait_ge(done, START + n + 1)
                        act.dma_start(dst[bass.ds(n * P, P), :], t[:, j, :]).then_inc(stored[j], DMA)
                for j in range(2):
                    act.wait_ge(stored[j], START + NT // 2 * DMA)


def mlp(nc, A, S, hT):
    FB = D_FF // P
    HT = NT // 2
    for half in range(2):
        with ExitStack() as outer:
            aT = outer.enter_context(nc.sbuf_tensor(f"aT{half}", [P, FB, HT * P], F32))
            with Phase(nc, f"up{half}") as ph:
                w = ph.sb("w", [P, 2, KC, COL])
                b1 = ph.sb("b1", [P, 2, 4])
                r = ph.sb("r", [P, 2, HT * P])
                acc = ph.ps("acc", [P, 4, COL])
                w_in = [ph.sem("w_in0"), ph.sem("w_in1")]
                made, relu, squared = ph.sem("made"), ph.sem("relu"), ph.sem("squared")
                w_v = A["w1"][0].rearrange("(k p) n -> p k n", p=P)
                with ph.block() as block:
                    @block.sync
                    def _(sp):
                        with sp.Fori(0, FB // 8) as i:
                            for j in range(2):
                                sp.wait_ge(relu, START + 8 * i)
                                c = 2 * i + j
                                sp.dma_start(w[:, j, :, :], w_v[:, :, bass.ds(c * COL, COL)]).then_inc(w_in[j], DMA)
                                sp.dma_start(b1[:, j, :], A["b1_cols"][:, bass.ds(c * 4, 4)]).then_inc(w_in[j], DMA)

                    @block.tensor
                    def _(pe):
                        with pe.Fori(0, FB // 8) as i:
                            for j in range(2):
                                pe.wait_ge(w_in[j], START + (i + 1) * 2 * DMA)
                                for f in range(4):
                                    pe.wait_ge(relu, START + 8 * i + (f + 1 if j else 0))
                                    for k in range(KC):
                                        mm = pe.matmul(acc[:, f, :], w[:, j, k, f * P:(f + 1) * P],
                                                       hT[:, k, half * HT * P:(half + 1) * HT * P], start=k == 0, stop=k == KC - 1)
                                    mm.then_inc(made, 1)

                    @block.vector
                    def _(dve):
                        with dve.Fori(0, FB // 8) as i:
                            for j in range(2):
                                for f in range(4):
                                    n = 8 * i + 4 * j + f
                                    dve.wait_ge(made, START + n + 1)
                                    dve.wait_ge(squared, START + 8 * i + (4 * j + f - 1 if 4 * j + f > 0 else 0))
                                    dve.tensor_scalar(r[:, f % 2, :], acc[:, f, :], b1[:, j, f:f + 1], 0.0, ALU.add, ALU.max).then_inc(relu, 1)

                    @block.scalar
                    def _(act):
                        with act.Fori(0, FB // 8) as i:
                            for m in range(8):
                                n = 8 * i + m
                                act.wait_ge(relu, START + n + 1)
                                act.activation(aT[:, n, :], r[:, m % 2, :], ACT.Square).then_inc(squared, 1)
            with Phase(nc, f"down{half}") as ph:
                w = ph.sb("w", [P, 2, 4, D])
                ot = ph.sb("ot", [P, HT, 2, COL])
                acc = ph.ps("acc", [P, HT, 2, COL])
                w_in = [ph.sem("w_in0"), ph.sem("w_in1")]
                used, out_v, out_s, stored = ph.sem("used"), ph.sem("out_v"), ph.sem("out_s"), ph.sem("stored")
                w_v = A["w2"][0].rearrange("(f p) n -> p f n", p=P)
                with ph.block() as block:
                    @block.sync
                    def _(sp):
                        for c in range(FB // 4):
                            if c >= 2:
                                sp.wait_ge(used, START + c - 1)
                            sp.dma_start(w[:, c % 2, :, :], w_v[:, 4 * c:4 * c + 4, :]).then_inc(w_in[c % 2], DMA)

                    @block.tensor
                    def _(pe):
                        for c in range(FB // 4):
                            pe.wait_ge(w_in[c % 2], START + (c // 2 + 1) * DMA)
                            for f in range(4):
                                for t in range(HT):
                                    for q in range(2):
                                        mm = pe.matmul(acc[:, t, q, :], aT[:, 4 * c + f, t * P:(t + 1) * P],
                                                       w[:, c % 2, f, q * COL:(q + 1) * COL],
                                                       start=c == 0 and f == 0, stop=c == FB // 4 - 1 and f == 3)
                            mm.then_inc(used, 1)

                    @block.vector
                    def _(dve):
                        dve.wait_ge(used, START + FB // 4)
                        for t in range(HT):
                            dve.tensor_copy(ot[:, t, 0, :], acc[:, t, 0, :]).then_inc(out_v, 1)

                    @block.scalar
                    def _(act):
                        act.wait_ge(used, START + FB // 4)
                        for t in range(HT):
                            act.copy(ot[:, t, 1, :], acc[:, t, 1, :]).then_inc(out_s, 1)
                            act.wait_ge(out_s, START + t + 1)
                            act.wait_ge(out_v, START + t + 1)
                            n = half * HT + t
                            act.dma_start(S["t1"][n * P:(n + 1) * P, :], ot[:, t, :, :].rearrange("p a n -> p (a n)")).then_inc(stored, DMA)
                        act.wait_ge(stored, START + HT * DMA)


def first_block(nc, A, S):
    ada_phase(nc, A, S)
    row = lambda q, r: S["mod"][r, q * D:(q + 1) * D]
    z = S["z1"]
    with nc.sbuf_tensor("hT", [P, KC, SEQ + CTX], F32) as hT:
        norm_transpose(nc, "nx", A["x"][0], NT, hT, 0, row(1, 0), row(0, 0), A, LN_EPS, True)
        norm_transpose(nc, "nctx", A["ctx"][0], NTC, hT, SEQ, row(1, 1), row(0, 1), A, LN_EPS, True)
        lat, ctx = z[ROW_LAT:ROW_LAT + SEQ, :], z[ROW_CTX:ROW_CTX + CTX, :]
        cols = [(c, min(COL, D_IN - c)) for c in range(0, D_IN, COL)]
        product(nc, "zlat", hT, NT, 0, A["w_in"][0], KC, [(c, w, tiles(lat, slice(c, c + w))) for c, w in cols], None)
        product(nc, "zctx", hT, NTC, NT, A["w_in"][0], KC, [(c, w, tiles(ctx, slice(c, c + w))) for c, w in (cols[2], cols[3], cols[5])], None)
    zero_rows(nc, S, "zpad", [z[r:r + 1, 1024:1536] for r in (0, ROW_LAT - 2, ROW_LAT - 1, ROWS_Z1 - 1)])
    mlstm_prep(nc, A, S, "pctx", NTC, ROW_CTX, 0)
    mlstm_prep(nc, A, S, "plat", NT, ROW_LAT, NTC)
    mlstm_chain(nc, A, S)
    with nc.sbuf_tensor("yT1", [P, KC, SEQ], F32) as yT:
        mixer_rows(nc, A, S, yT)
        product(nc, "wout", yT, NT, 0, A["w_out"][0], KC, [(c, COL, tiles(S["t1"], slice(c, c + COL))) for c in (0, COL)], None)
    deepnorm(nc, A, S, "dn1", A["x"][0], S["t1"], S["xa"], row(2, 0), A["ln1_g"][0], A["ln1_b"][0], None)
    with nc.sbuf_tensor("hT2", [P, KC, SEQ], F32) as hT:
        norm_transpose(nc, "nmlp", S["xa"], NT, hT, 0, row(4, 0), row(3, 0), A, LN_EPS, True)
        mlp(nc, A, S, hT)
    deepnorm(nc, A, S, "dn2", S["xa"], S["t1"], S["x"], row(5, 0), A["ln2_g"][0], A["ln2_b"][0], A["b2"][0])


def zero_rows(nc, S, name, views):
    with Phase(nc, name) as ph:
        zero = ph.sb("zero", [1, 4136])
        zeroed, stored = ph.sem("zeroed"), ph.sem("stored")
        with ph.block() as block:
            @block.vector
            def _(dve):
                dve.memset(zero[:, :], 0.0).then_inc(zeroed, 1)

            @block.sync
            def _(sp):
                sp.wait_ge(zeroed, START + 1)
                for v in views:
                    sp.dma_start(v, zero[:, 0:v.shape[1]]).then_inc(stored, DMA)
                sp.wait_ge(stored, START + len(views) * DMA)


def scratch(nc):
    shapes = {"mod": (2, 6 * D), "z1": (ROWS_Z1, D_IN), "num": (10, P, 8, VA), "own": (10, P, 4, VA), "qT": (10, P, 2, P),
              "sc": (10, P, 4, 8), "h": (2, NT, P, H_B, HV), "t1": (SEQ, D), "xa": (SEQ, D), "x": (SEQ, D)}
    return {k: nc.dram_tensor(f"s_{k}", s, F32, kind="Internal").ap() for k, s in shapes.items()}


def constants():
    f = np.float32
    s, t = np.arange(P)[:, None], np.arange(P)[None, :]
    c = {"ident": np.eye(P, dtype=f), "ones": np.ones((P, P), f),
         "upto": (s <= t).astype(f), "fromon": (s >= t).astype(f)}
    c["mask_ts"] = np.stack([np.where(t <= s, 0, -BIG), np.where(t >= s, 0, -BIG)], 1).astype(f)
    c["mask_st"] = np.stack([np.where(s <= t, 0, BIG), np.where(s >= t, 0, BIG)], 1).astype(f)
    return c


def layouts(inputs):
    i = inputs
    c = np.stack([np.asarray(i["c"]).reshape(D), np.asarray(i["c_ctx"]).reshape(D)], -1)
    return {"cond_cols": np.ascontiguousarray(c.reshape(KC, P, 2).transpose(1, 0, 2)),
            "w_sT": np.ascontiguousarray(np.asarray(i["w_s"])[0].transpose(2, 0, 1)),
            "b_sT": np.ascontiguousarray(np.asarray(i["b_s"])[0].T),
            "b1_cols": np.ascontiguousarray(np.asarray(i["b1"]).reshape(D_FF // P, P).T)}


LAYERS = 2
HD = 64
NORM_EPS = 1e-6
GN_EPS = 64e-5
DECAY = float(np.exp(-0.5))
RW = 384
RWH = RW // HD
RW_IN = 4 * RW + 128
DSA_IN = 936
DSA0 = RW_IN
DIL0 = RW_IN + DSA_IN
IN2 = DIL0 + 4 * 384
DSA_H = 4
IDX_H, IDX_D = 8, 32
TOPK = 256
CH = 64
RATES = (1, 4, 16)


def heads(ap, n=RWH):
    return ap.rearrange("p (h c) -> p h c", h=n)


def rwkv(nc, A, S, l):
    with Phase(nc, "rwkv") as ph:
        ident, id64 = ph.sb("ident", [P, P]), ph.sb("id64", [P, HD])
        tri, blk = ph.sb("tri", [P, P]), ph.sb("blk", [P, P])
        masks = ph.sb("masks", [P, 4, P])
        first = ph.sb("first", [P, 2, P])
        levels = ph.sb("levels", [P, 5, P])
        mu = ph.sb("mu", [P, RW_IN])
        rows = ph.sb("rows", [P, 7, RW])
        ups = ph.sb("ups", [P, RW])
        zc, zp = ph.sb("zc", [P, 2, RW_IN]), ph.sb("zp", [P, 2, RW_IN])
        wdT = ph.sb("wdT", [P, P])
        la = ph.sb("la", [P, 2, RW])
        kk, k2, b = ph.sb("kk", [P, RW]), ph.sb("k2", [P, RW]), ph.sb("b", [P, RW])
        t1, bv = ph.sb("t1", [P, RW]), ph.sb("bv", [P, RW])
        n6, r6 = ph.sb("n6", [P, RWH]), ph.sb("r6", [P, RWH])
        ex, f = ph.sb("ex", [P, 6, RW]), ph.sb("f", [P, 7, RW])
        x4 = ph.sb("x4", [P, 4, RW])
        be, ke, rf = ph.sb("be", [P, RW]), ph.sb("ke", [P, RW]), ph.sb("rf", [P, RW])
        xT = ph.sb("xT", [P, 3, 4, P])
        mT = ph.sb("mT", [P, RWH, 4, P])
        T, TT = ph.sb("T", [P, RWH, P]), ph.sb("TT", [P, RWH, P])
        LT, PS = ph.sb("LT", [P, RWH, P]), ph.sb("PS", [P, RWH, P])
        wv, uw = ph.sb("wv", [P, RWH, P]), ph.sb("uw", [P, RWH, P])
        y0, r2 = ph.sb("y0", [P, RW]), ph.sb("r2", [P, RW])
        dg, tr, own = ph.sb("dg", [P, RW]), ph.sb("tr", [P, RW]), ph.sb("own", [P, RW])
        St = ph.sb("St", [P, RW])
        y = ph.sb("y", [P, RW])
        bk = ph.ps("bk", [P, 8, 512])
        const_in, in_, step = ph.sem("const_in"), [ph.sem("in0"), ph.sem("in1")], ph.sem("step")
        names = ("mixed tanhd wd_turned wdT_ready lowrank pre sig lw_ready cums n6_ready rn_ready ex_ready f_ready x4_ready turned xT_ready "
                 "scores scores_read A_ready T_first LT_ready P_made P_ready TP_made T_ready dv_made dv_ready uw_made uw_ready "
                 "last_made tr_ready r2_ready y0_ready S_made S_ready var_ready sd_ready silu done zeroed").split()
        (mixed, tanhd, wd_turned, wdT_ready, lowrank, pre, sig, lw_ready, cums, n6_ready, rn_ready, ex_ready, f_ready, x4_ready, turned, xT_ready,
         scores, scores_read, A_ready, T_first, LT_ready, P_made, P_ready, TP_made, T_ready, dv_made, dv_ready, uw_made, uw_ready,
         last_made, tr_ready, r2_ready, y0_ready, S_made, S_ready, var_ready, sd_ready, silu, done, zeroed) = (ph.sem(n) for n in names)
        stored, passed = ph.sem("stored"), ph.sem("passed")
        N_CONST, STEPS = 17, 87
        two = lambda ap: ap.rearrange("p (m t) -> p m t", t=P)
        with ph.block() as block:
            @block.sync
            def _(sp):
                for dst, src in ((ident[:, :], A["ident"]), (id64[:, :], A["id64"]), (tri[:, :], A["tri64"]), (blk[:, :], A["blk64"]),
                                 (masks[:, :, :], A["rw_masks"]), (first[:, :, :], A["rw_first"]), (levels[:, :, :], A["rw_levels"]),
                                 (mu[:, :], rows_to_all(A["tshift_mu_2"][l])),
                                 (ups[0:64, :], A["rwkv_w_up_2"][l]), (ups[64:128, :], A["rwkv_a_up_2"][l])):
                    sp.dma_start(dst, src).then_inc(const_in, DMA)
                for q, n in enumerate("w0 a0 k_k k_a r_k ln_g ln_b".split()):
                    src = A[f"rwkv_{n}_2"][l]
                    if n == "r_k":
                        src = src.rearrange("h c -> (h c)")
                    sp.dma_start(rows[:, q, :], rows_to_all(src)).then_inc(const_in, DMA)
                with sp.Fori(0, NT // 2) as i:
                    for j in range(2):
                        n = 2 * i + j
                        sp.wait_ge(stored, START + 2 * i * DMA)
                        sp.dma_start(zc[:, j, :], S["z2"][bass.ds(n * P + 1, P), 0:RW_IN]).then_inc(in_[j], DMA)
                        sp.dma_start(zp[:, j, :], S["z2"][bass.ds(n * P, P), 0:RW_IN]).then_inc(in_[j], DMA)

            @block.vector
            def _(dve):
                dve.memset(St[:, :], 0.0).then_inc(zeroed, 1)
                dve.wait_ge(zeroed, START + 1)
                dve.wait_ge(const_in, START + N_CONST * DMA)
                with dve.Fori(0, NT // 2) as i:
                    for j in range(2):
                        n = 2 * i + j
                        s = Steps(dve, step, n, STEPS)
                        tt = lambda o, a, c, op: s(dve.tensor_tensor(o, a, c, op))
                        z = zc[:, j, :]
                        r, k, v, g = (z[:, q * RW:(q + 1) * RW] for q in range(4))
                        dve.wait_ge(in_[j], START + (i + 1) * 2 * DMA)
                        tt(zp[:, j, :], zp[:, j, :], z, ALU.subtract)
                        tt(zp[:, j, :], zp[:, j, :], mu[:, :], ALU.mult)
                        tt(z, z, zp[:, j, :], ALU.add)
                        dve.sem_inc(mixed, 1)
                        tt(kk[:, :], k, rows[:, 2, :], ALU.mult)
                        tt(t1[:, :], kk[:, :], kk[:, :], ALU.mult)
                        s(dve.tensor_reduce(n6[:, :], heads(t1[:, :]), X, ALU.add))
                        dve.sem_inc(n6_ready, 1)
                        dve.wait_ge(lowrank, START + n + 1)
                        for q in range(2):
                            tt(la[:, q, :], bk[:, 6 + q, 0:RW], rows[:, q, :], ALU.add)
                        dve.sem_inc(pre, 1)
                        dve.wait_ge(rn_ready, START + n + 1)
                        s(dve.tensor_scalar(n6[:, :], n6[:, :], 1e-12, None, ALU.max))
                        s(dve.reciprocal(n6[:, :], n6[:, :]))
                        tt(heads(kk[:, :]), heads(kk[:, :]), bc_last(n6[:, :], HD), ALU.mult)
                        dve.wait_ge(sig, START + n + 1)
                        s(dve.tensor_scalar(la[:, 0, :], la[:, 0, :], -DECAY, None, ALU.mult))
                        dve.sem_inc(lw_ready, 1)
                        s(dve.scalar_tensor_tensor(t1[:, :], la[:, 1, :], -1.0, rows[:, 3, :], ALU.add, ALU.mult))
                        s(dve.scalar_tensor_tensor(k2[:, :], t1[:, :], 1.0, k, ALU.add, ALU.mult))
                        tt(b[:, :], kk[:, :], la[:, 1, :], ALU.mult)
                        tt(t1[:, :], r, k2[:, :], ALU.mult)
                        tt(t1[:, :], t1[:, :], rows[:, 4, :], ALU.mult)
                        s(dve.tensor_reduce(r6[:, :], heads(t1[:, :]), X, ALU.add))
                        tt(heads(bv[:, :]), heads(v), bc_last(r6[:, :], HD), ALU.mult)
                        dve.wait_ge(cums, START + n + 1)
                        s(dve.tensor_copy(ex[:, 4, :], bk[:, 6, 0:RW]))
                        s(dve.tensor_copy(ex[:, 5, :], bk[:, 7, 0:RW]))
                        s(dve.scalar_tensor_tensor(ex[:, 0, :], ex[:, 5, :], -0.5, ex[:, 4, :], ALU.mult, ALU.add))
                        tt(ex[:, 1, :], ex[:, 0, :], la[:, 0, :], ALU.subtract)
                        tt(ex[:, 2, :], ex[:, 5, :], ex[:, 4, :], ALU.subtract)
                        tt(ex[:, 3, :], ex[:, 4, :], la[:, 0, :], ALU.subtract)
                        dve.sem_inc(ex_ready, 1)
                        dve.wait_ge(f_ready, START + n + 1)
                        tt(x4[:, 0, :], kk[:, :], f[:, 1, :], ALU.mult)
                        tt(x4[:, 1, :], r, f[:, 0, :], ALU.mult)
                        tt(x4[:, 2, :], b[:, :], f[:, 6, :], ALU.mult)
                        tt(x4[:, 3, :], k2[:, :], f[:, 6, :], ALU.mult)
                        dve.sem_inc(x4_ready, 1)
                        tt(be[:, :], b[:, :], f[:, 2, :], ALU.mult)
                        tt(ke[:, :], k2[:, :], f[:, 2, :], ALU.mult)
                        tt(rf[:, :], r, f[:, 4, :], ALU.mult)
                        tt(wv[:, :, HD:P], heads(kk[:, :]), heads(f[:, 3, :]), ALU.mult)
                        tt(heads(dg[:, :]), heads(f[:, 5, :]), bc_mid(id64[:, :], RWH), ALU.mult)
                        for h in range(RWH):
                            dve.wait_ge(scores, START + n * RWH + h + 1)
                            tt(mT[:, h, :, :], two(bk[:, 2 + h % 4, :]), masks[:, :, :], ALU.mult)
                            dve.sem_inc(scores_read, 1)
                        dve.wait_ge(A_ready, START + n + 1)
                        for q in range(2):
                            tt(T[:, q::2, :], two(bk[:, q, 0:3 * P]), bc_mid(first[:, 0, :], 3), ALU.mult)
                        tt(T[:, :, :], bc_mid(ident[:, :], RWH), T[:, :, :], ALU.subtract)
                        tt(TT[:, :, :], mT[:, :, 0, :], bc_mid(first[:, 1, :], RWH), ALU.mult)
                        tt(TT[:, :, :], bc_mid(ident[:, :], RWH), TT[:, :, :], ALU.subtract)
                        for q in range(5):
                            tt(LT[:, :, :], mT[:, :, 0, :], bc_mid(levels[:, q, :], RWH), ALU.mult)
                            dve.sem_inc(LT_ready, 1)
                            dve.wait_ge(TP_made, START + 5 * n + q + 1)
                            for m in range(2):
                                if q < 4:
                                    tt(T[:, 3 * m:3 * m + 3, :], T[:, 3 * m:3 * m + 3, :], two(bk[:, 2 + m, 0:3 * P]), ALU.subtract)
                                tt(TT[:, 3 * m:3 * m + 3, :], TT[:, 3 * m:3 * m + 3, :], two(bk[:, 4 + m, 0:3 * P]), ALU.subtract)
                        dve.sem_inc(T_ready, 1)
                        dve.wait_ge(last_made, START + n + 1)
                        for c in range(2):
                            pr = slice(64 * c, 64 * c + 64)
                            tt(tr[pr, :], bk[pr, 7 * (1 - c), 0:RW], dg[pr, :], ALU.add)
                        for c in range(2):
                            pr = slice(64 * (1 - c), 64 * (1 - c) + 64)
                            s(dve.tensor_copy(own[pr, :], bk[pr, 1 + c, 0:RW]))
                        dve.sem_inc(tr_ready, 1)
                        for c in range(2):
                            pr = slice(64 * (1 - c), 64 * (1 - c) + 64)
                            dve.wait_ge(S_made, START + 2 * n + c + 1)
                            tt(St[pr, :], bk[pr, 5 + c, 0:RW], own[pr, :], ALU.add)
                            dve.sem_inc(S_ready, 1)
                        dve.wait_ge(y0_ready, START + n + 1)
                        tt(y[:, :], bk[:, 3, 0:RW], y0[:, :], ALU.add)
                        s(dve.tensor_reduce(r6[:, :], heads(y[:, :]), X, ALU.add))
                        s(dve.tensor_scalar(r6[:, :], r6[:, :], 1.0 / HD, None, ALU.mult))
                        tt(heads(y[:, :]), heads(y[:, :]), bc_last(r6[:, :], HD), ALU.subtract)
                        tt(t1[:, :], y[:, :], y[:, :], ALU.mult)
                        s(dve.tensor_reduce(r6[:, :], heads(t1[:, :]), X, ALU.add))
                        s(dve.tensor_scalar(r6[:, :], r6[:, :], 1.0 / HD, GN_EPS, ALU.mult, ALU.add))
                        dve.sem_inc(var_ready, 1)
                        dve.wait_ge(sd_ready, START + n + 1)
                        s(dve.reciprocal(r6[:, :], r6[:, :]))
                        tt(heads(y[:, :]), heads(y[:, :]), bc_last(r6[:, :], HD), ALU.mult)
                        tt(y[:, :], y[:, :], rows[:, 5, :], ALU.mult)
                        tt(y[:, :], y[:, :], rows[:, 6, :], ALU.add)
                        tt(y[:, :], y[:, :], bv[:, :], ALU.add)
                        dve.wait_ge(silu, START + n + 1)
                        tt(f[:, 0, :], y[:, :], g, ALU.mult)
                        dve.sem_inc(done, 1)
                        s.end()

            @block.scalar
            def _(act):
                with act.Fori(0, NT // 2) as i:
                    for j in range(2):
                        n = 2 * i + j
                        act.wait_ge(mixed, START + n + 1)
                        act.activation(zc[:, j, 4 * RW:4 * RW + 64], zc[:, j, 4 * RW:4 * RW + 64], ACT.Tanh).then_inc(tanhd, 1)
                        act.activation(zc[:, j, 3 * RW:4 * RW], zc[:, j, 3 * RW:4 * RW], ACT.Silu).then_inc(silu, 1)
                        act.wait_ge(wd_turned, START + n + 1)
                        act.activation(wdT[:, :], bk[:, 0, 0:P], ACT.Copy).then_inc(wdT_ready, 1)
                        act.wait_ge(n6_ready, START + n + 1)
                        act.activation(n6[:, :], n6[:, :], ACT.Sqrt).then_inc(rn_ready, 1)
                        act.wait_ge(pre, START + n + 1)
                        act.activation(la[:, :, :], la[:, :, :], ACT.Sigmoid).then_inc(sig, 1)
                        act.wait_ge(ex_ready, START + n + 1)
                        act.wait_ge(stored, START + n * DMA)
                        act.activation(f[:, 6, :], ex[:, 0, :], ACT.Exp, scale=-1.0)
                        act.activation(f[:, 0:6, :], ex[:, :, :], ACT.Exp).then_inc(f_ready, 1)
                        for q in range(3):
                            act.wait_ge(turned, START + 3 * n + q + 1)
                            act.activation(xT[:, q, :, :], two(bk[:, (6, 7, 0)[q], :]), ACT.Copy).then_inc(xT_ready, 1)
                        for q in range(5):
                            act.wait_ge(P_made, START + 5 * n + q + 1)
                            for m in range(2):
                                ins = act.activation(PS[:, 3 * m:3 * m + 3, :], two(bk[:, m, 0:3 * P]), ACT.Copy)
                            ins.then_inc(P_ready, 1)
                        act.wait_ge(dv_made, START + n + 1)
                        act.activation(wv[:, :, 0:HD], heads(bk[:, 0, 0:RW]), ACT.Copy).then_inc(dv_ready, 1)
                        act.wait_ge(uw_made, START + n + 1)
                        for m in range(2):
                            ins = act.activation(uw[:, 3 * m:3 * m + 3, :], two(bk[:, 2 + m, 0:3 * P]), ACT.Copy, scale=-1.0)
                        ins.then_inc(uw_ready, 1)
                        act.wait_ge(last_made, START + n + 1)
                        for c in range(2):
                            pr = slice(64 * c, 64 * c + 64)
                            ins = act.activation(r2[pr, :], bk[pr, 5 + c, 0:RW], ACT.Copy)
                        ins.then_inc(r2_ready, 1)
                        act.activation(y0[:, :], bk[:, 4, 0:RW], ACT.Copy).then_inc(y0_ready, 1)
                        act.wait_ge(var_ready, START + n + 1)
                        act.activation(r6[:, :], r6[:, :], ACT.Sqrt).then_inc(sd_ready, 1)
                        act.wait_ge(done, START + n + 1)
                        act.dma_start(S["y2"][bass.ds(n * P, P), 0:RW], f[:, 0, :]).then_inc(stored, DMA)
                act.wait_ge(stored, START + NT * DMA)

            @block.tensor
            def _(pe):
                pe.wait_ge(const_in, START + N_CONST * DMA)
                with pe.Fori(0, NT // 2) as i:
                    for j in range(2):
                        n = 2 * i + j
                        v = heads(zc[:, j, 2 * RW:3 * RW])
                        pe.wait_ge(tanhd, START + n + 1)
                        pe.transpose(bk[:, 0, 0:P], zc[:, j, 4 * RW:4 * RW + P], ident[:, :]).then_inc(wd_turned, 1)
                        pe.wait_ge(wdT_ready, START + n + 1)
                        for q in range(2):
                            pr = slice(64 * q, 64 * q + 64)
                            mm = pe.matmul(bk[:, 6 + q, 0:RW], wdT[pr, :], ups[pr, :], start=True, stop=True)
                        mm.then_inc(lowrank, 1)
                        pe.wait_ge(lw_ready, START + n + 1)
                        pe.matmul(bk[:, 6, 0:RW], tri[:, :], la[:, 0, :], start=True, stop=True)
                        pe.matmul(bk[:, 7, 0:RW], blk[:, :], la[:, 0, :], start=True, stop=True).then_inc(cums, 1)
                        pe.wait_ge(x4_ready, START + n + 1)
                        for q in range(3):
                            for m in range(4):
                                mm = pe.transpose(bk[:, (6, 7, 0)[q], m * P:(m + 1) * P], x4[:, m, q * P:(q + 1) * P], ident[:, :])
                            mm.then_inc(turned, 1)
                        pe.wait_ge(xT_ready, START + 3 * n + 3)
                        for h in range(RWH):
                            pr = slice(64 * (h % 2), 64 * (h % 2) + 64)
                            if h >= 4:
                                pe.wait_ge(scores_read, START + n * RWH + h - 3)
                            kr = xT[pr, h // 2, 0:2, :]
                            pe.matmul(bk[:, 2 + h % 4, 0:256], xT[pr, h // 2, 2, :], kr, start=True, stop=True)
                            pe.matmul(bk[:, 2 + h % 4, 256:512], xT[pr, h // 2, 3, :], kr, start=True, stop=True).then_inc(scores, 1)
                        for h in range(RWH):
                            pr = slice(64 * (h % 2), 64 * (h % 2) + 64)
                            mm = pe.matmul(bk[:, h % 2, (h // 2) * P:(h // 2 + 1) * P], xT[pr, h // 2, 0, :], xT[pr, h // 2, 2, :], start=True, stop=True)
                        mm.then_inc(A_ready, 1)
                        for q in range(5):
                            pe.wait_ge(LT_ready, START + 5 * n + q + 1)
                            for h in range(RWH):
                                mm = pe.matmul(bk[:, h // 3, (h % 3) * P:(h % 3 + 1) * P], LT[:, h, :], T[:, h, :], start=True, stop=True)
                            mm.then_inc(P_made, 1)
                            pe.wait_ge(P_ready, START + 5 * n + q + 1)
                            for h in range(RWH):
                                at = slice((h % 3) * P, (h % 3 + 1) * P)
                                if q < 4:
                                    pe.matmul(bk[:, 2 + h // 3, at], TT[:, h, :], PS[:, h, :], start=True, stop=True)
                                mm = pe.matmul(bk[:, 4 + h // 3, at], PS[:, h, :], TT[:, h, :], start=True, stop=True)
                            mm.then_inc(TP_made, 1)
                        for h in range(RWH):
                            mm = pe.matmul(bk[:, 0, h * HD:(h + 1) * HD], mT[:, h, 2, :], v[:, h, :], start=True, stop=True)
                        mm.then_inc(dv_made, 1)
                        pe.wait_ge(dv_ready, START + n + 1)
                        pe.wait_ge(T_ready, START + n + 1)
                        for h in range(RWH):
                            mm = pe.matmul(bk[:, 2 + h // 3, (h % 3) * P:(h % 3 + 1) * P], TT[:, h, :], wv[:, h, :], start=True, stop=True)
                        mm.then_inc(uw_made, 1)
                        pe.wait_ge(uw_ready, START + n + 1)
                        for h in range(RWH):
                            at = slice(h * HD, (h + 1) * HD)
                            pe.matmul(bk[:, 4, at], mT[:, h, 1, :], uw[:, h, 0:HD], start=True, stop=False)
                            pe.matmul(bk[:, 4, at], mT[:, h, 3, :], v[:, h, :], start=False, stop=True)
                        for c in range(2):
                            pr, po = slice(64 * c, 64 * c + 64), slice(64 * (1 - c), 64 * (1 - c) + 64)
                            for h in range(RWH):
                                at = slice(h * HD, (h + 1) * HD)
                                W = uw[pr, h, HD:P]
                                pe.matmul(bk[pr, 5 + c, at], W, mT[pr, h, 1, 64 * c:64 * c + 64], start=True, stop=False)
                                pe.matmul(bk[pr, 5 + c, at], rf[pr, at], ident[pr, 64 * c:64 * c + 64], start=False, stop=True)
                                pe.matmul(bk[pr, 7 * (1 - c), at], W, be[pr, at], start=True, stop=True)
                                pe.matmul(bk[po, 1 + c, at], be[pr, at], uw[pr, h, 0:HD], start=True, stop=False)
                                mm = pe.matmul(bk[po, 1 + c, at], ke[pr, at], v[pr, h, :], start=False, stop=True)
                        mm.then_inc(last_made, 1)
                        for c in range(2):
                            pr, po = slice(64 * c, 64 * c + 64), slice(64 * (1 - c), 64 * (1 - c) + 64)
                            if c == 0:
                                pe.wait_ge(r2_ready, START + n + 1)
                                pe.wait_ge(tr_ready, START + n + 1)
                                pe.wait_ge(S_ready, START + 2 * n)
                            else:
                                pe.wait_ge(S_ready, START + 2 * n + 1)
                            pe.sem_inc(passed, 1)
                            for h in range(RWH):
                                at = slice(h * HD, (h + 1) * HD)
                                pe.matmul(bk[pr, 3, at], r2[pr, at], St[pr, at], start=True, stop=True)
                            for h in range(RWH):
                                at = slice(h * HD, (h + 1) * HD)
                                mm = pe.matmul(bk[po, 5 + c, at], tr[pr, at], St[pr, at], start=True, stop=True)
                            mm.then_inc(S_made, 1)


def rope(s, dve, x, x1, x2, cos, sin, ta, tb):
    s(dve.tensor_tensor(ta[0], x1, cos, ALU.mult))
    s(dve.tensor_tensor(ta[1], x2, sin, ALU.mult))
    s(dve.tensor_tensor(tb[0], x2, cos, ALU.mult))
    s(dve.tensor_tensor(tb[1], x1, sin, ALU.mult))
    s(dve.tensor_tensor(x1, ta[0], ta[1], ALU.subtract))
    s(dve.tensor_tensor(x2, tb[0], tb[1], ALU.add))


def dsa_prep(nc, A, S, B):
    with Phase(nc, "dprep") as ph:
        ident = ph.sb("ident", [P, P])
        cs = ph.sb("cs", [P, NT, 2, 12])
        z = ph.sb("z", [P, 2, DSA_IN])
        kd, ikd = ph.sb("kd", [P, 2, HD]), ph.sb("ikd", [P, 4, IDX_D])
        tmp = ph.sb("tmp", [P, 4, 9 * 8])
        pT = ph.ps("pT", [P, 2, 8, P])
        const_in, in_, step = ph.sem("const_in"), [ph.sem("in0"), ph.sem("in1")], ph.sem("step")
        roped, turned, placed = ph.sem("roped"), ph.sem("turned"), ph.sem("placed")
        STEPS = 15
        with ph.block() as block:
            @block.sync
            def _(sp):
                sp.dma_start(ident[:, :], A["ident"]).then_inc(const_in, DMA)
                sp.dma_start(cs[:, :, :, :], A["rope_dsa"]).then_inc(const_in, DMA)
                with sp.Fori(0, NT // 2) as i:
                    for j in range(2):
                        sp.wait_ge(placed, START + 2 * i)
                        sp.dma_start(z[:, j, :], S["z2"][bass.ds((2 * i + j) * P + 1, P), DSA0:DIL0]).then_inc(in_[j], DMA)

            @block.vector
            def _(dve):
                dve.wait_ge(const_in, START + 2 * DMA)
                with dve.Fori(0, NT // 2) as i:
                    for j in range(2):
                        n = 2 * i + j
                        s = Steps(dve, step, n, STEPS)
                        dve.wait_ge(in_[j], START + (i + 1) * DMA)
                        for c0, nh, w, half, f0 in ((0, 5, HD, 8, 0), (384, 9, IDX_D, 4, 8)):
                            x = z[:, j, c0:c0 + nh * w].rearrange("p (h c) -> p h c", h=nh)
                            tv = [tmp[:, q, 0:nh * half].rearrange("p (h c) -> p h c", h=nh) for q in range(4)]
                            cos, sin = (cs[:, bass.ds(n, 1), q, f0:f0 + half].to_broadcast([P, nh, half]) for q in range(2))
                            rope(s, dve, x, x[:, :, 0:half], x[:, :, half:2 * half], cos, sin, tv[0:2], tv[2:4])
                        dve.wait_ge(turned, START + n)
                        s(dve.tensor_copy(kd[:, :, :], bc_mid(z[:, j, 256:320], 2)))
                        s(dve.tensor_copy(ikd[:, :, :], bc_mid(z[:, j, 640:672], 4)))
                        s(dve.tensor_scalar(B["iw"][:, bass.ds(n, 1), :], z[:, j, 672:680].unsqueeze(1), float(IDX_H) ** -0.5, None, ALU.mult))
                        dve.sem_inc(roped, 1)
                        s.end()

            @block.tensor
            def _(pe):
                pe.wait_ge(const_in, START + 2 * DMA)
                with pe.Fori(0, NT // 2) as i:
                    for j in range(2):
                        n = 2 * i + j
                        pe.wait_ge(roped, START + n + 1)
                        pe.wait_ge(placed, START + n)
                        src = [z[:, j, 0:128], z[:, j, 128:256], kd[:, :, :], z[:, j, 384:512], z[:, j, 512:640], ikd[:, :, :]]
                        for q, x in enumerate(src):
                            mm = pe.transpose(pT[:, j, q, :], x, ident[:, :])
                        mm.then_inc(turned, 1)

            @block.scalar
            def _(act):
                with act.Fori(0, NT // 2) as i:
                    for j in range(2):
                        n = 2 * i + j
                        act.wait_ge(in_[j], START + (i + 1) * DMA)
                        act.activation(B["v"][:, bass.ds(n, 1), :], z[:, j, 320:384].unsqueeze(1), ACT.Copy)
                        act.activation(B["g"][:, bass.ds(n, 1), :], z[:, j, 680:936].unsqueeze(1), ACT.Silu)
                        act.wait_ge(turned, START + n + 1)
                        at = bass.ds(n * P, P)
                        act.activation(B["qT"][:, :, at], pT[:, j, 0:2, :], ACT.Copy)
                        act.activation(B["kT"][:, at], pT[:, j, 2, :], ACT.Copy)
                        act.activation(B["iqT"][:, :, at], pT[:, j, 3:5, :], ACT.Copy)
                        act.activation(B["ikT"][:, at], pT[:, j, 5, :], ACT.Copy).then_inc(placed, 1)


T0 = TOPK // P
NS = NT - T0
BISECT = 32


def dsa_scores(nc, A, S, B, sc):
    with Phase(nc, "dsc") as ph:
        causal = ph.sb("causal", [P, P])
        rl = ph.sb("rl", [P, 2, SEQ])
        acc = ph.ps("acc", [P, 4, 2, COL])
        const_in, made, relu, summed, step = (ph.sem(n) for n in ("const_in", "made", "relu", "summed", "step"))
        with ph.block() as block:
            @block.sync
            def _(sp):
                sp.dma_start(causal[:, :], A["causal_ts"]).then_inc(const_in, DMA)

            @block.tensor
            def _(pe):
                m = 0
                for t in range(T0, NT):
                    L = (t + 1) * P
                    for h in range(IDX_H):
                        r = h % 4
                        pr = slice(32 * r, 32 * r + 32)
                        if m >= 4:
                            pe.wait_ge(relu, START + m - 3)
                        for c in range(0, L, COL):
                            w = min(COL, L - c)
                            mm = pe.matmul(acc[:, r, c // COL, 0:w], B["iqT"][pr, h // 4, t * P:(t + 1) * P], B["ikT"][pr, c:c + w],
                                           start=True, stop=True, tile_position=(32 * r, 0))
                        mm.then_inc(made, 1)
                        m += 1

            @block.scalar
            def _(act):
                m = 0
                for t in range(T0, NT):
                    L = (t + 1) * P
                    for h in range(IDX_H):
                        act.wait_ge(made, START + m + 1)
                        if m >= 2:
                            act.wait_ge(summed, START + m - 1)
                        act.activation(rl[:, m % 2, 0:L], acc[:, h % 4, :, :].rearrange("p a n -> p (a n)")[:, 0:L], ACT.Relu,
                                       scale=float(IDX_D) ** -0.5).then_inc(relu, 1)
                        m += 1

            @block.vector
            def _(dve):
                dve.wait_ge(const_in, START + DMA)
                m, st = 0, 0
                for t in range(T0, NT):
                    L = (t + 1) * P
                    x, q = sc[t - T0], t - T0
                    for h in range(IDX_H):
                        dve.wait_ge(relu, START + m + 1)
                        iw = B["iw"][:, t, h:h + 1]
                        if h == 0:
                            dve.tensor_scalar(x[:, :], rl[:, m % 2, 0:L], iw, None, ALU.mult).then_inc(summed, 1)
                        else:
                            dve.wait_ge(summed, START + m)
                            dve.scalar_tensor_tensor(x[:, :], rl[:, m % 2, 0:L], iw, x[:, :], ALU.mult, ALU.add).then_inc(summed, 1)
                        m += 1
                    dve.wait_ge(summed, START + m)
                    dve.tensor_reduce(B["lo"][:, q:q + 1], x[:, :], X, ALU.min).then_inc(step, 1)
                    dve.tensor_reduce(B["hi"][:, q:q + 1], x[:, :], X, ALU.max).then_inc(step, 1)
                    st += 2
                    dve.wait_ge(step, START + st)
                    dve.tensor_tensor(x[:, t * P:L], x[:, t * P:L], causal[:, :], ALU.add).then_inc(step, 1)
                    st += 1
                dve.wait_ge(step, START + st)


def dsa_search(nc, A, S, B, sc):
    with Phase(nc, "dse") as ph:
        junk = ph.sb("junk", [P, 2, SEQ])
        mid, cnt, w = ph.sb("mid", [P, NS]), ph.sb("cnt", [P, NS]), ph.sb("w", [P, NS])
        ge, lt = ph.sb("ge", [P, NS], U8), ph.sb("lt", [P, NS], U8)
        step, passed = ph.sem("step"), ph.sem("passed")
        lo, hi = B["lo"], B["hi"]
        PRE, PER = 8, 6 + NS
        with ph.block() as block:
            @block.vector
            def _(dve):
                s = Steps(dve, step, 0, PRE)
                s(dve.tensor_tensor(w[:, :], hi[:, :], lo[:, :], ALU.subtract))
                s(dve.scalar_tensor_tensor(cnt[:, :], lo[:, :], -1.0, lo[:, :], ALU.mult, ALU.max))
                s(dve.tensor_scalar(cnt[:, :], cnt[:, :], 1e-6, 1e-35, ALU.mult, ALU.add))
                s(dve.tensor_tensor(w[:, :], w[:, :], cnt[:, :], ALU.add))
                s(dve.tensor_tensor(lo[:, :], lo[:, :], w[:, :], ALU.subtract))
                s(dve.tensor_tensor(mid[:, :], lo[:, :], hi[:, :], ALU.add))
                s(dve.tensor_scalar(mid[:, :], mid[:, :], 0.5, None, ALU.mult))
                s(dve.memset(cnt[:, :], 0.0))
                s.end()
                with dve.Fori(0, BISECT) as i:
                    s = Steps(dve, step, 0, PER)
                    s.base = PRE + i * PER
                    for q in range(NS):
                        L = (q + T0 + 1) * P
                        s(dve.tensor_scalar(junk[:, q % 2, 0:L], sc[q][:, :], mid[:, q:q + 1], 0.0, ALU.is_gt, ALU.add, accum_out=cnt[:, q:q + 1]))
                    s(dve.tensor_scalar(ge[:, :], cnt[:, :], float(TOPK), None, ALU.is_ge))
                    s(dve.tensor_scalar(lt[:, :], cnt[:, :], float(TOPK), None, ALU.is_lt))
                    s.settle(passed)
                    s(dve.copy_predicated(lo[:, :], ge[:, :], mid[:, :]))
                    s.settle(passed)
                    s(dve.copy_predicated(hi[:, :], lt[:, :], mid[:, :]))
                    s(dve.tensor_tensor(mid[:, :], lo[:, :], hi[:, :], ALU.add))
                    s(dve.tensor_scalar(mid[:, :], mid[:, :], 0.5, None, ALU.mult))
                    s.end()


def dsa_attend(nc, A, S, B, sc):
    with Phase(nc, "datt") as ph:
        ident = ph.sb("ident", [P, P])
        causal = ph.sb("causal", [P, P])
        ones = ph.sb("ones", [P, SEQ])
        gt, cand, pre = ph.sb("gt", [P, SEQ]), ph.sb("cand", [P, SEQ]), ph.sb("pre", [P, SEQ])
        mask = ph.sb("mask", [P, 2, SEQ])
        need = ph.sb("need", [P, 1])
        att = ph.sb("att", [P, 2, SEQ])
        nm, l = ph.sb("nm", [P, 2]), ph.sb("l", [P, 4])
        pT = ph.sb("pT", [P, 2, 4, P])
        o = ph.sb("o", [P, 2, 4, HD])
        acc = ph.ps("acc", [P, 2, 2, COL])
        tp = ph.ps("tp", [P, 2, 4, P])
        po = ph.ps("po", [P, 2, 512])
        (const_in, step, made, nm_ready, expd, turned, pT_ready, o_made, o_read, row_done) = (
            ph.sem(n) for n in "const_in step made nm_ready expd turned pT_ready o_made o_read row_done".split())
        stored = [ph.sem("stored0"), ph.sem("stored1")]
        groups = []
        for t in range(NT):
            for h in range(DSA_H):
                for b0 in range(0, t + 1, 4):
                    groups.append((t, h, b0, min(4, t + 1 - b0)))
        with ph.block() as block:
            @block.sync
            def _(sp):
                sp.dma_start(ident[:, :], A["ident"]).then_inc(const_in, DMA)
                sp.dma_start(causal[:, :], A["causal_ts"]).then_inc(const_in, DMA)
                for t in range(NT):
                    sp.wait_ge(row_done, START + DSA_H * (t + 1))
                    sp.dma_start(S["y2"][t * P:(t + 1) * P, RW:RW + 256], o[:, t % 2, :, :]).then_inc(stored[t % 2], DMA)
                for j in range(2):
                    sp.wait_ge(stored[j], START + NT // 2 * DMA)

            @block.tensor
            def _(pe):
                pe.wait_ge(const_in, START + 2 * DMA)

                def scores(m):
                    t, h = m // DSA_H, m % DSA_H
                    L, r = (t + 1) * P, h % 2
                    pr = slice(64 * r, 64 * r + 64)
                    if m >= 2:
                        pe.wait_ge(nm_ready, START + m - 1)
                    for c in range(0, L, COL):
                        w = min(COL, L - c)
                        mm = pe.matmul(acc[:, r, c // COL, 0:w], B["qT"][pr, h // 2, t * P:(t + 1) * P], B["kT"][pr, c:c + w], start=True, stop=True)
                    mm.then_inc(made, 1)

                def turn(k):
                    t, h, b0, nb = groups[k]
                    pe.wait_ge(expd, START + t * DSA_H + h + 1)
                    if k >= 2:
                        pe.wait_ge(pT_ready, START + k - 1)
                    for b in range(nb):
                        mm = pe.transpose(tp[:, k % 2, b, :], att[:, h % 2, (b0 + b) * P:(b0 + b + 1) * P], ident[:, :])
                    mm.then_inc(turned, 1)

                def values(k):
                    t, h, b0, nb = groups[k]
                    m = t * DSA_H + h
                    pe.wait_ge(pT_ready, START + k + 1)
                    if b0 == 0 and m >= 2:
                        pe.wait_ge(o_read, START + m - 1)
                    for b in range(nb):
                        mm = pe.matmul(po[:, m % 2, 0:HD], pT[:, k % 2, b, :], B["v"][:, b0 + b, :], start=b0 + b == 0, stop=b0 + b == t)
                    if b0 + nb == t + 1:
                        mm.then_inc(o_made, 1)

                scores(0)
                k = 0
                for m in range(NT * DSA_H):
                    if m + 1 < NT * DSA_H:
                        scores(m + 1)
                    while k < len(groups) and groups[k][0] * DSA_H + groups[k][1] == m:
                        turn(k)
                        if k >= 1:
                            values(k - 1)
                        k += 1
                values(k - 1)

            @block.vector
            def _(dve):
                n_steps = [0]

                def s(ins):
                    n_steps[0] += 1
                    ins.then_inc(step, 1)
                    dve.wait_ge(step, START + n_steps[0])

                s(dve.memset(ones[:, :], 1.0))
                dve.wait_ge(const_in, START + 2 * DMA)

                def row_out(m):
                    t, h = m // DSA_H, m % DSA_H
                    dve.wait_ge(o_made, START + m + 1)
                    if h == 0 and t >= 2:
                        dve.wait_ge(stored[t % 2], START + t // 2 * DMA)
                    s(dve.reciprocal(l[:, m % 4:m % 4 + 1], l[:, m % 4:m % 4 + 1]))
                    s(dve.scalar_tensor_tensor(o[:, t % 2, h, :], po[:, m % 2, 0:HD], l[:, m % 4:m % 4 + 1],
                                               B["g"][:, t, h * HD:(h + 1) * HD], ALU.mult, ALU.mult))
                    dve.sem_inc(o_read, 1)
                    dve.sem_inc(row_done, 1)

                def choose(t):
                    L, mk = (t + 1) * P, mask[:, t % 2, :]
                    if t < T0:
                        if t > 0:
                            s(dve.memset(mk[:, 0:t * P], 0.0))
                        s(dve.tensor_copy(mk[:, t * P:L], causal[:, :]))
                        return
                    q = t - T0
                    x, lo, hi = sc[q], B["lo"][:, q:q + 1], B["hi"][:, q:q + 1]
                    s(dve.tensor_scalar(gt[:, 0:L], x[:, :], hi, 0.0, ALU.is_gt, ALU.add, accum_out=need[:, :]))
                    s(dve.tensor_scalar(need[:, :], need[:, :], -1.0, float(TOPK), ALU.mult, ALU.add))
                    s(dve.scalar_tensor_tensor(cand[:, 0:L], x[:, :], lo, gt[:, 0:L], ALU.is_gt, ALU.subtract))
                    s(dve.tensor_tensor_scan(pre[:, 0:L], ones[:, 0:L], cand[:, 0:L], 0.0, ALU.mult, ALU.add))
                    s(dve.scalar_tensor_tensor(pre[:, 0:L], pre[:, 0:L], need[:, 0:1], cand[:, 0:L], ALU.is_le, ALU.mult))
                    s(dve.tensor_tensor(pre[:, 0:L], pre[:, 0:L], gt[:, 0:L], ALU.add))
                    s(dve.tensor_scalar(mk[:, 0:L], pre[:, 0:L], -1.0, BIG, ALU.add, ALU.mult))

                for m in range(NT * DSA_H):
                    t, h = m // DSA_H, m % DSA_H
                    L = (t + 1) * P
                    if h == 0:
                        choose(t)
                    dve.wait_ge(made, START + m + 1)
                    if m >= 2:
                        dve.wait_ge(turned, START + sum(1 for g in groups if g[0] * DSA_H + g[1] <= m - 2))
                    s(dve.scalar_tensor_tensor(att[:, h % 2, 0:L], acc[:, h % 2, :, :].rearrange("p a n -> p (a n)")[:, 0:L],
                                               float(HD) ** -0.5, mask[:, t % 2, 0:L], ALU.mult, ALU.add))
                    if m >= 2:
                        dve.wait_ge(expd, START + m - 1)
                    s(dve.tensor_reduce(nm[:, h % 2:h % 2 + 1], att[:, h % 2, 0:L], X, ALU.max, negate=True))
                    dve.sem_inc(nm_ready, 1)
                    if m >= 2:
                        row_out(m - 2)
                row_out(NT * DSA_H - 2)
                row_out(NT * DSA_H - 1)

            @block.scalar
            def _(act):
                k = 0
                for m in range(NT * DSA_H + 1):
                    if m < NT * DSA_H:
                        t, h = m // DSA_H, m % DSA_H
                        act.wait_ge(nm_ready, START + m + 1)
                        if m >= 4:
                            act.wait_ge(o_read, START + m - 3)
                        act.activation(att[:, h % 2, 0:(t + 1) * P], att[:, h % 2, 0:(t + 1) * P], ACT.Exp, bias=nm[:, h % 2:h % 2 + 1],
                                       accum_out=l[:, m % 4:m % 4 + 1]).then_inc(expd, 1)
                    while k < len(groups) and groups[k][0] * DSA_H + groups[k][1] == m - 1:
                        nb = groups[k][3]
                        act.wait_ge(turned, START + k + 1)
                        act.activation(pT[:, k % 2, 0:nb, :], tp[:, k % 2, 0:nb, :], ACT.Copy).then_inc(pT_ready, 1)
                        k += 1


def dil_rows(ap, gi, n, cols):
    if RATES[gi] == 1:
        return [(slice(0, P), ap[bass.ds(n * P, P), cols])]
    v = ap[:, cols]
    if RATES[gi] == 4:
        return [(slice(0, P), v.rearrange("(b j r) c -> b r j c", r=4, j=P)[n % 2, n // 2])]
    v = v.rearrange("(j r) c -> r j c", r=16)
    return [(slice(64 * m, 64 * m + 64), v[2 * n + m]) for m in range(2)]


def dil_cols(gi, n):
    if RATES[gi] == 1:
        return lambda t: t[:, n * P:(n + 1) * P].unsqueeze(1)
    if RATES[gi] == 4:
        return lambda t: t.rearrange("p (b j r) -> p b r j", r=4, j=P)[:, n % 2, n // 2, :].unsqueeze(1)
    return lambda t: t.rearrange("p (j r) -> p r j", r=16)[:, 2 * n:2 * n + 2, :]


def dilated(nc, A, S, yT):
    NG = 3
    with Phase(nc, "dil") as ph:
        ident = ph.sb("ident", [P, P])
        masks = ph.sb("masks", [P, 3, 2 * P])
        cs = ph.sb("cs", [P, NG * NT, 2, 8])
        z = ph.sb("z", [P, 2, 4, P])
        vp = ph.sb("vp", [P, 2, P])
        kT = ph.sb("kT", [P, 2, 2, P])
        qT = ph.sb("qT", [P, 2, P])
        tmp = ph.sb("tmp", [P, 4, 32])
        att = ph.sb("att", [P, 2, 2 * P])
        nm, l, rl_, ls = ph.sb("nm", [P, 2]), ph.sb("l", [P, 2]), ph.sb("rl", [P, 2]), ph.sb("ls", [P, 2])
        pT = ph.sb("pT", [P, 4, P])
        og, lb = ph.sb("og", [P, P]), ph.sb("lb", [P, P])
        LT = ph.sb("LT", [P, NG, SEQ])
        mx, sm = ph.sb("mx", [P, SEQ]), ph.sb("sm", [P, SEQ])
        pa = ph.ps("pa", [P, 2, 512])
        pt = ph.ps("pt", [P, 4, P])
        pq = ph.ps("pq", [P, 4, P])
        po = ph.ps("po", [P, 512])
        pz = ph.ps("pz", [P, 4, P])
        (const_in, step, roped, turned_qk, qk_ready, made, nm_ready, expd, turned_p, pT_ready, o_made, log_ready, og_ready,
         turned_o, placed, gated, M_ready, E_ready, W_ready, zeroed) = (ph.sem(n) for n in (
             "const_in step roped turned_qk qk_ready made nm_ready expd turned_p pT_ready o_made log_ready og_ready "
             "turned_o placed gated M_ready E_ready W_ready zeroed").split())
        in_ = [ph.sem("in0"), ph.sem("in1")]
        tiles_ = [(gi, n) for gi in range(NG) for n in range(NT)]
        n_loads = [0, 0]
        loads_by = []
        for m, (gi, n) in enumerate(tiles_):
            n_loads[m % 2] += 8 if gi == 2 else 4
            loads_by.append(n_loads[m % 2])
        has_prev = lambda gi, n: (gi == 0 and n > 0) or (gi == 1 and n % 2 == 1)
        with ph.block() as block:
            @block.sync
            def _(sp):
                sp.dma_start(ident[:, :], A["ident"]).then_inc(const_in, DMA)
                sp.dma_start(masks[:, :, :], A["dil_masks"]).then_inc(const_in, DMA)
                sp.dma_start(cs[:, :, :, :], A["rope_dil"]).then_inc(const_in, DMA)
                for m, (gi, n) in enumerate(tiles_):
                    if m >= 2:
                        sp.wait_ge(placed, START + m - 1)
                    for q in range(4):
                        c = DIL0 + 384 * q + P * gi
                        for pr, src in dil_rows(S["z2"][1:SEQ + 1, :], gi, n, slice(c, c + P)):
                            sp.dma_start(z[pr, m % 2, q, :], src).then_inc(in_[m % 2], DMA)

            @block.vector
            def _(dve):
                n_steps = [0]

                def s(ins):
                    n_steps[0] += 1
                    ins.then_inc(step, 1)
                    dve.wait_ge(step, START + n_steps[0])

                s(dve.memset(kT[:, :, :, :], 0.0))
                s(dve.memset(vp[:, :, :], 0.0))
                dve.sem_inc(zeroed, 1)
                dve.wait_ge(const_in, START + 3 * DMA)
                for m, (gi, n) in enumerate(tiles_):
                    j = m % 2
                    dve.wait_ge(in_[j], START + loads_by[m] * DMA)
                    x = z[:, j, 0:2, :].rearrange("p a (h c) -> p (a h) c", h=2)
                    tv = [tmp[:, q, :].rearrange("p (h c) -> p h c", h=4) for q in range(4)]
                    cos, sin = (bc_mid(cs[:, m, q, :], 4) for q in range(2))
                    rope(s, dve, x, x[:, :, 0:8], x[:, :, 8:16], cos, sin, tv[0:2], tv[2:4])
                    dve.sem_inc(roped, 1)
                    s(dve.tensor_copy(vp[:, j, :], z[:, j, 2, :]))
                    mk = masks[:, 0 if has_prev(gi, n) else (2 if gi == 2 else 1), :]
                    dve.wait_ge(made, START + m + 1)
                    for h in range(2):
                        s(dve.scalar_tensor_tensor(att[:, h, :], pa[:, h, 0:2 * P], float(HD) ** -0.5, mk, ALU.mult, ALU.add))
                    s(dve.tensor_reduce(nm[:, :], att[:, :, :], X, ALU.max, negate=True))
                    dve.sem_inc(nm_ready, 1)
                    dve.wait_ge(expd, START + m + 1)
                    s(dve.reciprocal(rl_[:, :], l[:, :]))
                    dve.wait_ge(log_ready, START + m + 1)
                    s(dve.tensor_tensor(ls[:, :], ls[:, :], nm[:, :], ALU.subtract))
                    if m >= 1:
                        dve.wait_ge(turned_o, START + m)
                    s(dve.tensor_copy(lb[:, :].rearrange("p (h c) -> p h c", h=2), bc_last(ls[:, :], HD)))
                    dve.wait_ge(o_made, START + m + 1)
                    s(dve.tensor_tensor(og[:, :].rearrange("p (h c) -> p h c", h=2), po[:, 0:P].rearrange("p (h c) -> p h c", h=2),
                                        bc_last(rl_[:, :], HD), ALU.mult))
                    dve.wait_ge(gated, START + m + 1)
                    s(dve.tensor_tensor(og[:, :], og[:, :], z[:, j, 3, :], ALU.mult))
                    dve.sem_inc(og_ready, 1)
                dve.wait_ge(placed, START + len(tiles_))
                s(dve.tensor_tensor(mx[:, :], LT[:, 0, :], LT[:, 1, :], ALU.max))
                s(dve.tensor_tensor(mx[:, :], mx[:, :], LT[:, 2, :], ALU.max))
                for q in range(NG):
                    s(dve.tensor_tensor(LT[:, q, :], LT[:, q, :], mx[:, :], ALU.subtract))
                dve.sem_inc(M_ready, 1)
                dve.wait_ge(E_ready, START + 1)
                s(dve.tensor_tensor(sm[:, :], LT[:, 0, :], LT[:, 1, :], ALU.add))
                s(dve.tensor_tensor(sm[:, :], sm[:, :], LT[:, 2, :], ALU.add))
                s(dve.reciprocal(sm[:, :], sm[:, :]))
                for q in range(NG):
                    s(dve.tensor_tensor(LT[:, q, :], LT[:, q, :], sm[:, :], ALU.mult))
                    s(dve.tensor_tensor(yT[:, 5 + q, :], yT[:, 5 + q, :], LT[:, q, :], ALU.mult))

            @block.scalar
            def _(act):
                act.wait_ge(zeroed, START + 1)
                for m, (gi, n) in enumerate(tiles_):
                    j = m % 2
                    act.wait_ge(in_[j], START + loads_by[m] * DMA)
                    act.activation(z[:, j, 3, :], z[:, j, 3, :], ACT.Silu).then_inc(gated, 1)
                    act.wait_ge(turned_qk, START + m + 1)
                    act.activation(qT[:, j, :], pq[:, 2 * j, :], ACT.Copy)
                    act.activation(kT[:, 0, j, :], pq[:, 2 * j + 1, :], ACT.Copy).then_inc(qk_ready, 1)
                    act.wait_ge(nm_ready, START + m + 1)
                    for h in range(2):
                        ins = act.activation(att[:, h, :], att[:, h, :], ACT.Exp, bias=nm[:, h:h + 1], accum_out=l[:, h:h + 1])
                    ins.then_inc(expd, 1)
                    act.wait_ge(expd, START + m + 1)
                    act.activation(ls[:, :], l[:, :], ACT.Ln).then_inc(log_ready, 1)
                    act.wait_ge(turned_p, START + m + 1)
                    act.activation(pT[:, :, :], pt[:, :, :], ACT.Copy).then_inc(pT_ready, 1)
                    act.wait_ge(turned_o, START + m + 1)
                    place = dil_cols(gi, n)
                    for q, (src, dst) in enumerate(((0, yT[:, 5 + gi, :]), (1, LT[:, gi, :]))):
                        dst = place(dst)
                        ins = act.activation(dst, pz[:, src, :].rearrange("p (a t) -> p a t", a=dst.shape[1]), ACT.Copy)
                    ins.then_inc(placed, 1)
                act.wait_ge(M_ready, START + 1)
                act.activation(LT[:, :, :], LT[:, :, :], ACT.Exp).then_inc(E_ready, 1)

            @block.tensor
            def _(pe):
                pe.wait_ge(const_in, START + 3 * DMA)
                for m, (gi, n) in enumerate(tiles_):
                    j = m % 2
                    pe.wait_ge(roped, START + m + 1)
                    for q in range(2):
                        mm = pe.transpose(pq[:, 2 * j + q, :], z[:, j, q, :], ident[:, :])
                    mm.then_inc(turned_qk, 1)
                    pe.wait_ge(qk_ready, START + m + 1)
                    for h in range(2):
                        pr = slice(64 * h, 64 * h + 64)
                        pe.matmul(pa[:, h, 0:P], qT[pr, j, :], kT[pr, 0, 1 - j, :], start=True, stop=True)
                        mm = pe.matmul(pa[:, h, P:2 * P], qT[pr, j, :], kT[pr, 0, j, :], start=True, stop=True)
                    mm.then_inc(made, 1)
                    pe.wait_ge(expd, START + m + 1)
                    for h in range(2):
                        for b in range(2):
                            mm = pe.transpose(pt[:, 2 * h + b, :], att[:, h, b * P:(b + 1) * P], ident[:, :])
                    mm.then_inc(turned_p, 1)
                    pe.wait_ge(pT_ready, START + m + 1)
                    for h in range(2):
                        at = slice(h * HD, (h + 1) * HD)
                        pe.matmul(po[:, at], pT[:, 2 * h, :], vp[:, 1 - j, at], start=True, stop=False)
                        mm = pe.matmul(po[:, at], pT[:, 2 * h + 1, :], vp[:, j, at], start=False, stop=True)
                    mm.then_inc(o_made, 1)
                    pe.wait_ge(og_ready, START + m + 1)
                    if m >= 1:
                        pe.wait_ge(placed, START + m)
                    pe.transpose(pz[:, 0, :], og[:, :], ident[:, :])
                    pe.transpose(pz[:, 1, :], lb[:, :], ident[:, :]).then_inc(turned_o, 1)


def turn_rows(nc, A, S, yT):
    NC = 5
    with Phase(nc, "turn") as ph:
        ident = ph.sb("ident", [P, P])
        x = ph.sb("x", [P, 2, NC * P])
        pT = ph.ps("pT", [P, 2, 8, P])
        const_in, in_, turned, placed = ph.sem("const_in"), [ph.sem("in0"), ph.sem("in1")], ph.sem("turned"), [ph.sem("placed0"), ph.sem("placed1")]
        with ph.block() as block:
            @block.sync
            def _(sp):
                sp.dma_start(ident[:, :], A["ident"]).then_inc(const_in, DMA)
                with sp.Fori(0, NT // 2) as i:
                    for j in range(2):
                        sp.wait_ge(placed[j], START + i)
                        sp.dma_start(x[:, j, :], S["y2"][bass.ds((2 * i + j) * P, P), :]).then_inc(in_[j], DMA)

            @block.tensor
            def _(pe):
                pe.wait_ge(const_in, START + DMA)
                with pe.Fori(0, NT // 2) as i:
                    for j in range(2):
                        pe.wait_ge(in_[j], START + (i + 1) * DMA)
                        for q in range(NC):
                            mm = pe.transpose(pT[:, j, q, :], x[:, j, q * P:(q + 1) * P], ident[:, :])
                        mm.then_inc(turned, 1)

            @block.scalar
            def _(act):
                with act.Fori(0, NT // 2) as i:
                    for j in range(2):
                        act.wait_ge(turned, START + 2 * i + j + 1)
                        act.activation(yT[:, 0:NC, bass.ds((2 * i + j) * P, P)], pT[:, j, 0:NC, :], ACT.Copy).then_inc(placed[j], 1)


def add_rows(nc, name, x, t, gate):
    with Phase(nc, name) as ph:
        xs, ts, gs = ph.sb("xs", [P, 2, D]), ph.sb("ts", [P, 2, D]), ph.sb("gs", [P, 2, D])
        in_, sig, step, stored = [ph.sem("in0"), ph.sem("in1")], ph.sem("sig"), ph.sem("step"), [ph.sem("stored0"), ph.sem("stored1")]
        done = ph.sem("done")
        n_in = 2 + (gate is not None)
        with ph.block() as block:
            @block.sync
            def _(sp):
                with sp.Fori(0, NT // 2) as i:
                    for j in range(2):
                        sp.wait_ge(stored[j], START + i * DMA)
                        at = bass.ds((2 * i + j) * P, P)
                        sp.dma_start(xs[:, j, :], x[at, :]).then_inc(in_[j], DMA)
                        sp.dma_start(ts[:, j, :], t[at, :]).then_inc(in_[j], DMA)
                        if gate is not None:
                            sp.dma_start(gs[:, j, :], gate[at, :]).then_inc(in_[j], DMA)

            @block.vector
            def _(dve):
                with dve.Fori(0, NT // 2) as i:
                    for j in range(2):
                        n = 2 * i + j
                        dve.wait_ge(in_[j], START + (i + 1) * n_in * DMA)
                        if gate is not None:
                            dve.wait_ge(sig, START + n + 1)
                            dve.tensor_tensor(ts[:, j, :], ts[:, j, :], gs[:, j, :], ALU.mult).then_inc(step, 1)
                            dve.wait_ge(step, START + n + 1)
                        dve.tensor_tensor(xs[:, j, :], xs[:, j, :], ts[:, j, :], ALU.add).then_inc(done, 1)

            @block.scalar
            def _(act):
                with act.Fori(0, NT // 2) as i:
                    for j in range(2):
                        n = 2 * i + j
                        if gate is not None:
                            act.wait_ge(in_[j], START + (i + 1) * n_in * DMA)
                            act.activation(gs[:, j, :], gs[:, j, :], ACT.Sigmoid).then_inc(sig, 1)
                        act.wait_ge(done, START + n + 1)
                        act.dma_start(x[bass.ds(n * P, P), :], xs[:, j, :]).then_inc(stored[j], DMA)
                for j in range(2):
                    act.wait_ge(stored[j], START + NT // 2 * DMA)


def final_norm(nc, A, x, out):
    with Phase(nc, "final") as ph:
        g = ph.sb("g", [P, D])
        xs, sq = ph.sb("xs", [P, 2, D]), ph.sb("sq", [P, 2, D])
        ss = ph.sb("ss", [P, 2])
        const_in, in_, stored = ph.sem("const_in"), [ph.sem("in0"), ph.sem("in1")], [ph.sem("stored0"), ph.sem("stored1")]
        squares, mean, root, step, done = (ph.sem(n) for n in ("squares", "mean", "root", "step", "done"))
        with ph.block() as block:
            @block.sync
            def _(sp):
                sp.dma_start(g[:, :], rows_to_all(A["final_norm_g_2"])).then_inc(const_in, DMA)
                with sp.Fori(0, NT // 2) as i:
                    for j in range(2):
                        sp.wait_ge(stored[j], START + i * DMA)
                        sp.dma_start(xs[:, j, :], x[bass.ds((2 * i + j) * P, P), :]).then_inc(in_[j], DMA)

            @block.scalar
            def _(act):
                with act.Fori(0, NT // 2) as i:
                    for j in range(2):
                        n = 2 * i + j
                        act.wait_ge(in_[j], START + (i + 1) * DMA)
                        act.activation(sq[:, j, :], xs[:, j, :], ACT.Square, accum_out=ss[:, j:j + 1]).then_inc(squares, 1)
                        act.wait_ge(mean, START + n + 1)
                        act.activation(ss[:, j:j + 1], ss[:, j:j + 1], ACT.Sqrt).then_inc(root, 1)
                        act.wait_ge(done, START + n + 1)
                        act.dma_start(out[bass.ds(n * P, P), :], xs[:, j, :]).then_inc(stored[j], DMA)
                for j in range(2):
                    act.wait_ge(stored[j], START + NT // 2 * DMA)

            @block.vector
            def _(dve):
                dve.wait_ge(const_in, START + DMA)
                with dve.Fori(0, NT // 2) as i:
                    for j in range(2):
                        n = 2 * i + j
                        s = Steps(dve, step, n, 1)
                        dve.wait_ge(squares, START + n + 1)
                        dve.tensor_scalar(ss[:, j:j + 1], ss[:, j:j + 1], 1.0 / D, NORM_EPS, ALU.mult, ALU.add).then_inc(mean, 1)
                        dve.wait_ge(root, START + n + 1)
                        s(dve.reciprocal(ss[:, j:j + 1], ss[:, j:j + 1]))
                        dve.scalar_tensor_tensor(xs[:, j, :], xs[:, j, :], ss[:, j:j + 1], g[:, :], ALU.mult, ALU.mult).then_inc(done, 1)


def layer(nc, A, S, l):
    z2 = S["z2"][1:SEQ + 1, :]
    with nc.sbuf_tensor("hTl", [P, KC, SEQ], F32) as hT:
        norm_transpose(nc, "nl", S["x"], NT, hT, 0, A["norm_g_2"][l], None, A, NORM_EPS, False)
        product(nc, "win2", hT, NT, 0, A["w_in_2"][l], KC, [(8 * COL, 40, tiles(z2, slice(8 * COL, IN2)))],
                (4, lambda c: c * COL, lambda c: tiles(z2, bass.ds(c * COL, COL))))
    rwkv(nc, A, S, l)
    with ExitStack() as st:
        sb = lambda n, sh: st.enter_context(nc.sbuf_tensor(n, sh, F32))
        B = {"qT": sb("d_qT", [P, 2, SEQ]), "kT": sb("d_kT", [P, SEQ]), "iqT": sb("d_iqT", [P, 2, SEQ]), "ikT": sb("d_ikT", [P, SEQ]),
             "v": sb("d_v", [P, NT, HD]), "iw": sb("d_iw", [P, NT, IDX_H]), "g": sb("d_g", [P, NT, 256]),
             "lo": sb("d_lo", [P, NS]), "hi": sb("d_hi", [P, NS])}
        dsa_prep(nc, A, S, B)
        sc = [sb(f"d_sc{t}", [P, (t + 1) * P]) for t in range(T0, NT)]
        dsa_scores(nc, A, S, B, sc)
        dsa_search(nc, A, S, B, sc)
        dsa_attend(nc, A, S, B, sc)
    with nc.sbuf_tensor("yTl", [P, KC, SEQ], F32) as yT:
        dilated(nc, A, S, yT)
        turn_rows(nc, A, S, yT)
        product(nc, "wout2", yT, NT, 0, A["w_out_2"][l], KC, [(c, COL, tiles(S["t1"], slice(c, c + COL))) for c in (0, COL)], None)
    add_rows(nc, "addy", S["x"], S["t1"], None)
    with nc.sbuf_tensor("hTp", [P, KC, SEQ], F32) as hT:
        norm_transpose(nc, "np", S["x"], NT, hT, 0, A["ple_norm_g_2"][l], None, A, NORM_EPS, False)
        product(nc, "wgate", hT, NT, 0, A["ple_w_gate_2"][l], KC, [(c, COL, tiles(S["xa"], slice(c, c + COL))) for c in (0, COL)], None)
    with nc.sbuf_tensor("pT", [P, 2, SEQ], F32) as pT:
        load_p(nc, A, pT, l)
        product(nc, "wproj", pT, NT, 0, A["ple_w_proj_2"][l], 2, [(c, COL, tiles(S["t1"], slice(c, c + COL))) for c in (0, COL)], None)
    add_rows(nc, "addp", S["x"], S["t1"], S["xa"])


def load_p(nc, A, pT, l):
    with Phase(nc, "loadp") as ph:
        loaded = ph.sem("loaded")
        with ph.block() as block:
            @block.sync
            def _(sp):
                sp.dma_start(pT[:, :, :], A["pT_2"][l].rearrange("(k p) t -> p k t", p=P)).then_inc(loaded, DMA)
                sp.wait_ge(loaded, START + DMA)


def second_block(nc, A, S, out):
    zero_rows(nc, S, "z2pad", [S["z2"][0:1, :]])
    with nc.Fori(0, LAYERS) as l:
        layer(nc, A, S, l)
    final_norm(nc, A, S["x"], out)


def constants_2():
    f = np.float32
    s, t = np.arange(P)[:, None], np.arange(P)[None, :]
    same = s // CH == t // CH
    c = {"id64": np.tile(np.eye(HD, dtype=f), (2, 1)), "tri64": ((s <= t) & same).astype(f), "blk64": same.astype(f)}
    strict, incl = (s < t) & same, (s <= t) & same
    c["rw_masks"] = np.stack([strict, incl, strict, incl], 1).astype(f)
    pair = (s // 2 == t // 2)
    c["rw_first"] = np.stack([pair & (s > t), pair & (s < t)], 1).astype(f)
    c["rw_levels"] = np.stack([(s // (2 * b) == t // (2 * b)) & (s % (2 * b) < b) & (t % (2 * b) >= b) for b in (2, 4, 8, 16, 32)], 1).astype(f)
    c["causal_ts"] = np.where(t <= s, 0, -BIG).astype(f)
    kj = np.arange(2 * P)[None, :]
    dist = s + P - kj
    band = (dist >= 0) & (dist <= P)
    own = (kj >= P) & (dist >= 0)
    c["dil_masks"] = np.stack([np.where(m, 0, -BIG) for m in (band, own, own & ((kj - P) // 64 == s // 64))], 1).astype(f)

    def table(pos, rot):
        half = rot // 2
        inv = (f(500000.0) ** (-np.arange(half, dtype=f) / f(half))).astype(f)
        ang = pos.astype(f)[..., None] * inv
        return np.stack([np.cos(ang), np.sin(ang)], -2).astype(f)
    pos = np.arange(SEQ).reshape(NT, P)
    c["rope_dsa"] = np.ascontiguousarray(np.concatenate([table(pos, 16), table(pos, 8)], -1).transpose(1, 0, 2, 3))
    orders = []
    for r in RATES:
        if r == 1:
            o = pos
        elif r == 4:
            o = np.stack([(np.arange(P) + (n % 2) * P) * 4 + n // 2 for n in range(NT)])
        else:
            o = np.stack([np.concatenate([np.arange(64) * 16 + 2 * n + m for m in range(2)]) for n in range(NT)])
        orders.append(o)
    c["rope_dil"] = np.ascontiguousarray(table(np.concatenate(orders), 16).transpose(1, 0, 2, 3))
    return c


def scratch_2(nc):
    shapes = {"z2": (SEQ + 1, IN2), "y2": (SEQ, RW + 256)}
    return {k: nc.dram_tensor(f"s_{k}", s, F32, kind="Internal").ap() for k, s in shapes.items()}


def build_program(nc, A, out):
    S = scratch(nc)
    S.update(scratch_2(nc))
    first_block(nc, A, S)
    second_block(nc, A, S, out)


_INS = ("x ctx w_ada b_ada w_in ln_v_g ln_v_b conv_qk b_gates hn_g w_out ln1_g ln1_b w1 w2 b2 ln2_g ln2_b "
        "norm_g_2 w_in_2 tshift_mu_2 rwkv_w0_2 rwkv_w_up_2 rwkv_a0_2 rwkv_a_up_2 rwkv_k_k_2 rwkv_k_a_2 rwkv_r_k_2 "
        "rwkv_ln_g_2 rwkv_ln_b_2 w_out_2 ple_norm_g_2 ple_w_gate_2 ple_w_proj_2 final_norm_g_2").split()


def kernel(**inputs):
    import concourse.bacc as bacc
    from concourse.bass_utils import run_bass_kernel_spmd

    arrays = {n: np.ascontiguousarray(inputs[n]) for n in _INS}
    arrays["pT_2"] = np.ascontiguousarray(np.asarray(inputs["p_2"])[:, 0].transpose(0, 2, 1))
    arrays.update(layouts(inputs))
    arrays.update(constants())
    arrays.update(constants_2())
    nc = bacc.Bacc("TRN2", target_bir_lowering=False, num_devices=1)
    A = {n: nc.dram_tensor(f"in_{n}", a.shape, mybir.dt.from_np(a.dtype), kind="ExternalInput").ap() for n, a in arrays.items()}
    out = nc.dram_tensor("out_y", (SEQ, D), F32, kind="ExternalOutput").ap()
    build_program(nc, A, out)
    r = run_bass_kernel_spmd(nc, [{f"in_{n}": a for n, a in arrays.items()}], core_ids=[0])
    return r.results[0]["out_y"].reshape(1, SEQ, D)
```

```python
from contextlib import ExitStack

import numpy as np
import concourse.bass as bass
from concourse import mybir

F32 = mybir.dt.float32
U8 = mybir.dt.uint8
ALU = mybir.AluOpType
ACT = mybir.ActivationFunctionType
X = mybir.AxisListType.X

P = 128
D = 1024
KC = D // P
SEQ = 1024
CTX = 256
NT = SEQ // P
NTC = CTX // P
DMA = 16
COL = 512

D_IN = 2576
H_B, HK, HV = 4, 64, 128
G_A, GA = 4, 128
D_FF = 4096
ALPHA = 2.0 ** 0.25
LN_EPS = 1e-5
VA = HV + 1
BIG = 1e30
ROW_CTX = 1
ROW_LAT = CTX + 3
ROWS_Z1 = CTX + SEQ + 4


START = 80


class Phase:

    def __init__(self, nc, name):
        self.nc, self.name, self.stack, self.sems = nc, name, ExitStack(), []

    def __enter__(self):
        return self

    def sb(self, name, shape, dt=F32):
        return self.stack.enter_context(self.nc.sbuf_tensor(f"{self.name}_{name}", shape, dt))

    def ps(self, name, shape, dt=F32):
        return self.stack.enter_context(self.nc.psum_tensor(f"{self.name}_{name}", shape, dt))

    def sem(self, name):
        s = self.stack.enter_context(self.nc.semaphore(f"{self.name}_{name}"))
        self.sems.append(s)
        self.nc.sync.sem_inc(s, START)
        return s

    def block(self):
        self.nc.all_engine_barrier()
        return self.nc.Block()

    def __exit__(self, *a):
        if a[0] is None:
            for s in self.sems:
                self.nc.sync.sem_clear(s)
        self.stack.close()


class Steps:

    def __init__(self, eng, sem, trip, per_trip):
        self.eng, self.sem, self.base, self.k, self.n = eng, sem, trip * per_trip, 0, per_trip

    def __call__(self, ins):
        self.k += 1
        ins.then_inc(self.sem, 1)
        self.eng.wait_ge(self.sem, START + self.base + self.k)

    def settle(self, passed):
        self.eng.sem_inc(passed, 1)

    def end(self):
        assert self.k == self.n, f"{self.k} steps in a trip, not {self.n}"


def rows_to_all(ap):
    return ap.partition_broadcast(P)


def columns(ap):
    return ap.rearrange("(k p) -> p k", p=P)


def bc_last(ap, n):
    return ap.unsqueeze(2).to_broadcast([ap.shape[0], ap.shape[1], n])


def bc_mid(ap, n):
    return ap.unsqueeze(1).to_broadcast([ap.shape[0], n, ap.shape[1]])


def ada_phase(nc, A, S):
    W = 6 * D
    NCH = W // COL
    with Phase(nc, "ada") as ph:
        cond = ph.sb("cond", [P, KC, 2])
        scond = ph.sb("scond", [P, KC, 2])
        bias = ph.sb("bias", [2, W])
        mod = ph.sb("mod", [2, W])
        w = ph.sb("w", [P, 2, KC, COL])
        acc = ph.ps("acc", [2, 2, COL])
        cond_in, cond_silu = ph.sem("cond_in"), ph.sem("cond_silu")
        w_in = [ph.sem("w_in0"), ph.sem("w_in1")]
        w_used = [ph.sem("w_used0"), ph.sem("w_used1")]
        summed = [ph.sem("summed0"), ph.sem("summed1")]
        stored = ph.sem("stored")
        w_v = A["w_ada"][0].rearrange("(k p) n -> p k n", p=P)
        with ph.block() as block:
            @block.sync
            def _(sp):
                sp.dma_start(cond[:, :, :], A["cond_cols"]).then_inc(cond_in, DMA)
                for r in range(2):
                    sp.dma_start(bias[r:r + 1, :], A["b_ada"]).then_inc(cond_in, DMA)
                with sp.Fori(0, NCH // 2) as i:
                    for j in range(2):
                        sp.wait_ge(w_used[j], START + i)
                        sp.dma_start(w[:, j, :, :], w_v[:, :, bass.ds((2 * i + j) * COL, COL)]).then_inc(w_in[j], DMA)
                for j in range(2):
                    sp.wait_ge(summed[j], START + NCH // 2)
                sp.dma_start(S["mod"], mod[:, :]).then_inc(stored, DMA)
                sp.wait_ge(stored, START + DMA)

            @block.scalar
            def _(act):
                act.wait_ge(cond_in, START + 3 * DMA)
                act.activation(scond[:, :, :], cond[:, :, :], ACT.Silu).then_inc(cond_silu, 1)

            @block.tensor
            def _(pe):
                pe.wait_ge(cond_silu, START + 1)
                with pe.Fori(0, NCH // 2) as i:
                    for j in range(2):
                        pe.wait_ge(w_in[j], START + DMA * i + DMA)
                        pe.wait_ge(summed[j], START + i)
                        for k in range(KC):
                            mm = pe.matmul(acc[:, j, :], scond[:, k, :], w[:, j, k, :], start=k == 0, stop=k == KC - 1)
                        mm.then_inc(w_used[j], 1)

            @block.vector
            def _(dve):
                dve.wait_ge(cond_in, START + 3 * DMA)
                with dve.Fori(0, NCH // 2) as i:
                    for j in range(2):
                        dve.wait_ge(w_used[j], START + i + 1)
                        cols = bass.ds((2 * i + j) * COL, COL)
                        dve.tensor_tensor(mod[:, cols], acc[:, j, :], bias[:, cols], ALU.add).then_inc(summed[j], 1)


def norm_transpose(nc, name, src, nt, hT, tok0, scale_row, shift_row, const, eps, center, addend=None):
    with Phase(nc, name) as ph:
        ident = ph.sb("ident", [P, P])
        scale = ph.sb("scale", [P, KC])
        shift = ph.sb("shift", [P, KC])
        x = ph.sb("x", [P, 4, D])
        t = ph.sb("t", [P, 2, D])
        xn = ph.sb("xn", [P, 2, D])
        stats = ph.sb("stats", [P, 2, 6])
        mv = ph.sb("mv", [P, 2, 2])
        sd = ph.sb("sd", [P, 2])
        xT = ph.ps("xT", [P, 2, KC, P])
        const_in, x_in = ph.sem("const_in"), [ph.sem(f"x_in{k}") for k in range(4)]
        step, var_ready, sd_ready = ph.sem("step"), ph.sem("var_ready"), ph.sem("sd_ready")
        normed, turned, placed = ph.sem("normed"), ph.sem("turned"), ph.sem("placed")
        scale_ready, passed, added = ph.sem("scale_ready"), ph.sem("passed"), ph.sem("added")
        stored = [ph.sem(f"stored{k}") for k in range(4)]
        n_const = 1 + 1 + (shift_row is not None)
        n_in = 1 + (addend is not None)
        STATS = 3 + (not center) + (addend is not None)
        with ph.block() as block:
            @block.sync
            def _(sp):
                sp.dma_start(ident[:, :], const["ident"]).then_inc(const_in, DMA)
                sp.dma_start(scale[:, :], columns(scale_row), allow_slow_non_contiguous=True).then_inc(const_in, DMA)
                if shift_row is not None:
                    sp.dma_start(shift[:, :], columns(shift_row), allow_slow_non_contiguous=True).then_inc(const_in, DMA)
                for n in range(nt):
                    at = slice(n * P, (n + 1) * P)
                    if n >= 4:
                        sp.wait_ge(placed, START + n - 3)
                        if addend is not None:
                            sp.wait_ge(stored[n % 4], START + n // 4 * DMA)
                    sp.dma_start(x[:, n % 4, :], src[at, :]).then_inc(x_in[n % 4], DMA)
                    if addend is not None:
                        if n >= 2:
                            sp.wait_ge(added, START + n - 1)
                        sp.dma_start(t[:, n % 2, :], addend[at, :]).then_inc(x_in[n % 4], DMA)

            @block.vector
            def _(dve):
                def statistics(s, n):
                    j, q = n % 2, n % 4
                    dve.wait_ge(x_in[q], START + (n // 4 + 1) * n_in * DMA)
                    if addend is not None:
                        s(dve.tensor_tensor(x[:, q, :], x[:, q, :], t[:, j, :], ALU.add))
                        dve.sem_inc(added, 1)
                    for c in range(2):
                        s(dve.bn_stats(stats[:, c, :], x[:, q, c * COL:(c + 1) * COL]))
                    s(dve.bn_aggr(mv[:, j, :], stats[:, :, :]))
                    if not center:
                        s(dve.scalar_tensor_tensor(sd[:, j:j + 1], mv[:, j, 0:1], mv[:, j, 0:1], mv[:, j, 1:2], ALU.mult, ALU.add))
                    var = mv[:, j, 1:2] if center else sd[:, j:j + 1]
                    dve.tensor_scalar(sd[:, j:j + 1], var, eps, None, ALU.add).then_inc(var_ready, 1)

                def scaled(s, n):
                    j, q = n % 2, n % 4
                    dve.wait_ge(sd_ready, START + n + 1)
                    s(dve.reciprocal(sd[:, j:j + 1], sd[:, j:j + 1]))
                    if n >= 2:
                        dve.wait_ge(turned, START + n - 1)
                    if center:
                        dve.tensor_scalar(xn[:, j, :], x[:, q, :], mv[:, j, 0:1], sd[:, j:j + 1], ALU.subtract, ALU.mult).then_inc(normed, 1)
                    else:
                        dve.tensor_scalar(xn[:, j, :], x[:, q, :], sd[:, j:j + 1], None, ALU.mult).then_inc(normed, 1)

                dve.wait_ge(const_in, START + n_const * DMA)
                if center:
                    dve.tensor_scalar(scale[:, :], scale[:, :], 1.0, None, ALU.add).then_inc(scale_ready, 1)
                s = Steps(dve, step, 0, nt * (STATS + 1))
                statistics(s, 0)
                for n in range(nt):
                    if n + 1 < nt:
                        statistics(s, n + 1)
                    scaled(s, n)
                s.end()

            @block.scalar
            def _(act):
                def root(n):
                    j = n % 2
                    act.wait_ge(var_ready, START + n + 1)
                    act.activation(sd[:, j:j + 1], sd[:, j:j + 1], ACT.Sqrt).then_inc(sd_ready, 1)
                    if addend is not None:
                        act.dma_start(src[n * P:(n + 1) * P, :], x[:, n % 4, :]).then_inc(stored[n % 4], DMA)

                if center:
                    act.wait_ge(scale_ready, START + 1)
                root(0)
                for n in range(nt):
                    if n + 1 < nt:
                        root(n + 1)
                    act.wait_ge(turned, START + n + 1)
                    for k in range(KC):
                        ins = act.activation(hT[:, k, tok0 + n * P:tok0 + (n + 1) * P], xT[:, n % 2, k, :], ACT.Identity,
                                             scale=scale[:, k:k + 1],
                                             bias=shift[:, k:k + 1] if shift_row is not None else 0.0)
                    ins.then_inc(placed, 1)
                if addend is not None:
                    for k in range(4):
                        act.wait_ge(stored[k], START + nt // 4 * DMA)

            @block.tensor
            def _(pe):
                pe.wait_ge(const_in, START + n_const * DMA)
                for n in range(nt):
                    pe.wait_ge(normed, START + n + 1)
                    if n >= 2:
                        pe.wait_ge(placed, START + n - 1)
                    for k in range(KC):
                        mm = pe.transpose(xT[:, n % 2, k, :], xn[:, n % 2, k * P:(k + 1) * P], ident[:, :])
                    mm.then_inc(turned, 1)


def product(nc, name, hT, nt, tok0, w, kc, chunks, looped, beside=None):
    with Phase(nc, name) as ph:
        wt = ph.sb("wt", [P, 2, kc, COL])
        ot = ph.sb("ot", [P, 2, nt, COL])
        acc = ph.ps("acc", [P, 8, COL])
        w_in = [ph.sem("w_in0"), ph.sem("w_in1")]
        made = [ph.sem("made0"), ph.sem("made1")]
        out_v = [ph.sem("out_v0"), ph.sem("out_v1")]
        out_s = [ph.sem("out_s0"), ph.sem("out_s1")]
        stored = [ph.sem("stored0"), ph.sem("stored1")]
        w_v = w.rearrange("(k p) n -> p k n", p=P)
        half = 0 if beside else (nt + 1) // 2
        beside_run = beside(ph) if beside else None
        bank = lambda j, t: (t if nt == 8 else j * nt + t)
        pairs = looped[0] if looped else 0
        tail = [(pairs + n // 2, n % 2) + c for n, c in enumerate(chunks)]

        def steps(eng, body):
            if pairs:
                with eng.Fori(0, pairs) as i:
                    for j in range(2):
                        body(i, j, looped[1](i, j), COL, looped[2](i, j))
            for trip, j, c, width, view in tail:
                body(trip, j, c, width, view)

        last = [0, 0]
        for j in range(2):
            last[j] = pairs + sum(1 for t in tail if t[1] == j)
        with ph.block() as block:
            @block.sync
            def _(sp):
                def load(trip, j, c, width, view):
                    sp.wait_ge(made[j], START + trip * nt)
                    sp.dma_start(wt[:, j, :, 0:width], w_v[:, :, bass.ds(c, width)]).then_inc(w_in[j], DMA)
                steps(sp, load)

            @block.tensor
            def _(pe):
                def body(trip, j, c, width, view):
                    pe.wait_ge(w_in[j], START + DMA * trip + DMA)
                    for t in range(nt):
                        out, n = (out_v, half) if t % 2 == 0 and not beside else (out_s, nt - half)
                        if nt == 8:
                            pe.wait_ge(out[1 - j], START + (trip + j - 1) * n + (t if beside else t // 2) + 1)
                        else:
                            pe.wait_ge(out[j], START + trip * n)
                        for k in range(kc):
                            mm = pe.matmul(acc[:, bank(j, t), 0:width], hT[:, k, (tok0 + t) * P:(tok0 + t + 1) * P],
                                           wt[:, j, k, 0:width], start=k == 0, stop=k == kc - 1)
                        mm.then_inc(made[j], 1)
                steps(pe, body)

            def copy_tiles(eng, copy, first, out_sem, trip, j, width):
                eng.wait_ge(stored[j], START + DMA * trip)
                for t in range(first, nt, 1 if beside else 2):
                    eng.wait_ge(made[j], START + trip * nt + t + 1)
                    copy(ot[:, j, t, 0:width], acc[:, bank(j, t), 0:width]).then_inc(out_sem[j], 1)

            @block.vector
            def _(dve):
                def body(trip, j, c, width, view):
                    copy_tiles(dve, dve.tensor_copy, 0, out_v, trip, j, width)
                if beside:
                    beside_run(dve)
                else:
                    steps(dve, body)

            @block.scalar
            def _(act):
                def body(trip, j, c, width, view):
                    copy_tiles(act, act.copy, 0 if beside else 1, out_s, trip, j, width)
                    if not beside:
                        act.wait_ge(out_v[j], START + (trip + 1) * half)
                    act.wait_ge(out_s[j], START + (trip + 1) * (nt - half))
                    act.dma_start(view, ot[:, j, :, 0:width]).then_inc(stored[j], DMA)
                steps(act, body)
                for j in range(2):
                    if last[j]:
                        act.wait_ge(stored[j], START + DMA * last[j])


def tiles(ap, cols):
    return ap[:, cols].rearrange("(t p) n -> p t n", p=P)


def mlstm_prep(nc, A, S, name, nt, row0, chunk0):
    z = S["z1"]
    NJ = 2 * H_B
    with Phase(nc, name) as ph:
        ident, ones = ph.sb("ident", [P, P]), ph.sb("ones", [P, P])
        upto, fromon = ph.sb("upto", [P, P]), ph.sb("fromon", [P, P])
        mask_ts, mask_st = ph.sb("mask_ts", [P, 2, P]), ph.sb("mask_st", [P, 2, P])
        cw = ph.sb("cw", [P, 3, 512])
        bg = ph.sb("bg", [P, 16])
        zq = ph.sb("zq", [P, 2, 3, 512])
        gt = ph.sb("gt", [P, 2, 16])
        va = ph.sb("va", [P, 2, H_B, VA])
        qk = ph.sb("qk", [P, 512])
        qkT = ph.sb("qkT", [P, 4, P])
        lf, lg = ph.sb("lf", [P, 16]), ph.sb("lg", [P, 16])
        sc = ph.sb("sc", [P, 4, NJ])
        a = ph.sb("a", [P, NJ])
        diag, am = ph.sb("diag", [P, NJ, P]), ph.sb("am", [P, NJ, P])
        wT = ph.sb("wT", [P, NJ, P])
        ea = ph.sb("ea", [P, NJ])
        kw = ph.sb("kw", [P, NJ, HK])
        num, own = ph.sb("num", [P, NJ, VA]), ph.sb("own", [P, H_B, VA])
        pT = ph.ps("pT", [P, 4, P])
        psmall = ph.ps("psmall", [P, 4 * NJ])
        pa = ph.ps("pa", [P, 3, 512])
        pb = ph.ps("pb", [P, 3, 512])
        const_in, in_ = ph.sem("const_in"), [ph.sem("in0"), ph.sem("in1")]
        step = ph.sem("step")
        conv, silu, qk_turned, qkT_ready = ph.sem("conv"), ph.sem("silu"), ph.sem("qk_turned"), ph.sem("qkT_ready")
        gated, absd, expd, logd = ph.sem("gated"), ph.sem("absd"), ph.sem("expd"), ph.sem("logd")
        lf_ready, b_made, diag_a, arow, diag_g, grow = (ph.sem(n) for n in ("lf_ready", "b_made", "diag_a", "arow", "diag_g", "grow"))
        gmask, wexp, ascale, eexp = ph.sem("gmask"), ph.sem("wexp"), ph.sem("ascale"), ph.sem("eexp")
        scores, weighted, kw_ready = ph.sem("scores"), ph.sem("weighted"), ph.sem("kw_ready")
        num_made, own_made, num_out, own_out = ph.sem("num_made"), ph.sem("own_made"), ph.sem("num_out"), ph.sem("own_out")
        stored, ones_set = ph.sem("stored"), ph.sem("ones_set")
        N_IN, N_OUT, DVE_STEPS = 5, 4, 26
        with ph.block() as block:
            @block.sync
            def _(sp):
                for dst, src in ((ident, "ident"), (ones, "ones"), (upto, "upto"), (fromon, "fromon")):
                    sp.dma_start(dst[:, :], A[src]).then_inc(const_in, DMA)
                sp.dma_start(mask_ts[:, :, :], A["mask_ts"]).then_inc(const_in, DMA)
                sp.dma_start(mask_st[:, :, :], A["mask_st"]).then_inc(const_in, DMA)
                for q in range(3):
                    sp.dma_start(cw[:, q, :], rows_to_all(A["conv_qk"][0, q])).then_inc(const_in, DMA)
                sp.dma_start(bg[:, :], rows_to_all(A["b_gates"][0])).then_inc(const_in, DMA)
                with sp.Fori(0, nt // 2) as i:
                    for j in range(2):
                        n = 2 * i + j
                        row = row0 + n * P
                        sp.wait_ge(stored, START + (n - 1) * N_OUT * DMA)
                        for q in range(3):
                            sp.dma_start(zq[:, j, q, :], z[bass.ds(row + (q - 1), P), 1024:1536]).then_inc(in_[j], DMA)
                        sp.dma_start(va[:, j, :, 0:HV], z[bass.ds(row, P), 1536:2048].rearrange("p (h v) -> p h v", h=H_B)).then_inc(in_[j], DMA)
                        sp.dma_start(gt[:, j, :], z[bass.ds(row, P), 2560:2576]).then_inc(in_[j], DMA)

            @block.vector
            def _(dve):
                dve.memset(va[:, :, :, HV:VA], 1.0).then_inc(ones_set, 1)
                dve.wait_ge(const_in, START + 10 * DMA)
                with dve.Fori(0, nt // 2) as i:
                    for j in range(2):
                        n = 2 * i + j
                        s = Steps(dve, step, n, DVE_STEPS)
                        dve.wait_ge(in_[j], START + (i + 1) * N_IN * DMA)
                        s(dve.tensor_tensor(gt[:, j, :], gt[:, j, :], bg[:, :], ALU.add))
                        s(dve.tensor_scalar(lf[:, :], gt[:, j, :], 0.0, None, ALU.min))
                        dve.scalar_tensor_tensor(lg[:, :], gt[:, j, :], -1.0, gt[:, j, :], ALU.mult, ALU.max).then_inc(gated, 1)
                        for q in range(3):
                            s(dve.tensor_tensor(zq[:, j, q, :], zq[:, j, q, :], cw[:, q, :], ALU.mult))
                        s(dve.tensor_tensor(qk[:, :], zq[:, j, 0, :], zq[:, j, 1, :], ALU.add))
                        dve.tensor_tensor(qk[:, :], qk[:, :], zq[:, j, 2, :], ALU.add).then_inc(conv, 1)
                        dve.wait_ge(logd, START + n + 1)
                        dve.tensor_tensor(lf[:, :], lf[:, :], lg[:, :], ALU.subtract).then_inc(lf_ready, 1)
                        dve.wait_ge(stored, START + n * N_OUT * DMA)
                        dve.wait_ge(b_made, START + n + 1)
                        s(dve.tensor_copy(sc[:, 0, :], psmall[:, 0:NJ]))
                        s(dve.tensor_copy(sc[:, 3, :], psmall[:, NJ:2 * NJ]))
                        for d in range(2):
                            s(dve.tensor_tensor(a[:, 4 * d:4 * d + 4], gt[:, j, 8 * d:8 * d + 4], sc[:, 0, 4 * d:4 * d + 4], ALU.subtract))
                        dve.tensor_tensor(diag[:, :, :], bc_mid(ident[:, :], NJ), bc_last(a[:, :], P), ALU.mult).then_inc(diag_a, 1)
                        dve.wait_ge(arow, START + n + 1)
                        for d in range(2):
                            s(dve.tensor_tensor(am[:, 4 * d:4 * d + 4, :], pa[:, d, :].rearrange("p (h t) -> p h t", h=4),
                                                bc_mid(mask_ts[:, d, :], 4), ALU.add))
                        s(dve.tensor_reduce(sc[:, 1, :], am[:, :, :], X, ALU.max))
                        s(dve.tensor_reduce(sc[:, 2, :], pa[:, 0:2, :].rearrange("p d (h t) -> p (d h) t", h=4), X, ALU.max))
                        dve.tensor_tensor(diag[:, :, :], bc_mid(ident[:, :], NJ), bc_last(sc[:, 1, :], P), ALU.mult).then_inc(diag_g, 1)
                        s(dve.tensor_tensor(ea[:, :], a[:, :], sc[:, 2, :], ALU.subtract))
                        dve.sem_inc(ascale, 1)
                        dve.wait_ge(grow, START + n + 1)
                        for d in range(2):
                            s(dve.tensor_tensor(am[:, 4 * d:4 * d + 4, :], pb[:, d, :].rearrange("p (h t) -> p h t", h=4),
                                                bc_mid(mask_st[:, d, :], 4), ALU.add))
                        dve.sem_inc(gmask, 1)
                        dve.wait_ge(scores, START + n + 1)
                        dve.wait_ge(wexp, START + n + 1)
                        for d in range(2):
                            for b, sT in enumerate((pT[:, 0:2, :], pa[:, 2, 0:2 * P].rearrange("p (m t) -> p m t", m=2))):
                                s(dve.tensor_tensor(wT[:, 4 * d + b:4 * d + 4:2, :], sT, wT[:, 4 * d + b:4 * d + 4:2, :], ALU.mult))
                        dve.sem_inc(weighted, 1)
                        dve.wait_ge(eexp, START + n + 1)
                        kh = qk[:, 256:512].rearrange("p (h c) -> p h c", h=4)
                        for d in range(2):
                            s(dve.tensor_tensor(kw[:, 4 * d:4 * d + 4, :], kh, bc_last(ea[:, 4 * d:4 * d + 4], HK), ALU.mult))
                        dve.sem_inc(kw_ready, 1)
                        dve.wait_ge(num_made, START + n + 1)
                        for b in range(3):
                            m = min(3, NJ - 3 * b)
                            s(dve.tensor_copy(num[:, 3 * b:3 * b + m, :], pa[:, b, 0:m * VA].rearrange("p (m v) -> p m v", m=m)))
                        dve.sem_inc(num_out, 1)
                        s.end()

            @block.scalar
            def _(act):
                with act.Fori(0, nt // 2) as i:
                    for j in range(2):
                        n = 2 * i + j
                        act.wait_ge(gated, START + n + 1)
                        act.activation(lg[:, :], lg[:, :], ACT.Exp, scale=-1.0).then_inc(expd, 1)
                        act.wait_ge(expd, START + n + 1)
                        act.activation(lg[:, :], lg[:, :], ACT.Ln, bias=1.0).then_inc(logd, 1)
                        act.wait_ge(conv, START + n + 1)
                        act.activation(qk[:, :], qk[:, :], ACT.Silu).then_inc(silu, 1)
                        act.wait_ge(stored, START + n * N_OUT * DMA)
                        act.wait_ge(qk_turned, START + n + 1)
                        act.activation(qkT[:, 0:2, :], pT[:, 0:2, :], ACT.Copy, scale=float(HK) ** -0.5)
                        act.activation(qkT[:, 2:4, :], pT[:, 2:4, :], ACT.Copy).then_inc(qkT_ready, 1)
                        act.wait_ge(ascale, START + n + 1)
                        act.activation(ea[:, :], ea[:, :], ACT.Exp).then_inc(eexp, 1)
                        act.wait_ge(gmask, START + n + 1)
                        for m in range(NJ):
                            ins = act.activation(wT[:, m, :], am[:, m, :], ACT.Exp, scale=-1.0, bias=a[:, m:m + 1])
                        ins.then_inc(wexp, 1)
                        act.wait_ge(own_made, START + n + 1)
                        for d in range(2):
                            ins = act.activation(own[:, 2 * d:2 * d + 2, :], pb[:, d, 0:2 * VA].rearrange("p (m v) -> p m v", m=2), ACT.Copy)
                        ins.then_inc(own_out, 1)
                        c = chunk0 + n
                        act.wait_ge(num_out, START + n + 1)
                        act.dma_start(S["num"][c], num[:, :, :]).then_inc(stored, DMA)
                        act.dma_start(S["sc"][c], sc[:, :, :]).then_inc(stored, DMA)
                        act.dma_start(S["qT"][c], qkT[:, 0:2, :]).then_inc(stored, DMA)
                        act.wait_ge(own_out, START + n + 1)
                        act.dma_start(S["own"][c], own[:, :, :]).then_inc(stored, DMA)
                act.wait_ge(stored, START + nt * N_OUT * DMA)

            @block.tensor
            def _(pe):
                pe.wait_ge(const_in, START + 10 * DMA)
                pe.wait_ge(ones_set, START + 1)
                with pe.Fori(0, nt // 2) as i:
                    for j in range(2):
                        n = 2 * i + j
                        pe.wait_ge(lf_ready, START + n + 1)
                        pe.matmul(psmall[:, 0:4], upto[:, :], lf[:, 4:8], start=True, stop=True)
                        pe.matmul(psmall[:, 4:8], fromon[:, :], lf[:, 12:16], start=True, stop=True)
                        pe.matmul(psmall[:, 8:12], ones[:, :], lf[:, 4:8], start=True, stop=True)
                        pe.matmul(psmall[:, 12:16], ones[:, :], lf[:, 12:16], start=True, stop=True).then_inc(b_made, 1)
                        pe.wait_ge(silu, START + n + 1)
                        for q in range(4):
                            mm = pe.transpose(pT[:, q, :], qk[:, q * P:(q + 1) * P], ident[:, :])
                        mm.then_inc(qk_turned, 1)
                        pe.wait_ge(diag_a, START + n + 1)
                        for d in range(2):
                            mm = pe.matmul(pa[:, d, :], ones[:, :], diag[:, 4 * d:4 * d + 4, :], start=True, stop=True)
                        mm.then_inc(arow, 1)
                        pe.wait_ge(own_out, START + n)
                        pe.wait_ge(diag_g, START + n + 1)
                        for d in range(2):
                            mm = pe.matmul(pb[:, d, :], ones[:, :], diag[:, 4 * d:4 * d + 4, :], start=True, stop=True)
                        mm.then_inc(grow, 1)
                        pe.wait_ge(qkT_ready, START + n + 1)
                        for h in range(H_B):
                            b = 64 * (h % 2)
                            out = pa[:, 2, (h // 2) * P:(h // 2 + 1) * P] if b else pT[:, h // 2, :]
                            mm = pe.matmul(out, qkT[b:b + 64, 2 + h // 2, :], qkT[b:b + 64, h // 2, :], start=True, stop=True)
                        mm.then_inc(scores, 1)
                        pe.wait_ge(weighted, START + n + 1)
                        for m in range(NJ):
                            mm = pe.matmul(pa[:, m // 3, (m % 3) * VA:(m % 3 + 1) * VA], wT[:, m, :], va[:, j, m % 4, :], start=True, stop=True)
                        mm.then_inc(num_made, 1)
                        pe.wait_ge(kw_ready, START + n + 1)
                        for m in range(NJ):
                            d, h = m // 4, m % 4
                            b = 64 * (h % 2)
                            mm = pe.matmul(pb[b:b + 64, d, (h // 2) * VA:(h // 2 + 1) * VA], kw[:, m, :], va[:, j, h, :], start=True, stop=True)
                        mm.then_inc(own_made, 1)


def mlstm_chain(nc, A, S):
    NJ = 2 * H_B
    with Phase(nc, "chain") as ph:
        num = ph.sb("num", [P, 2, NJ, VA])
        own = ph.sb("own", [P, 2, H_B, VA])
        qT = ph.sb("qT", [P, 2, 2, 2, P])
        sc = ph.sb("sc", [P, 2, 4, NJ])
        C = ph.sb("C", [P, H_B, VA])
        m0 = ph.sb("m0", [P, NJ])
        G = ph.sb("G", [P, NJ])
        w = ph.sb("w", [P, 2, NJ])
        wh = ph.sb("wh", [P, 2, H_B])
        g = ph.sb("g", [P, NJ])
        e = ph.sb("e", [P, 3, NJ])
        t = ph.sb("t", [P, NJ, VA])
        h = ph.sb("h", [P, 2, NJ, HV])
        den = ph.sb("den", [P, NJ])
        inter = ph.ps("inter", [P, 4, 512])
        in_ = [ph.sem("in0"), ph.sem("in1")]
        zeroed, step, w_ready, w_exp = ph.sem("zeroed"), ph.sem("step"), ph.sem("w_ready"), ph.sem("w_exp")
        inter_made, h_ready = ph.sem("inter_made"), ph.sem("h_ready")
        C_ready = ph.sem("C_ready")
        stored = [ph.sem("stored0"), ph.sem("stored1")]

        def load(sp, j, cf, cb):
            for d, c in ((0, cf), (1, cb)):
                hs = slice(4 * d, 4 * d + 4)
                sp.dma_start(num[:, j, hs, :], S["num"][c][:, hs, :]).then_inc(in_[j], DMA)
                sp.dma_start(own[:, j, 2 * d:2 * d + 2, :], S["own"][c][:, 2 * d:2 * d + 2, :]).then_inc(in_[j], DMA)
                sp.dma_start(qT[:, j, d, :, :], S["qT"][c]).then_inc(in_[j], DMA)
                sp.dma_start(sc[:, j, :, hs], S["sc"][c][:, :, hs]).then_inc(in_[j], DMA)

        with ph.block() as block:
            @block.sync
            def _(sp):
                load(sp, 0, 0, 1)
                load(sp, 1, 1, 0)
                with sp.Fori(0, NT // 2) as i:
                    for j in range(2):
                        k = 2 * i + j
                        sp.wait_ge(C_ready, START + k + 1)
                        load(sp, j, k + 2, 9 - k)
            @block.vector
            def _(dve):
                dve.memset(C[:, :, :], 0.0).then_inc(zeroed, 1)
                dve.memset(m0[:, :], 0.0).then_inc(zeroed, 1)
                dve.wait_ge(zeroed, START + 2)

                def output(s, i, k, j):
                    dve.wait_ge(inter_made, START + k + 1)
                    for d in range(2):
                        for b in range(2):
                            hs = slice(4 * d + b, 4 * d + 4, 2)
                            s(dve.tensor_tensor(t[:, hs, :], inter[:, 2 * b + d, 0:2 * VA].rearrange("p (m v) -> p m v", m=2),
                                                bc_last(e[:, 1, hs], VA), ALU.mult))
                    s(dve.tensor_tensor(num[:, j, :, :], num[:, j, :, :], bc_last(e[:, 0, :], VA), ALU.mult))
                    s(dve.tensor_tensor(t[:, :, :], t[:, :, :], num[:, j, :, :], ALU.add))
                    s(dve.scalar_tensor_tensor(den[:, :], t[:, :, HV], -1.0, t[:, :, HV], ALU.mult, ALU.max))
                    s(dve.tensor_tensor(den[:, :], den[:, :], e[:, 2, :], ALU.max))
                    s(dve.reciprocal(den[:, :], den[:, :]))
                    dve.wait_ge(stored[j], START + i * 2 * DMA)
                    s(dve.tensor_tensor(h[:, j, :, :], t[:, :, 0:HV], bc_last(den[:, :], HV), ALU.mult))
                    dve.sem_inc(h_ready, 1)

                def weights(s, j):
                    s(dve.tensor_tensor(G[:, :], m0[:, :], sc[:, j, 2, :], ALU.max))
                    s(dve.tensor_tensor(w[:, 0, :], m0[:, :], G[:, :], ALU.subtract))
                    s(dve.tensor_tensor(w[:, 1, :], sc[:, j, 2, :], G[:, :], ALU.subtract))
                    s(dve.tensor_tensor(g[:, :], m0[:, :], sc[:, j, 1, :], ALU.max))
                    s(dve.tensor_tensor(e[:, 0, :], sc[:, j, 1, :], g[:, :], ALU.subtract))
                    s(dve.tensor_tensor(e[:, 1, :], m0[:, :], g[:, :], ALU.subtract))
                    s(dve.scalar_tensor_tensor(e[:, 2, :], sc[:, j, 0, :], -1.0, g[:, :], ALU.mult, ALU.subtract))
                    s(dve.tensor_tensor(m0[:, :], sc[:, j, 3, :], G[:, :], ALU.add))
                    dve.sem_inc(w_ready, 1)

                def state(s, k, j):
                    dve.wait_ge(w_exp, START + k + 1)
                    for b in range(2):
                        s(dve.tensor_copy(wh[64 * b:64 * b + 64, :, :], w[64 * b:64 * b + 64, :, b::2]))
                    s(dve.tensor_tensor(own[:, j, :, :], own[:, j, :, :], bc_last(wh[:, 1, :], VA), ALU.mult))
                    s(dve.tensor_tensor(C[:, :, :], C[:, :, :], bc_last(wh[:, 0, :], VA), ALU.mult))
                    s(dve.tensor_tensor(C[:, :, :], C[:, :, :], own[:, j, :, :], ALU.add))
                    dve.sem_inc(C_ready, 1)

                CTX_STEPS, LAT_STEPS = 13, 23
                for k in range(2):
                    s = Steps(dve, step, k, CTX_STEPS)
                    dve.wait_ge(in_[k], START + 8 * DMA)
                    weights(s, k)
                    state(s, k, k)
                    s.end()
                with dve.Fori(0, NT // 2) as i:
                    for j in range(2):
                        k = 2 * i + j
                        s = Steps(dve, step, 0, LAT_STEPS)
                        s.base = 2 * CTX_STEPS + k * LAT_STEPS
                        dve.wait_ge(in_[j], START + (i + 2) * 8 * DMA)
                        weights(s, j)
                        dve.wait_ge(w_exp, START + k + 3)
                        output(s, i, k, j)
                        state(s, k + 2, j)
                        s.end()

            @block.scalar
            def _(act):
                def exps(k):
                    act.wait_ge(w_ready, START + k + 1)
                    act.activation(w[:, :, :], w[:, :, :], ACT.Exp)
                    act.activation(e[:, :, :], e[:, :, :], ACT.Exp).then_inc(w_exp, 1)
                for k in range(2):
                    exps(k)
                with act.Fori(0, NT // 2) as i:
                    for j in range(2):
                        k = 2 * i + j
                        exps(k + 2)
                        act.wait_ge(h_ready, START + k + 1)
                        act.dma_start(S["h"][0, k], h[:, j, 0:4, :]).then_inc(stored[j], DMA)
                        act.dma_start(S["h"][1, 7 - k], h[:, j, 4:8, :]).then_inc(stored[j], DMA)
                for j in range(2):
                    act.wait_ge(stored[j], START + NT * DMA)

            @block.tensor
            def _(pe):
                with pe.Fori(0, NT // 2) as i:
                    for j in range(2):
                        k = 2 * i + j
                        pe.wait_ge(in_[j], START + (i + 2) * 8 * DMA)
                        pe.wait_ge(C_ready, START + k + 2)
                        pe.wait_ge(h_ready, START + k)
                        for m in range(NJ):
                            d, hd = m // 4, m % 4
                            b = 64 * (hd % 2)
                            mm = pe.matmul(inter[:, 2 * (hd % 2) + d, (hd // 2) * VA:(hd // 2 + 1) * VA], qT[b:b + 64, j, d, hd // 2, :],
                                           C[b:b + 64, 2 * d + hd // 2, :], start=True, stop=True)
                        mm.then_inc(inter_made, 1)


def mixer_rows(nc, A, S, yT):
    with Phase(nc, "mixer") as ph:
        ident = ph.sb("ident", [P, P])
        wsT = ph.sb("wsT", [P, G_A, P])
        bs = ph.sb("bs", [P, G_A])
        rows = ph.sb("rows", [P, 3, 512])
        uv = ph.sb("uv", [P, 2, 2, 512])
        hh = ph.sb("hh", [P, 2, 2, 512])
        o = ph.sb("o", [P, 2, 512])
        stats = ph.sb("stats", [P, 5, 6])
        mv = ph.sb("mv", [P, 5, 2])
        sd = ph.sb("sd", [P, 5])
        vn = ph.sb("vn", [P, 512])
        hs = ph.sb("hs", [P, 512])
        y = ph.sb("y", [P, D])
        mixed = ph.ps("mixed", [P, 512])
        tp = ph.ps("tp", [P, KC, P])
        const_in, in_ = ph.sem("const_in"), [ph.sem("in0"), ph.sem("in1")]
        step, var_ready, sd_ready = ph.sem("step"), ph.sem("var_ready"), ph.sem("sd_ready")
        vn_ready, mixed_ready, y_ready, turned = ph.sem("vn_ready"), ph.sem("mixed_ready"), ph.sem("y_ready"), ph.sem("turned")
        placed, passed = ph.sem("placed"), ph.sem("passed")
        N_IN, STEPS = 4, 24
        with ph.block() as block:
            @block.sync
            def _(sp):
                sp.dma_start(ident[:, :], A["ident"]).then_inc(const_in, DMA)
                sp.dma_start(wsT[:, :, :], A["w_sT"]).then_inc(const_in, DMA)
                sp.dma_start(bs[:, :], A["b_sT"]).then_inc(const_in, DMA)
                for q, n in enumerate(("ln_v_g", "ln_v_b", "hn_g")):
                    sp.dma_start(rows[:, q, :], rows_to_all(A[n][0])).then_inc(const_in, DMA)
                with sp.Fori(0, NT // 2) as i:
                    for j in range(2):
                        n = 2 * i + j
                        sp.wait_ge(placed, START + n - 1)
                        z = S["z1"][bass.ds(ROW_LAT + n * P, P), :]
                        sp.dma_start(uv[:, j, :, :], z[:, 0:1024].rearrange("p (a n) -> p a n", a=2)).then_inc(in_[j], DMA)
                        sp.dma_start(o[:, j, :], z[:, 2048:2560]).then_inc(in_[j], DMA)
                        for d in range(2):
                            sp.dma_start(hh[:, j, d, :], S["h"][d, n].rearrange("p h v -> p (h v)")).then_inc(in_[j], DMA)

            @block.vector
            def _(dve):
                dve.wait_ge(const_in, START + 6 * DMA)
                with dve.Fori(0, NT // 2) as i:
                    for j in range(2):
                        n = 2 * i + j
                        s = Steps(dve, step, n, STEPS)
                        dve.wait_ge(in_[j], START + (i + 1) * N_IN * DMA)
                        s(dve.bn_stats(stats[:, 4, :], uv[:, j, 1, :]))
                        s(dve.tensor_tensor(hs[:, :], hh[:, j, 0, :], hh[:, j, 1, :], ALU.add))
                        for q in range(4):
                            s(dve.bn_stats(stats[:, q, :], hs[:, q * P:(q + 1) * P]))
                        for q in range(5):
                            s.settle(passed)
                            s(dve.bn_aggr(mv[:, q, :], stats[:, q, :]))
                        dve.tensor_scalar(sd[:, :], mv[:, :, 1], LN_EPS, None, ALU.add).then_inc(var_ready, 1)
                        dve.wait_ge(sd_ready, START + n + 1)
                        s(dve.reciprocal(sd[:, :], sd[:, :]))
                        s(dve.tensor_scalar(vn[:, :], uv[:, j, 1, :], mv[:, 4, 0:1], sd[:, 4:5], ALU.subtract, ALU.mult))
                        s(dve.tensor_tensor(vn[:, :], vn[:, :], rows[:, 0, :], ALU.mult))
                        dve.tensor_tensor(vn[:, :], vn[:, :], rows[:, 1, :], ALU.add).then_inc(vn_ready, 1)
                        for q in range(4):
                            s(dve.tensor_scalar(hs[:, q * P:(q + 1) * P], hs[:, q * P:(q + 1) * P], mv[:, q, 0:1], sd[:, q:q + 1], ALU.subtract, ALU.mult))
                        s(dve.tensor_tensor(hs[:, :], hs[:, :], rows[:, 2, :], ALU.mult))
                        dve.wait_ge(turned, START + n)
                        s(dve.tensor_tensor(y[:, 512:1024], hs[:, :], o[:, j, :], ALU.mult))
                        dve.wait_ge(mixed_ready, START + n + 1)
                        for q in range(4):
                            s(dve.scalar_tensor_tensor(y[:, q * P:(q + 1) * P], mixed[:, q * P:(q + 1) * P], bs[:, q:q + 1],
                                                       uv[:, j, 0, q * P:(q + 1) * P], ALU.add, ALU.mult))
                        dve.sem_inc(y_ready, 1)
                        s.end()

            @block.scalar
            def _(act):
                with act.Fori(0, NT // 2) as i:
                    for j in range(2):
                        n = 2 * i + j
                        act.wait_ge(var_ready, START + n + 1)
                        act.activation(o[:, j, :], o[:, j, :], ACT.Sigmoid)
                        act.activation(sd[:, :], sd[:, :], ACT.Sqrt).then_inc(sd_ready, 1)
                        act.wait_ge(turned, START + n + 1)
                        act.activation(yT[:, :, bass.ds(n * P, P)], tp[:, :, :], ACT.Copy).then_inc(placed, 1)

            @block.tensor
            def _(pe):
                pe.wait_ge(const_in, START + 6 * DMA)
                with pe.Fori(0, NT // 2) as i:
                    for j in range(2):
                        n = 2 * i + j
                        pe.wait_ge(vn_ready, START + n + 1)
                        for q in range(4):
                            mm = pe.matmul(mixed[:, q * P:(q + 1) * P], wsT[:, q, :], vn[:, q * P:(q + 1) * P], start=True, stop=True)
                        mm.then_inc(mixed_ready, 1)
                        pe.wait_ge(y_ready, START + n + 1)
                        pe.wait_ge(placed, START + n)
                        for k in range(KC):
                            mm = pe.transpose(tp[:, k, :], y[:, k * P:(k + 1) * P], ident[:, :])
                        mm.then_inc(turned, 1)


def deepnorm(nc, A, S, name, src, y, dst, gate_row, g_row, b_row, bias_row):
    DEEP = 4
    n_rows = 3 + (bias_row is not None)
    with Phase(nc, name) as ph:
        rows = ph.sb("rows", [P, 4, D])
        x = ph.sb("x", [P, DEEP, D])
        t = ph.sb("t", [P, DEEP, D])
        stats, mv, sd = ph.sb("stats", [P, 2, 6]), ph.sb("mv", [P, DEEP, 2]), ph.sb("sd", [P, DEEP])
        const_in, in_ = ph.sem("const_in"), [ph.sem(f"in{j}") for j in range(DEEP)]
        step, var_ready, sd_ready = ph.sem("step"), ph.sem("var_ready"), ph.sem("sd_ready")
        done, stored = ph.sem("done"), [ph.sem(f"stored{j}") for j in range(DEEP)]
        passed = ph.sem("passed")
        STEPS = 9 + (bias_row is not None)
        with ph.block() as block:
            @block.sync
            def _(sp):
                rr = [gate_row, g_row, b_row] + ([bias_row] if bias_row is not None else [])
                for q, r in enumerate(rr):
                    sp.dma_start(rows[:, q, :], rows_to_all(r)).then_inc(const_in, DMA)
                with sp.Fori(0, NT // DEEP) as i:
                    for j in range(DEEP):
                        n = DEEP * i + j
                        sp.wait_ge(stored[j], START + i * DMA)
                        sp.dma_start(x[:, j, :], src[bass.ds(n * P, P), :]).then_inc(in_[j], DMA)
                        sp.dma_start(t[:, j, :], y[bass.ds(n * P, P), :]).then_inc(in_[j], DMA)

            @block.vector
            def _(dve):
                def statistics(s, i, j):
                    dve.wait_ge(in_[j], START + (i + 1) * 2 * DMA)
                    if bias_row is not None:
                        s(dve.tensor_tensor(t[:, j, :], t[:, j, :], rows[:, 3, :], ALU.add))
                    s(dve.tensor_tensor(t[:, j, :], t[:, j, :], rows[:, 0, :], ALU.mult))
                    s(dve.scalar_tensor_tensor(t[:, j, :], x[:, j, :], ALPHA, t[:, j, :], ALU.mult, ALU.add))
                    for q in range(2):
                        s(dve.bn_stats(stats[:, q, :], t[:, j, q * COL:(q + 1) * COL]))
                    s.settle(passed)
                    s(dve.bn_aggr(mv[:, j, :], stats[:, :, :]))
                    dve.tensor_scalar(sd[:, j:j + 1], mv[:, j, 1:2], LN_EPS, None, ALU.add).then_inc(var_ready, 1)

                def finish(s, n, j):
                    dve.wait_ge(sd_ready, START + n + 1)
                    s(dve.reciprocal(sd[:, j:j + 1], sd[:, j:j + 1]))
                    s(dve.tensor_scalar(t[:, j, :], t[:, j, :], mv[:, j, 0:1], sd[:, j:j + 1], ALU.subtract, ALU.mult))
                    s(dve.tensor_tensor(t[:, j, :], t[:, j, :], rows[:, 1, :], ALU.mult))
                    s(dve.tensor_tensor(t[:, j, :], t[:, j, :], rows[:, 2, :], ALU.add))
                    dve.sem_inc(done, 1)

                dve.wait_ge(const_in, START + n_rows * DMA)
                with dve.Fori(0, NT // DEEP) as i:
                    s = Steps(dve, step, i, DEEP * STEPS)
                    statistics(s, i, 0)
                    for j in range(DEEP):
                        if j + 1 < DEEP:
                            statistics(s, i, j + 1)
                        finish(s, DEEP * i + j, j)
                    s.end()

            @block.scalar
            def _(act):
                with act.Fori(0, NT // DEEP) as i:
                    for j in range(DEEP):
                        n = DEEP * i + j
                        for m in ((0, 1), (2,), (3,), ())[j]:
                            act.wait_ge(var_ready, START + DEEP * i + m + 1)
                            act.activation(sd[:, m:m + 1], sd[:, m:m + 1], ACT.Sqrt).then_inc(sd_ready, 1)
                        act.wait_ge(done, START + n + 1)
                        act.dma_start(dst[bass.ds(n * P, P), :], t[:, j, :]).then_inc(stored[j], DMA)
                for j in range(DEEP):
                    act.wait_ge(stored[j], START + NT // DEEP * DMA)


def mlp(nc, A, S, hT):
    FB = D_FF // P
    HT = NT // 2
    for half in range(2):
        with ExitStack() as outer:
            aT = outer.enter_context(nc.sbuf_tensor(f"aT{half}", [P, FB, HT * P], F32))
            with Phase(nc, f"up{half}") as ph:
                w = ph.sb("w", [P, 2, KC, COL])
                b1 = ph.sb("b1", [P, 2, 4])
                r = ph.sb("r", [P, 2, HT * P])
                acc = ph.ps("acc", [P, 4, COL])
                w_in = [ph.sem("w_in0"), ph.sem("w_in1")]
                made, relu, squared = ph.sem("made"), ph.sem("relu"), ph.sem("squared")
                w_v = A["w1"][0].rearrange("(k p) n -> p k n", p=P)
                with ph.block() as block:
                    @block.sync
                    def _(sp):
                        with sp.Fori(0, FB // 8) as i:
                            for j in range(2):
                                sp.wait_ge(relu, START + 8 * i + 4 * j - 4)
                                c = 2 * i + j
                                sp.dma_start(w[:, j, :, :], w_v[:, :, bass.ds(c * COL, COL)]).then_inc(w_in[j], DMA)
                                sp.dma_start(b1[:, j, :], A["b1_cols"][:, bass.ds(c * 4, 4)]).then_inc(w_in[j], DMA)

                    @block.tensor
                    def _(pe):
                        with pe.Fori(0, FB // 8) as i:
                            for j in range(2):
                                pe.wait_ge(w_in[j], START + (i + 1) * 2 * DMA)
                                for f in range(4):
                                    pe.wait_ge(relu, START + 8 * i + 4 * j + f - 3)
                                    for k in range(KC):
                                        mm = pe.matmul(acc[:, f, :], w[:, j, k, f * P:(f + 1) * P],
                                                       hT[:, k, half * HT * P:(half + 1) * HT * P], start=k == 0, stop=k == KC - 1)
                                    mm.then_inc(made, 1)

                    @block.vector
                    def _(dve):
                        with dve.Fori(0, FB // 8) as i:
                            for j in range(2):
                                for f in range(4):
                                    n = 8 * i + 4 * j + f
                                    dve.wait_ge(made, START + n + 1)
                                    dve.wait_ge(squared, START + n - 1)
                                    dve.tensor_scalar(r[:, f % 2, :], acc[:, f, :], b1[:, j, f:f + 1], 0.0, ALU.add, ALU.max).then_inc(relu, 1)

                    @block.scalar
                    def _(act):
                        with act.Fori(0, FB // 8) as i:
                            for m in range(8):
                                n = 8 * i + m
                                act.wait_ge(relu, START + n + 1)
                                act.activation(aT[:, n, :], r[:, m % 2, :], ACT.Square).then_inc(squared, 1)
            with Phase(nc, f"down{half}") as ph:
                w = ph.sb("w", [P, 2, 4, D])
                ot = ph.sb("ot", [P, HT, 2, COL])
                acc = ph.ps("acc", [P, HT, 2, COL])
                w_in = [ph.sem("w_in0"), ph.sem("w_in1")]
                used, out_v, out_s, stored = ph.sem("used"), ph.sem("out_v"), ph.sem("out_s"), ph.sem("stored")
                w_v = A["w2"][0].rearrange("(f p) n -> p f n", p=P)
                with ph.block() as block:
                    @block.sync
                    def _(sp):
                        for c in range(FB // 4):
                            if c >= 2:
                                sp.wait_ge(used, START + c - 1)
                            sp.dma_start(w[:, c % 2, :, :], w_v[:, 4 * c:4 * c + 4, :]).then_inc(w_in[c % 2], DMA)

                    @block.tensor
                    def _(pe):
                        for c in range(FB // 4):
                            pe.wait_ge(w_in[c % 2], START + (c // 2 + 1) * DMA)
                            for f in range(4):
                                for t in range(HT):
                                    for q in range(2):
                                        mm = pe.matmul(acc[:, t, q, :], aT[:, 4 * c + f, t * P:(t + 1) * P],
                                                       w[:, c % 2, f, q * COL:(q + 1) * COL],
                                                       start=c == 0 and f == 0, stop=c == FB // 4 - 1 and f == 3)
                            mm.then_inc(used, 1)

                    @block.vector
                    def _(dve):
                        dve.wait_ge(used, START + FB // 4)
                        for t in range(HT):
                            dve.tensor_copy(ot[:, t, 0, :], acc[:, t, 0, :]).then_inc(out_v, 1)

                    @block.scalar
                    def _(act):
                        act.wait_ge(used, START + FB // 4)
                        for t in range(HT):
                            act.copy(ot[:, t, 1, :], acc[:, t, 1, :]).then_inc(out_s, 1)
                            act.wait_ge(out_s, START + t + 1)
                            act.wait_ge(out_v, START + t + 1)
                            n = half * HT + t
                            act.dma_start(S["t1"][n * P:(n + 1) * P, :], ot[:, t, :, :].rearrange("p a n -> p (a n)")).then_inc(stored, DMA)
                        act.wait_ge(stored, START + HT * DMA)


def first_block(nc, A, S):
    ada_phase(nc, A, S)
    row = lambda q, r: S["mod"][r, q * D:(q + 1) * D]
    z = S["z1"]
    with nc.sbuf_tensor("hT", [P, KC, SEQ + CTX], F32) as hT:
        norm_transpose(nc, "nx", A["x"][0], NT, hT, 0, row(1, 0), row(0, 0), A, LN_EPS, True)
        norm_transpose(nc, "nctx", A["ctx"][0], NTC, hT, SEQ, row(1, 1), row(0, 1), A, LN_EPS, True)
        lat, ctx = z[ROW_LAT:ROW_LAT + SEQ, :], z[ROW_CTX:ROW_CTX + CTX, :]
        cols = [(c, min(COL, D_IN - c)) for c in range(0, D_IN, COL)]
        product(nc, "zlat", hT, NT, 0, A["w_in"][0], KC, [(c, w, tiles(lat, slice(c, c + w))) for c, w in cols], None)
        product(nc, "zctx", hT, NTC, NT, A["w_in"][0], KC, [(c, w, tiles(ctx, slice(c, c + w))) for c, w in (cols[2], cols[3], cols[5])], None)
    zero_rows(nc, S, "zpad", [z[r:r + 1, 1024:1536] for r in (0, ROW_LAT - 2, ROW_LAT - 1, ROWS_Z1 - 1)])
    mlstm_prep(nc, A, S, "pctx", NTC, ROW_CTX, 0)
    mlstm_prep(nc, A, S, "plat", NT, ROW_LAT, NTC)
    mlstm_chain(nc, A, S)
    with nc.sbuf_tensor("yT1", [P, KC, SEQ], F32) as yT:
        mixer_rows(nc, A, S, yT)
        product(nc, "wout", yT, NT, 0, A["w_out"][0], KC, [(c, COL, tiles(S["t1"], slice(c, c + COL))) for c in (0, COL)], None)
    deepnorm(nc, A, S, "dn1", A["x"][0], S["t1"], S["xa"], row(2, 0), A["ln1_g"][0], A["ln1_b"][0], None)
    with nc.sbuf_tensor("hT2", [P, KC, SEQ], F32) as hT:
        norm_transpose(nc, "nmlp", S["xa"], NT, hT, 0, row(4, 0), row(3, 0), A, LN_EPS, True)
        mlp(nc, A, S, hT)
    deepnorm(nc, A, S, "dn2", S["xa"], S["t1"], S["x"], row(5, 0), A["ln2_g"][0], A["ln2_b"][0], A["b2"][0])


def zero_rows(nc, S, name, views):
    with Phase(nc, name) as ph:
        zero = ph.sb("zero", [1, 4136])
        zeroed, stored = ph.sem("zeroed"), ph.sem("stored")
        with ph.block() as block:
            @block.vector
            def _(dve):
                dve.memset(zero[:, :], 0.0).then_inc(zeroed, 1)

            @block.sync
            def _(sp):
                sp.wait_ge(zeroed, START + 1)
                for v in views:
                    sp.dma_start(v, zero[:, 0:v.shape[1]]).then_inc(stored, DMA)
                sp.wait_ge(stored, START + len(views) * DMA)


def scratch(nc):
    shapes = {"mod": (2, 6 * D), "z1": (ROWS_Z1, D_IN), "num": (10, P, 8, VA), "own": (10, P, 4, VA), "qT": (10, P, 2, P),
              "sc": (10, P, 4, 8), "h": (2, NT, P, H_B, HV), "t1": (SEQ, D), "xa": (SEQ, D), "x": (SEQ, D)}
    return {k: nc.dram_tensor(f"s_{k}", s, F32, kind="Internal").ap() for k, s in shapes.items()}


def constants():
    f = np.float32
    s, t = np.arange(P)[:, None], np.arange(P)[None, :]
    c = {"ident": np.eye(P, dtype=f), "ones": np.ones((P, P), f),
         "upto": (s <= t).astype(f), "fromon": (s >= t).astype(f)}
    c["mask_ts"] = np.stack([np.where(t <= s, 0, -BIG), np.where(t >= s, 0, -BIG)], 1).astype(f)
    c["mask_st"] = np.stack([np.where(s <= t, 0, BIG), np.where(s >= t, 0, BIG)], 1).astype(f)
    return c


def layouts(inputs):
    i = inputs
    c = np.stack([np.asarray(i["c"]).reshape(D), np.asarray(i["c_ctx"]).reshape(D)], -1)
    return {"cond_cols": np.ascontiguousarray(c.reshape(KC, P, 2).transpose(1, 0, 2)),
            "w_sT": np.ascontiguousarray(np.asarray(i["w_s"])[0].transpose(2, 0, 1)),
            "b_sT": np.ascontiguousarray(np.asarray(i["b_s"])[0].T),
            "b1_cols": np.ascontiguousarray(np.asarray(i["b1"]).reshape(D_FF // P, P).T)}


LAYERS = 2
HD = 64
NORM_EPS = 1e-6
GN_EPS = 64e-5
DECAY = float(np.exp(-0.5))
RW = 384
RWH = RW // HD
RW_IN = 4 * RW + 128
DSA_IN = 936
DSA0 = RW_IN
DIL0 = RW_IN + DSA_IN
IN2 = DIL0 + 4 * 384
DSA_H = 4
IDX_H, IDX_D = 8, 32
TOPK = 256
CH = 64
RATES = (1, 4, 16)


def heads(ap, n=RWH):
    return ap.rearrange("p (h c) -> p h c", h=n)


def rwkv(nc, A, S, l):
    with Phase(nc, "rwkv") as ph:
        ident, id64 = ph.sb("ident", [P, P]), ph.sb("id64", [P, HD])
        tri, blk = ph.sb("tri", [P, P]), ph.sb("blk", [P, P])
        masks = ph.sb("masks", [P, 4, P])
        first = ph.sb("first", [P, 2, P])
        levels = ph.sb("levels", [P, 5, P])
        mu = ph.sb("mu", [P, RW_IN])
        rows = ph.sb("rows", [P, 7, RW])
        ups = ph.sb("ups", [P, RW])
        zc, zp = ph.sb("zc", [P, 2, RW_IN]), ph.sb("zp", [P, 2, RW_IN])
        wdT = ph.sb("wdT", [P, P])
        la = ph.sb("la", [P, 2, RW])
        kk, k2, bb = ph.sb("kk", [P, RW]), ph.sb("k2", [P, RW]), ph.sb("b", [P, RW])
        t1, bv = ph.sb("t1", [P, RW]), ph.sb("bv", [P, 2, RW])
        n6, r6 = ph.sb("n6", [P, RWH]), ph.sb("r6", [P, RWH])
        ex, f = ph.sb("ex", [P, 6, RW]), ph.sb("f", [P, 7, RW])
        x4 = ph.sb("x4", [P, 4, RW])
        be, ke, rf = ph.sb("be", [P, 2, RW]), ph.sb("ke", [P, 2, RW]), ph.sb("rf", [P, 2, RW])
        xT = ph.sb("xT", [P, 3, 4, P])
        mT = ph.sb("mT", [P, RWH, 4, P])
        Tb = ph.sb("Tb", [P, 2, RWH, P])
        T, TT = Tb[:, 0], Tb[:, 1]
        LT, PS = ph.sb("LT", [P, RWH, P]), ph.sb("PS", [P, RWH, P])
        wv, uw = ph.sb("wv", [P, 2, RWH, P]), ph.sb("uw", [P, RWH, P])
        y0, r2 = ph.sb("y0", [P, RW]), ph.sb("r2", [P, RW])
        dg, tr, own = ph.sb("dg", [P, 2, RW]), ph.sb("tr", [P, RW]), ph.sb("own", [P, RW])
        St = ph.sb("St", [P, RW])
        y = ph.sb("y", [P, RW])
        yo = ph.sb("yo", [P, 2, RW])
        bk = ph.ps("bk", [P, 8, 512])
        const_in, in_, step = ph.sem("const_in"), [ph.sem("in0"), ph.sem("in1")], ph.sem("step")
        names = ("mixed tanhd wd_turned wdT_ready lowrank pre sig lw_ready cums n6_ready rn_ready ex_ready f_ready x4_ready turned xT_ready "
                 "scores scores_read A_ready T_first LT_ready P_made P_ready TP_made T_ready dv_made dv_ready uw_made uw_ready "
                 "last_made tr_ready r2_ready y0_ready S_made S_ready y_read var_ready sd_ready silu done zeroed").split()
        (mixed, tanhd, wd_turned, wdT_ready, lowrank, pre, sig, lw_ready, cums, n6_ready, rn_ready, ex_ready, f_ready, x4_ready, turned, xT_ready,
         scores, scores_read, A_ready, T_first, LT_ready, P_made, P_ready, TP_made, T_ready, dv_made, dv_ready, uw_made, uw_ready,
         last_made, tr_ready, r2_ready, y0_ready, S_made, S_ready, y_read, var_ready, sd_ready, silu, done, zeroed) = (ph.sem(n) for n in names)
        stored, passed = [ph.sem("stored0"), ph.sem("stored1")], ph.sem("passed")
        N_CONST, FRONT, BACK = 17, 33, 40
        two = lambda ap: ap.rearrange("p (m t) -> p m t", t=P)
        def trips(eng, tile):
            with eng.Fori(0, NT // 2 - 1) as i:
                for j in range(2):
                    tile(i, j, True)
            tile(NT // 2 - 1, 0, True)
            tile(NT // 2 - 1, 1, False)

        with ph.block() as block:
            @block.sync
            def _(sp):
                for dst, src in ((ident[:, :], A["ident"]), (id64[:, :], A["id64"]), (tri[:, :], A["tri64"]), (blk[:, :], A["blk64"]),
                                 (masks[:, :, :], A["rw_masks"]), (first[:, :, :], A["rw_first"]), (levels[:, :, :], A["rw_levels"]),
                                 (mu[:, :], rows_to_all(A["tshift_mu_2"][l])),
                                 (ups[0:64, :], A["rwkv_w_up_2"][l]), (ups[64:128, :], A["rwkv_a_up_2"][l])):
                    sp.dma_start(dst, src).then_inc(const_in, DMA)
                for q, n in enumerate("w0 a0 k_k k_a r_k ln_g ln_b".split()):
                    src = A[f"rwkv_{n}_2"][l]
                    if n == "r_k":
                        src = src.rearrange("h c -> (h c)")
                    sp.dma_start(rows[:, q, :], rows_to_all(src)).then_inc(const_in, DMA)

                def load(m, j):
                    sp.dma_start(zc[:, j, :], S["z2"][bass.ds(m * P + 1, P), 0:RW_IN]).then_inc(in_[j], DMA)
                    sp.dma_start(zp[:, j, :], S["z2"][bass.ds(m * P, P), 0:RW_IN]).then_inc(in_[j], DMA)
                load(0, 0)
                load(1, 1)
                with sp.Fori(0, NT // 2 - 1) as i:
                    for j in range(2):
                        sp.wait_ge(stored[j], START + (i + 1) * DMA)
                        load(2 * i + j + 2, j)

            @block.vector
            def _(dve):
                def front(s, m, b, trip):
                    tt = lambda o, a, c, op: s(dve.tensor_tensor(o, a, c, op))
                    z = zc[:, b, :]
                    r, k, v, g = (z[:, q * RW:(q + 1) * RW] for q in range(4))

                    def shift():
                        dve.wait_ge(in_[b], START + (trip + 1) * 2 * DMA)
                        tt(zp[:, b, :], zp[:, b, :], z, ALU.subtract)
                        tt(zp[:, b, :], zp[:, b, :], mu[:, :], ALU.mult)
                        tt(z, z, zp[:, b, :], ALU.add)
                        dve.sem_inc(mixed, 1)
                        tt(kk[:, :], k, rows[:, 2, :], ALU.mult)
                        tt(t1[:, :], kk[:, :], kk[:, :], ALU.mult)
                        s(dve.tensor_reduce(n6[:, :], heads(t1[:, :]), X, ALU.add))
                        dve.sem_inc(n6_ready, 1)

                    def unit():
                        dve.wait_ge(rn_ready, START + m + 1)
                        s(dve.tensor_scalar(n6[:, :], n6[:, :], 1e-12, None, ALU.max))
                        s(dve.reciprocal(n6[:, :], n6[:, :]))
                        tt(heads(kk[:, :]), heads(kk[:, :]), bc_last(n6[:, :], HD), ALU.mult)

                    def rates():
                        dve.wait_ge(lowrank, START + m + 1)
                        for q in range(2):
                            tt(la[:, q, :], bk[:, 6 + q, 0:RW], rows[:, q, :], ALU.add)
                        dve.sem_inc(pre, 1)

                    def keys():
                        dve.wait_ge(sig, START + m + 1)
                        s(dve.tensor_scalar(la[:, 0, :], la[:, 0, :], -DECAY, None, ALU.mult))
                        dve.sem_inc(lw_ready, 1)
                        s(dve.scalar_tensor_tensor(t1[:, :], la[:, 1, :], -1.0, rows[:, 3, :], ALU.add, ALU.mult))
                        s(dve.scalar_tensor_tensor(k2[:, :], t1[:, :], 1.0, k, ALU.add, ALU.mult))
                        tt(bb[:, :], kk[:, :], la[:, 1, :], ALU.mult)
                        tt(t1[:, :], r, k2[:, :], ALU.mult)
                        tt(t1[:, :], t1[:, :], rows[:, 4, :], ALU.mult)
                        s(dve.tensor_reduce(r6[:, :], heads(t1[:, :]), X, ALU.add))
                        tt(heads(bv[:, b, :]), heads(v), bc_last(r6[:, :], HD), ALU.mult)

                    def exponents():
                        dve.wait_ge(cums, START + m + 1)
                        s(dve.tensor_copy(ex[:, 4:6, :], bk[:, 6:8, 0:RW]))
                        s(dve.scalar_tensor_tensor(ex[:, 0, :], ex[:, 5, :], -0.5, ex[:, 4, :], ALU.mult, ALU.add))
                        tt(ex[:, 1, :], ex[:, 0, :], la[:, 0, :], ALU.subtract)
                        tt(ex[:, 2, :], ex[:, 5, :], ex[:, 4, :], ALU.subtract)
                        tt(ex[:, 3, :], ex[:, 4, :], la[:, 0, :], ALU.subtract)
                        dve.sem_inc(ex_ready, 1)

                    def scaled():
                        dve.wait_ge(f_ready, START + m + 1)
                        tt(x4[:, 0, :], kk[:, :], f[:, 1, :], ALU.mult)
                        tt(x4[:, 1, :], r, f[:, 0, :], ALU.mult)
                        tt(x4[:, 2, :], bb[:, :], f[:, 6, :], ALU.mult)
                        tt(x4[:, 3, :], k2[:, :], f[:, 6, :], ALU.mult)
                        dve.sem_inc(x4_ready, 1)
                        tt(be[:, b, :], bb[:, :], f[:, 2, :], ALU.mult)
                        tt(ke[:, b, :], k2[:, :], f[:, 2, :], ALU.mult)
                        tt(rf[:, b, :], r, f[:, 4, :], ALU.mult)
                        tt(wv[:, b, :, HD:P], heads(kk[:, :]), heads(f[:, 3, :]), ALU.mult)
                        tt(heads(dg[:, b, :]), heads(f[:, 5, :]), bc_mid(id64[:, :], RWH), ALU.mult)

                    return [shift, unit, rates, keys, exponents, scaled]

                def tile(i, j, nxt):
                    n = 2 * i + j
                    s = Steps(dve, step, 0, FRONT + BACK)
                    s.base = FRONT + n * (FRONT + BACK)
                    tt = lambda o, a, c, op: s(dve.tensor_tensor(o, a, c, op))
                    g = zc[:, j, 3 * RW:4 * RW]
                    parts = front(s, n + 1, 1 - j, i + j) if nxt else [lambda: None] * 6
                    for h in range(RWH):
                        dve.wait_ge(scores, START + n * RWH + h + 1)
                        tt(mT[:, h, :, :], two(bk[:, 2 + h % 4, :]), masks[:, :, :], ALU.mult)
                        dve.sem_inc(scores_read, 1)
                    dve.wait_ge(A_ready, START + n + 1)
                    for q in range(2):
                        tt(T[:, q::2, :], two(bk[:, q, 0:3 * P]), bc_mid(first[:, 0, :], 3), ALU.mult)
                    tt(T, bc_mid(ident[:, :], RWH), T, ALU.subtract)
                    tt(TT, mT[:, :, 0, :], bc_mid(first[:, 1, :], RWH), ALU.mult)
                    tt(TT, bc_mid(ident[:, :], RWH), TT, ALU.subtract)
                    for q in range(5):
                        tt(LT[:, :, :], mT[:, :, 0, :], bc_mid(levels[:, q, :], RWH), ALU.mult)
                        dve.sem_inc(LT_ready, 1)
                        parts[q]()
                        dve.wait_ge(TP_made, START + 5 * n + q + 1)
                        k0 = 0 if q < 4 else 2
                        tv = Tb[:, :, :, :].rearrange("p a (m h) t -> p (a m) (h t)", m=2)[:, k0:4, :]
                        tt(tv, tv, bk[:, 2 + k0:6, 0:3 * P], ALU.subtract)
                    dve.sem_inc(T_ready, 1)
                    parts[5]()
                    dve.wait_ge(last_made, START + n + 1)
                    for c in range(2):
                        pr = slice(64 * c, 64 * c + 64)
                        tt(tr[pr, :], bk[pr, 7 * (1 - c), 0:RW], dg[pr, j, :], ALU.add)
                    for c in range(2):
                        pr = slice(64 * (1 - c), 64 * (1 - c) + 64)
                        s(dve.tensor_copy(own[pr, :], bk[pr, 1 + c, 0:RW]))
                    dve.sem_inc(tr_ready, 1)
                    for c in range(2):
                        pr = slice(64 * (1 - c), 64 * (1 - c) + 64)
                        dve.wait_ge(S_made, START + 2 * n + c + 1)
                        tt(St[pr, :], bk[pr, 5 + c, 0:RW], own[pr, :], ALU.add)
                        dve.sem_inc(S_ready, 1)
                    dve.wait_ge(y0_ready, START + n + 1)
                    tt(y[:, :], bk[:, 3, 0:RW], y0[:, :], ALU.add)
                    dve.sem_inc(y_read, 1)
                    s(dve.tensor_reduce(r6[:, :], heads(y[:, :]), X, ALU.add))
                    s(dve.tensor_scalar(r6[:, :], r6[:, :], 1.0 / HD, None, ALU.mult))
                    tt(heads(y[:, :]), heads(y[:, :]), bc_last(r6[:, :], HD), ALU.subtract)
                    tt(t1[:, :], y[:, :], y[:, :], ALU.mult)
                    s(dve.tensor_reduce(r6[:, :], heads(t1[:, :]), X, ALU.add))
                    s(dve.tensor_scalar(r6[:, :], r6[:, :], 1.0 / HD, GN_EPS, ALU.mult, ALU.add))
                    dve.sem_inc(var_ready, 1)
                    dve.wait_ge(sd_ready, START + n + 1)
                    s(dve.reciprocal(r6[:, :], r6[:, :]))
                    tt(heads(y[:, :]), heads(y[:, :]), bc_last(r6[:, :], HD), ALU.mult)
                    tt(y[:, :], y[:, :], rows[:, 5, :], ALU.mult)
                    tt(y[:, :], y[:, :], rows[:, 6, :], ALU.add)
                    tt(y[:, :], y[:, :], bv[:, j, :], ALU.add)
                    dve.wait_ge(silu, START + n + 1)
                    tt(yo[:, j, :], y[:, :], g, ALU.mult)
                    dve.sem_inc(done, 1)
                    if nxt:
                        s.end()

                dve.memset(St[:, :], 0.0).then_inc(zeroed, 1)
                dve.wait_ge(zeroed, START + 1)
                dve.wait_ge(const_in, START + N_CONST * DMA)
                s = Steps(dve, step, 0, FRONT)
                for part in front(s, 0, 0, 0):
                    part()
                s.end()
                trips(dve, tile)

            @block.scalar
            def _(act):
                def front(m, b, trip):
                    def shifted():
                        act.wait_ge(mixed, START + m + 1)
                        act.activation(zc[:, b, 4 * RW:4 * RW + 64], zc[:, b, 4 * RW:4 * RW + 64], ACT.Tanh).then_inc(tanhd, 1)
                        act.activation(zc[:, b, 3 * RW:4 * RW], zc[:, b, 3 * RW:4 * RW], ACT.Silu).then_inc(silu, 1)
                        act.wait_ge(n6_ready, START + m + 1)
                        act.activation(n6[:, :], n6[:, :], ACT.Sqrt).then_inc(rn_ready, 1)

                    def low():
                        act.wait_ge(wd_turned, START + m + 1)
                        act.activation(wdT[:, :], bk[:, 7, RW:RW + P], ACT.Copy).then_inc(wdT_ready, 1)

                    def sigmoids():
                        act.wait_ge(pre, START + m + 1)
                        act.activation(la[:, :, :], la[:, :, :], ACT.Sigmoid).then_inc(sig, 1)

                    def exps():
                        act.wait_ge(ex_ready, START + m + 1)
                        act.activation(f[:, 6, :], ex[:, 0, :], ACT.Exp, scale=-1.0)
                        act.activation(f[:, 0:6, :], ex[:, :, :], ACT.Exp).then_inc(f_ready, 1)

                    return [shifted, low, sigmoids, lambda: None, exps]

                def tile(i, j, nxt):
                    n = 2 * i + j
                    parts = front(n + 1, 1 - j, i + j) if nxt else [lambda: None] * 5
                    for q in range(3):
                        act.wait_ge(turned, START + 3 * n + q + 1)
                        act.activation(xT[:, q, :, :], two(bk[:, (6, 7, 0)[q], :]), ACT.Copy).then_inc(xT_ready, 1)
                    for q in range(5):
                        act.wait_ge(P_made, START + 5 * n + q + 1)
                        act.activation(PS[:, :, :].rearrange("p (m h) t -> p m (h t)", m=2), bk[:, 0:2, 0:3 * P], ACT.Copy).then_inc(P_ready, 1)
                        parts[q]()
                    act.wait_ge(dv_made, START + n + 1)
                    act.activation(wv[:, j, :, 0:HD], heads(bk[:, 0, 0:RW]), ACT.Copy).then_inc(dv_ready, 1)
                    act.wait_ge(uw_made, START + n + 1)
                    act.activation(uw[:, :, :].rearrange("p (m h) t -> p m (h t)", m=2), bk[:, 2:4, 0:3 * P], ACT.Copy, scale=-1.0).then_inc(uw_ready, 1)
                    act.wait_ge(last_made, START + n + 1)
                    for c in range(2):
                        pr = slice(64 * c, 64 * c + 64)
                        ins = act.activation(r2[pr, :], bk[pr, 5 + c, 0:RW], ACT.Copy)
                    ins.then_inc(r2_ready, 1)
                    act.activation(y0[:, :], bk[:, 4, 0:RW], ACT.Copy).then_inc(y0_ready, 1)
                    act.wait_ge(var_ready, START + n + 1)
                    act.activation(r6[:, :], r6[:, :], ACT.Sqrt).then_inc(sd_ready, 1)
                    act.wait_ge(done, START + n + 1)
                    act.dma_start(S["y2"][bass.ds(n * P, P), 0:RW], yo[:, j, :]).then_inc(stored[j], DMA)

                for part in front(0, 0, 0):
                    part()
                trips(act, tile)
                for j in range(2):
                    act.wait_ge(stored[j], START + NT // 2 * DMA)

            @block.tensor
            def _(pe):
                def front(m, b):
                    def turn_low():
                        pe.wait_ge(tanhd, START + m + 1)
                        pe.transpose(bk[:, 7, RW:RW + P], zc[:, b, 4 * RW:4 * RW + P], ident[:, :]).then_inc(wd_turned, 1)

                    def low():
                        pe.wait_ge(wdT_ready, START + m + 1)
                        for q in range(2):
                            pr = slice(64 * q, 64 * q + 64)
                            mm = pe.matmul(bk[:, 6 + q, 0:RW], wdT[pr, :], ups[pr, :], start=True, stop=True)
                        mm.then_inc(lowrank, 1)

                    def sums():
                        pe.wait_ge(lw_ready, START + m + 1)
                        pe.matmul(bk[:, 6, 0:RW], tri[:, :], la[:, 0, :], start=True, stop=True)
                        pe.matmul(bk[:, 7, 0:RW], blk[:, :], la[:, 0, :], start=True, stop=True).then_inc(cums, 1)

                    return [turn_low, low, lambda: None, sums, lambda: None]

                def tile(i, j, nxt):
                    n = 2 * i + j
                    parts = front(n + 1, 1 - j) if nxt else [lambda: None] * 5
                    v = heads(zc[:, j, 2 * RW:3 * RW])
                    pe.wait_ge(x4_ready, START + n + 1)
                    pe.wait_ge(y_read, START + n)
                    for q in range(3):
                        for m in range(4):
                            mm = pe.transpose(bk[:, (6, 7, 0)[q], m * P:(m + 1) * P], x4[:, m, q * P:(q + 1) * P], ident[:, :])
                        mm.then_inc(turned, 1)
                    for h in range(RWH):
                        pr = slice(64 * (h % 2), 64 * (h % 2) + 64)
                        if h % 2 == 0:
                            pe.wait_ge(xT_ready, START + 3 * n + h // 2 + 1)
                        if h >= 4:
                            pe.wait_ge(scores_read, START + n * RWH + h - 3)
                        kr = xT[pr, h // 2, 0:2, :]
                        pe.matmul(bk[:, 2 + h % 4, 0:256], xT[pr, h // 2, 2, :], kr, start=True, stop=True)
                        pe.matmul(bk[:, 2 + h % 4, 256:512], xT[pr, h // 2, 3, :], kr, start=True, stop=True).then_inc(scores, 1)
                    for h in range(RWH):
                        pr = slice(64 * (h % 2), 64 * (h % 2) + 64)
                        mm = pe.matmul(bk[:, h % 2, (h // 2) * P:(h // 2 + 1) * P], xT[pr, h // 2, 0, :], xT[pr, h // 2, 2, :], start=True, stop=True)
                    mm.then_inc(A_ready, 1)
                    for q in range(5):
                        pe.wait_ge(LT_ready, START + 5 * n + q + 1)
                        for h in range(RWH):
                            mm = pe.matmul(bk[:, h // 3, (h % 3) * P:(h % 3 + 1) * P], LT[:, h, :], T[:, h, :], start=True, stop=True)
                        mm.then_inc(P_made, 1)
                        pe.wait_ge(P_ready, START + 5 * n + q + 1)
                        for h in range(RWH):
                            at = slice((h % 3) * P, (h % 3 + 1) * P)
                            if q < 4:
                                pe.matmul(bk[:, 2 + h // 3, at], TT[:, h, :], PS[:, h, :], start=True, stop=True)
                            mm = pe.matmul(bk[:, 4 + h // 3, at], PS[:, h, :], TT[:, h, :], start=True, stop=True)
                        mm.then_inc(TP_made, 1)
                        parts[q]()
                    for h in range(RWH):
                        mm = pe.matmul(bk[:, 0, h * HD:(h + 1) * HD], mT[:, h, 2, :], v[:, h, :], start=True, stop=True)
                    mm.then_inc(dv_made, 1)
                    pe.wait_ge(dv_ready, START + n + 1)
                    pe.wait_ge(T_ready, START + n + 1)
                    for h in range(RWH):
                        mm = pe.matmul(bk[:, 2 + h // 3, (h % 3) * P:(h % 3 + 1) * P], TT[:, h, :], wv[:, j, h, :], start=True, stop=True)
                    mm.then_inc(uw_made, 1)
                    pe.wait_ge(uw_ready, START + n + 1)
                    for h in range(RWH):
                        at = slice(h * HD, (h + 1) * HD)
                        pe.matmul(bk[:, 4, at], mT[:, h, 1, :], uw[:, h, 0:HD], start=True, stop=False)
                        pe.matmul(bk[:, 4, at], mT[:, h, 3, :], v[:, h, :], start=False, stop=True)
                    for c in range(2):
                        pr, po = slice(64 * c, 64 * c + 64), slice(64 * (1 - c), 64 * (1 - c) + 64)
                        for h in range(RWH):
                            at = slice(h * HD, (h + 1) * HD)
                            W = uw[pr, h, HD:P]
                            pe.matmul(bk[pr, 5 + c, at], W, mT[pr, h, 1, 64 * c:64 * c + 64], start=True, stop=False)
                            pe.matmul(bk[pr, 5 + c, at], rf[pr, j, at], ident[pr, 64 * c:64 * c + 64], start=False, stop=True)
                            pe.matmul(bk[pr, 7 * (1 - c), at], W, be[pr, j, at], start=True, stop=True)
                            pe.matmul(bk[po, 1 + c, at], be[pr, j, at], uw[pr, h, 0:HD], start=True, stop=False)
                            mm = pe.matmul(bk[po, 1 + c, at], ke[pr, j, at], v[pr, h, :], start=False, stop=True)
                    mm.then_inc(last_made, 1)
                    for c in range(2):
                        pr, po = slice(64 * c, 64 * c + 64), slice(64 * (1 - c), 64 * (1 - c) + 64)
                        if c == 0:
                            pe.wait_ge(r2_ready, START + n + 1)
                            pe.wait_ge(tr_ready, START + n + 1)
                        else:
                            pe.wait_ge(S_ready, START + 2 * n + 1)
                        pe.sem_inc(passed, 1)
                        for h in range(RWH):
                            at = slice(h * HD, (h + 1) * HD)
                            pe.matmul(bk[pr, 3, at], r2[pr, at], St[pr, at], start=True, stop=True)
                        for h in range(RWH):
                            at = slice(h * HD, (h + 1) * HD)
                            mm = pe.matmul(bk[po, 5 + c, at], tr[pr, at], St[pr, at], start=True, stop=True)
                        mm.then_inc(S_made, 1)

                pe.wait_ge(const_in, START + N_CONST * DMA)
                for part in front(0, 0):
                    part()
                trips(pe, tile)


def rope(s, dve, x, x1, x2, cos, sin, ta, tb):
    s(dve.tensor_tensor(ta[0], x1, cos, ALU.mult))
    s(dve.tensor_tensor(ta[1], x2, sin, ALU.mult))
    s(dve.tensor_tensor(tb[0], x2, cos, ALU.mult))
    s(dve.tensor_tensor(tb[1], x1, sin, ALU.mult))
    s(dve.tensor_tensor(x1, ta[0], ta[1], ALU.subtract))
    s(dve.tensor_tensor(x2, tb[0], tb[1], ALU.add))


def dsa_prep(nc, A, S, B):
    with Phase(nc, "dprep") as ph:
        ident = ph.sb("ident", [P, P])
        cs = ph.sb("cs", [P, NT, 2, 12])
        z = ph.sb("z", [P, 2, DSA_IN])
        kd, ikd = ph.sb("kd", [P, 2, HD]), ph.sb("ikd", [P, 4, IDX_D])
        tmp = ph.sb("tmp", [P, 4, 9 * 8])
        pT = ph.ps("pT", [P, 2, 8, P])
        const_in, in_, step = ph.sem("const_in"), [ph.sem("in0"), ph.sem("in1")], ph.sem("step")
        roped, turned, placed = ph.sem("roped"), ph.sem("turned"), ph.sem("placed")
        STEPS = 15
        with ph.block() as block:
            @block.sync
            def _(sp):
                sp.dma_start(ident[:, :], A["ident"]).then_inc(const_in, DMA)
                sp.dma_start(cs[:, :, :, :], A["rope_dsa"]).then_inc(const_in, DMA)
                with sp.Fori(0, NT // 2) as i:
                    for j in range(2):
                        sp.wait_ge(placed, START + 2 * i + j - 1)
                        sp.dma_start(z[:, j, :], S["z2"][bass.ds((2 * i + j) * P + 1, P), DSA0:DIL0]).then_inc(in_[j], DMA)

            @block.vector
            def _(dve):
                dve.wait_ge(const_in, START + 2 * DMA)
                with dve.Fori(0, NT // 2) as i:
                    for j in range(2):
                        n = 2 * i + j
                        s = Steps(dve, step, n, STEPS)
                        dve.wait_ge(in_[j], START + (i + 1) * DMA)
                        for c0, nh, w, half, f0 in ((0, 5, HD, 8, 0), (384, 9, IDX_D, 4, 8)):
                            x = z[:, j, c0:c0 + nh * w].rearrange("p (h c) -> p h c", h=nh)
                            tv = [tmp[:, q, 0:nh * half].rearrange("p (h c) -> p h c", h=nh) for q in range(4)]
                            cos, sin = (cs[:, bass.ds(n, 1), q, f0:f0 + half].to_broadcast([P, nh, half]) for q in range(2))
                            rope(s, dve, x, x[:, :, 0:half], x[:, :, half:2 * half], cos, sin, tv[0:2], tv[2:4])
                        dve.wait_ge(turned, START + n)
                        s(dve.tensor_copy(kd[:, :, :], bc_mid(z[:, j, 256:320], 2)))
                        s(dve.tensor_copy(ikd[:, :, :], bc_mid(z[:, j, 640:672], 4)))
                        s(dve.tensor_scalar(B["iw"][:, bass.ds(n, 1), :], z[:, j, 672:680].unsqueeze(1), float(IDX_H) ** -0.5, None, ALU.mult))
                        dve.sem_inc(roped, 1)
                        s.end()

            @block.tensor
            def _(pe):
                pe.wait_ge(const_in, START + 2 * DMA)
                with pe.Fori(0, NT // 2) as i:
                    for j in range(2):
                        n = 2 * i + j
                        pe.wait_ge(roped, START + n + 1)
                        pe.wait_ge(placed, START + n)
                        src = [z[:, j, 0:128], z[:, j, 128:256], kd[:, :, :], z[:, j, 384:512], z[:, j, 512:640], ikd[:, :, :]]
                        for q, x in enumerate(src):
                            mm = pe.transpose(pT[:, j, q, :], x, ident[:, :])
                        mm.then_inc(turned, 1)

            @block.scalar
            def _(act):
                with act.Fori(0, NT // 2) as i:
                    for j in range(2):
                        n = 2 * i + j
                        act.wait_ge(in_[j], START + (i + 1) * DMA)
                        act.activation(B["v"][:, bass.ds(n, 1), :], z[:, j, 320:384].unsqueeze(1), ACT.Copy)
                        act.activation(B["g"][:, bass.ds(n, 1), :], z[:, j, 680:936].unsqueeze(1), ACT.Silu)
                        act.wait_ge(turned, START + n + 1)
                        at = bass.ds(n * P, P)
                        act.activation(B["qT"][:, :, at], pT[:, j, 0:2, :], ACT.Copy)
                        act.activation(B["kT"][:, at], pT[:, j, 2, :], ACT.Copy)
                        act.activation(B["iqT"][:, :, at], pT[:, j, 3:5, :], ACT.Copy)
                        act.activation(B["ikT"][:, at], pT[:, j, 5, :], ACT.Copy).then_inc(placed, 1)


T0 = TOPK // P
NS = NT - T0
BISECT = 32


def dsa_scores(nc, A, S, B, sc):
    with Phase(nc, "dsc") as ph:
        causal = ph.sb("causal", [P, P])
        rl = ph.sb("rl", [P, 2, SEQ])
        acc = ph.ps("acc", [P, 4, 2, COL])
        const_in, made, relu, summed, step = (ph.sem(n) for n in ("const_in", "made", "relu", "summed", "step"))
        with ph.block() as block:
            @block.sync
            def _(sp):
                sp.dma_start(causal[:, :], A["causal_ts"]).then_inc(const_in, DMA)

            @block.tensor
            def _(pe):
                m = 0
                for t in range(T0, NT):
                    L = (t + 1) * P
                    for h in range(IDX_H):
                        r = h % 4
                        pr = slice(32 * r, 32 * r + 32)
                        if m >= 4:
                            pe.wait_ge(relu, START + m - 3)
                        for c in range(0, L, COL):
                            w = min(COL, L - c)
                            mm = pe.matmul(acc[:, r, c // COL, 0:w], B["iqT"][pr, h // 4, t * P:(t + 1) * P], B["ikT"][pr, c:c + w],
                                           start=True, stop=True, tile_position=(32 * r, 0))
                        mm.then_inc(made, 1)
                        m += 1

            @block.scalar
            def _(act):
                m = 0
                for t in range(T0, NT):
                    L = (t + 1) * P
                    for h in range(IDX_H):
                        act.wait_ge(made, START + m + 1)
                        if m >= 2:
                            act.wait_ge(summed, START + m - 1)
                        act.activation(rl[:, m % 2, 0:L], acc[:, h % 4, :, :].rearrange("p a n -> p (a n)")[:, 0:L], ACT.Relu,
                                       scale=float(IDX_D) ** -0.5).then_inc(relu, 1)
                        m += 1

            @block.vector
            def _(dve):
                dve.wait_ge(const_in, START + DMA)
                m, st = 0, 0
                for t in range(T0, NT):
                    L = (t + 1) * P
                    x, q = sc[t - T0], t - T0
                    for h in range(IDX_H):
                        dve.wait_ge(relu, START + m + 1)
                        iw = B["iw"][:, t, h:h + 1]
                        if h == 0:
                            dve.tensor_scalar(x[:, :], rl[:, m % 2, 0:L], iw, None, ALU.mult).then_inc(summed, 1)
                        else:
                            dve.wait_ge(summed, START + m)
                            dve.scalar_tensor_tensor(x[:, :], rl[:, m % 2, 0:L], iw, x[:, :], ALU.mult, ALU.add).then_inc(summed, 1)
                        m += 1
                    dve.wait_ge(summed, START + m)
                    dve.tensor_reduce(B["lo"][:, q:q + 1], x[:, :], X, ALU.min).then_inc(step, 1)
                    dve.tensor_reduce(B["hi"][:, q:q + 1], x[:, :], X, ALU.max).then_inc(step, 1)
                    st += 2
                    dve.wait_ge(step, START + st)
                    dve.tensor_tensor(x[:, t * P:L], x[:, t * P:L], causal[:, :], ALU.add).then_inc(step, 1)
                    st += 1
                dve.wait_ge(step, START + st)


def dsa_search(ph, B, sc):
    junk = ph.sb("junk", [P, 2, SEQ])
    mid, cnt, w = ph.sb("mid", [P, NS]), ph.sb("cnt", [P, NS]), ph.sb("w", [P, NS])
    ge, lt = ph.sb("ge", [P, NS], U8), ph.sb("lt", [P, NS], U8)
    step, passed = ph.sem("step"), ph.sem("passed")
    lo, hi = B["lo"], B["hi"]
    PRE, PER = 8, 6 + NS
    def search(dve):
        s = Steps(dve, step, 0, PRE)
        s(dve.tensor_tensor(w[:, :], hi[:, :], lo[:, :], ALU.subtract))
        s(dve.scalar_tensor_tensor(cnt[:, :], lo[:, :], -1.0, lo[:, :], ALU.mult, ALU.max))
        s(dve.tensor_scalar(cnt[:, :], cnt[:, :], 1e-6, 1e-35, ALU.mult, ALU.add))
        s(dve.tensor_tensor(w[:, :], w[:, :], cnt[:, :], ALU.add))
        s(dve.tensor_tensor(lo[:, :], lo[:, :], w[:, :], ALU.subtract))
        s(dve.tensor_tensor(mid[:, :], lo[:, :], hi[:, :], ALU.add))
        s(dve.tensor_scalar(mid[:, :], mid[:, :], 0.5, None, ALU.mult))
        s(dve.memset(cnt[:, :], 0.0))
        s.end()
        with dve.Fori(0, BISECT) as i:
            s = Steps(dve, step, 0, PER)
            s.base = PRE + i * PER
            for q in range(NS):
                L = (q + T0 + 1) * P
                s(dve.tensor_scalar(junk[:, q % 2, 0:L], sc[q][:, :], mid[:, q:q + 1], 0.0, ALU.is_gt, ALU.add, accum_out=cnt[:, q:q + 1]))
            s(dve.tensor_scalar(ge[:, :], cnt[:, :], float(TOPK), None, ALU.is_ge))
            s(dve.tensor_scalar(lt[:, :], cnt[:, :], float(TOPK), None, ALU.is_lt))
            s.settle(passed)
            s(dve.copy_predicated(lo[:, :], ge[:, :], mid[:, :]))
            s.settle(passed)
            s(dve.copy_predicated(hi[:, :], lt[:, :], mid[:, :]))
            s(dve.tensor_tensor(mid[:, :], lo[:, :], hi[:, :], ALU.add))
            s(dve.tensor_scalar(mid[:, :], mid[:, :], 0.5, None, ALU.mult))
            s.end()
    return search


def dsa_attend(nc, A, S, B, sc):
    with Phase(nc, "datt") as ph:
        ident = ph.sb("ident", [P, P])
        causal = ph.sb("causal", [P, P])
        ones = ph.sb("ones", [P, SEQ])
        gt, cand, pre = ph.sb("gt", [P, SEQ]), ph.sb("cand", [P, SEQ]), ph.sb("pre", [P, SEQ])
        mask = ph.sb("mask", [P, 2, SEQ])
        need = ph.sb("need", [P, 1])
        att = ph.sb("att", [P, 2, SEQ])
        nm, l = ph.sb("nm", [P, 2]), ph.sb("l", [P, 4])
        pT = ph.sb("pT", [P, 2, 4, P])
        o = ph.sb("o", [P, 2, 4, HD])
        acc = ph.ps("acc", [P, 2, 2, COL])
        tp = ph.ps("tp", [P, 2, 4, P])
        po = ph.ps("po", [P, 2, 512])
        (const_in, step, made, nm_ready, expd, turned, pT_ready, o_made, o_read, row_done) = (
            ph.sem(n) for n in "const_in step made nm_ready expd turned pT_ready o_made o_read row_done".split())
        stored = [ph.sem("stored0"), ph.sem("stored1")]
        groups = []
        for t in range(NT):
            for h in range(DSA_H):
                for b0 in range(0, t + 1, 4):
                    groups.append((t, h, b0, min(4, t + 1 - b0)))
        with ph.block() as block:
            @block.sync
            def _(sp):
                sp.dma_start(ident[:, :], A["ident"]).then_inc(const_in, DMA)
                sp.dma_start(causal[:, :], A["causal_ts"]).then_inc(const_in, DMA)
                for t in range(NT):
                    sp.wait_ge(row_done, START + DSA_H * (t + 1))
                    sp.dma_start(S["y2"][t * P:(t + 1) * P, RW:RW + 256], o[:, t % 2, :, :]).then_inc(stored[t % 2], DMA)
                for j in range(2):
                    sp.wait_ge(stored[j], START + NT // 2 * DMA)

            @block.tensor
            def _(pe):
                pe.wait_ge(const_in, START + 2 * DMA)

                def scores(m):
                    t, h = m // DSA_H, m % DSA_H
                    L, r = (t + 1) * P, h % 2
                    pr = slice(64 * r, 64 * r + 64)
                    if m >= 2:
                        pe.wait_ge(nm_ready, START + m - 1)
                    for c in range(0, L, COL):
                        w = min(COL, L - c)
                        mm = pe.matmul(acc[:, r, c // COL, 0:w], B["qT"][pr, h // 2, t * P:(t + 1) * P], B["kT"][pr, c:c + w], start=True, stop=True)
                    mm.then_inc(made, 1)

                def turn(k):
                    t, h, b0, nb = groups[k]
                    pe.wait_ge(expd, START + t * DSA_H + h + 1)
                    if k >= 2:
                        pe.wait_ge(pT_ready, START + k - 1)
                    for b in range(nb):
                        mm = pe.transpose(tp[:, k % 2, b, :], att[:, h % 2, (b0 + b) * P:(b0 + b + 1) * P], ident[:, :])
                    mm.then_inc(turned, 1)

                def values(k):
                    t, h, b0, nb = groups[k]
                    m = t * DSA_H + h
                    pe.wait_ge(pT_ready, START + k + 1)
                    if b0 == 0 and m >= 2:
                        pe.wait_ge(o_read, START + m - 1)
                    for b in range(nb):
                        mm = pe.matmul(po[:, m % 2, 0:HD], pT[:, k % 2, b, :], B["v"][:, b0 + b, :], start=b0 + b == 0, stop=b0 + b == t)
                    if b0 + nb == t + 1:
                        mm.then_inc(o_made, 1)

                scores(0)
                k = 0
                for m in range(NT * DSA_H):
                    if m + 1 < NT * DSA_H:
                        scores(m + 1)
                    while k < len(groups) and groups[k][0] * DSA_H + groups[k][1] == m:
                        turn(k)
                        if k >= 1:
                            values(k - 1)
                        k += 1
                values(k - 1)

            @block.vector
            def _(dve):
                n_steps = [0]

                def s(ins):
                    n_steps[0] += 1
                    ins.then_inc(step, 1)
                    dve.wait_ge(step, START + n_steps[0])

                s(dve.memset(ones[:, :], 1.0))
                dve.wait_ge(const_in, START + 2 * DMA)

                def row_out(m):
                    t, h = m // DSA_H, m % DSA_H
                    dve.wait_ge(o_made, START + m + 1)
                    if h == 0 and t >= 2:
                        dve.wait_ge(stored[t % 2], START + t // 2 * DMA)
                    s(dve.reciprocal(l[:, m % 4:m % 4 + 1], l[:, m % 4:m % 4 + 1]))
                    s(dve.scalar_tensor_tensor(o[:, t % 2, h, :], po[:, m % 2, 0:HD], l[:, m % 4:m % 4 + 1],
                                               B["g"][:, t, h * HD:(h + 1) * HD], ALU.mult, ALU.mult))
                    dve.sem_inc(o_read, 1)
                    dve.sem_inc(row_done, 1)

                def choose(t):
                    L, mk = (t + 1) * P, mask[:, t % 2, :]
                    if t < T0:
                        if t > 0:
                            s(dve.memset(mk[:, 0:t * P], 0.0))
                        s(dve.tensor_copy(mk[:, t * P:L], causal[:, :]))
                        return
                    q = t - T0
                    x, lo, hi = sc[q], B["lo"][:, q:q + 1], B["hi"][:, q:q + 1]
                    s(dve.tensor_scalar(gt[:, 0:L], x[:, :], hi, 0.0, ALU.is_gt, ALU.add, accum_out=need[:, :]))
                    s(dve.tensor_scalar(need[:, :], need[:, :], -1.0, float(TOPK), ALU.mult, ALU.add))
                    s(dve.scalar_tensor_tensor(cand[:, 0:L], x[:, :], lo, gt[:, 0:L], ALU.is_gt, ALU.subtract))
                    s(dve.tensor_tensor_scan(pre[:, 0:L], ones[:, 0:L], cand[:, 0:L], 0.0, ALU.mult, ALU.add))
                    s(dve.scalar_tensor_tensor(pre[:, 0:L], pre[:, 0:L], need[:, 0:1], cand[:, 0:L], ALU.is_le, ALU.mult))
                    s(dve.tensor_tensor(pre[:, 0:L], pre[:, 0:L], gt[:, 0:L], ALU.add))
                    s(dve.tensor_scalar(mk[:, 0:L], pre[:, 0:L], -1.0, BIG, ALU.add, ALU.mult))

                for m in range(NT * DSA_H):
                    t, h = m // DSA_H, m % DSA_H
                    L = (t + 1) * P
                    if h == 0:
                        choose(t)
                    dve.wait_ge(made, START + m + 1)
                    if m >= 2:
                        dve.wait_ge(turned, START + sum(1 for g in groups if g[0] * DSA_H + g[1] <= m - 2))
                    s(dve.scalar_tensor_tensor(att[:, h % 2, 0:L], acc[:, h % 2, :, :].rearrange("p a n -> p (a n)")[:, 0:L],
                                               float(HD) ** -0.5, mask[:, t % 2, 0:L], ALU.mult, ALU.add))
                    if m >= 2:
                        dve.wait_ge(expd, START + m - 1)
                    s(dve.tensor_reduce(nm[:, h % 2:h % 2 + 1], att[:, h % 2, 0:L], X, ALU.max, negate=True))
                    dve.sem_inc(nm_ready, 1)
                    if m >= 2:
                        row_out(m - 2)
                row_out(NT * DSA_H - 2)
                row_out(NT * DSA_H - 1)

            @block.scalar
            def _(act):
                k = 0
                for m in range(NT * DSA_H + 1):
                    if m < NT * DSA_H:
                        t, h = m // DSA_H, m % DSA_H
                        act.wait_ge(nm_ready, START + m + 1)
                        if m >= 4:
                            act.wait_ge(o_read, START + m - 3)
                        act.activation(att[:, h % 2, 0:(t + 1) * P], att[:, h % 2, 0:(t + 1) * P], ACT.Exp, bias=nm[:, h % 2:h % 2 + 1],
                                       accum_out=l[:, m % 4:m % 4 + 1]).then_inc(expd, 1)
                    while k < len(groups) and groups[k][0] * DSA_H + groups[k][1] == m - 1:
                        nb = groups[k][3]
                        act.wait_ge(turned, START + k + 1)
                        act.activation(pT[:, k % 2, 0:nb, :], tp[:, k % 2, 0:nb, :], ACT.Copy).then_inc(pT_ready, 1)
                        k += 1


def dil_rows(ap, gi, n, cols):
    if RATES[gi] == 1:
        return [(slice(0, P), ap[bass.ds(n * P, P), cols])]
    v = ap[:, cols]
    if RATES[gi] == 4:
        return [(slice(0, P), v.rearrange("(b j r) c -> b r j c", r=4, j=P)[n % 2, n // 2])]
    v = v.rearrange("(j r) c -> r j c", r=16)
    return [(slice(64 * m, 64 * m + 64), v[2 * n + m]) for m in range(2)]


def dil_cols(gi, n):
    if RATES[gi] == 1:
        return lambda t: t[:, n * P:(n + 1) * P].unsqueeze(1)
    if RATES[gi] == 4:
        return lambda t: t.rearrange("p (b j r) -> p b r j", r=4, j=P)[:, n % 2, n // 2, :].unsqueeze(1)
    return lambda t: t.rearrange("p (j r) -> p r j", r=16)[:, 2 * n:2 * n + 2, :]


def dilated(nc, A, S, yT):
    NG = 3
    with Phase(nc, "dil") as ph:
        ident = ph.sb("ident", [P, P])
        masks = ph.sb("masks", [P, 3, 2 * P])
        cs = ph.sb("cs", [P, NG * NT, 2, 8])
        z = ph.sb("z", [P, 4, 4, P])
        vp = ph.sb("vp", [P, 3, P])
        kT = ph.sb("kT", [P, 2, P])
        qT = ph.sb("qT", [P, 2, P])
        tmp = ph.sb("tmp", [P, 4, 32])
        att = ph.sb("att", [P, 2, 2, 2 * P])
        nm, l = ph.sb("nm", [P, 2, 2]), ph.sb("l", [P, 2, 2])
        pT = ph.sb("pT", [P, 4, P])
        og = ph.sb("og", [P, 3, P])
        MT, LT = ph.sb("MT", [P, NG, SEQ]), ph.sb("LT", [P, NG, SEQ])
        mx, sm = ph.sb("mx", [P, SEQ]), ph.sb("sm", [P, SEQ])
        pa = ph.ps("pa", [P, 2, 512])
        pt = ph.ps("pt", [P, 4, P])
        pq = ph.ps("pq", [P, 4, P])
        po = ph.ps("po", [P, 512])
        pz = ph.ps("pz", [P, 4, P])
        (const_in, step, roped, turned_qk, qk_ready, made, nm_ready, expd, turned_p, pT_ready, o_made, og_ready,
         turned_o, placed, gated, M_ready, E_ready, zeroed) = (ph.sem(n) for n in (
             "const_in step roped turned_qk qk_ready made nm_ready expd turned_p pT_ready o_made og_ready "
             "turned_o placed gated M_ready E_ready zeroed").split())
        in_ = [ph.sem(f"in{k}") for k in range(4)]
        tiles_ = [(gi, n) for gi in range(NG) for n in range(NT)]
        NM = len(tiles_)
        n_loads, loads_by = [0] * 4, []
        for m, (gi, n) in enumerate(tiles_):
            n_loads[m % 4] += 8 if gi == 2 else 4
            loads_by.append(n_loads[m % 4])
        has_prev = lambda gi, n: (gi == 0 and n > 0) or (gi == 1 and n % 2 == 1)
        by_head = lambda t: t.rearrange("p (h c) -> p h c", h=2)

        def trips(scores, values):
            scores(0)
            for m in range(NM):
                if m + 1 < NM:
                    scores(m + 1)
                values(m)

        with ph.block() as block:
            @block.sync
            def _(sp):
                sp.dma_start(ident[:, :], A["ident"]).then_inc(const_in, DMA)
                sp.dma_start(masks[:, :, :], A["dil_masks"]).then_inc(const_in, DMA)
                sp.dma_start(cs[:, :, :, :], A["rope_dil"]).then_inc(const_in, DMA)
                for m, (gi, n) in enumerate(tiles_):
                    if m >= 4:
                        sp.wait_ge(placed, START + m - 3)
                    for q in range(4):
                        c = DIL0 + 384 * q + P * gi
                        for pr, src in dil_rows(S["z2"][1:SEQ + 1, :], gi, n, slice(c, c + P)):
                            sp.dma_start(z[pr, m % 4, q, :], src).then_inc(in_[m % 4], DMA)

            @block.vector
            def _(dve):
                n_steps = [0]

                def s(ins):
                    n_steps[0] += 1
                    ins.then_inc(step, 1)
                    dve.wait_ge(step, START + n_steps[0])

                def scores(m):
                    gi, n = tiles_[m]
                    b = m % 4
                    dve.wait_ge(in_[b], START + loads_by[m] * DMA)
                    x = z[:, b, 0:2, :].rearrange("p a (h c) -> p (a h) c", h=2)
                    tv = [tmp[:, q, :].rearrange("p (h c) -> p h c", h=4) for q in range(4)]
                    cos, sin = (bc_mid(cs[:, m, q, :], 4) for q in range(2))
                    rope(s, dve, x, x[:, :, 0:8], x[:, :, 8:16], cos, sin, tv[0:2], tv[2:4])
                    dve.sem_inc(roped, 1)
                    s(dve.tensor_copy(vp[:, m % 3, :], z[:, b, 2, :]))
                    mk = masks[:, 0 if has_prev(gi, n) else (2 if gi == 2 else 1), :]
                    dve.wait_ge(made, START + m + 1)
                    for h in range(2):
                        s(dve.scalar_tensor_tensor(att[:, m % 2, h, :], pa[:, h, 0:2 * P], float(HD) ** -0.5, mk, ALU.mult, ALU.add))
                    s(dve.tensor_reduce(nm[:, m % 2, :], att[:, m % 2, :, :], X, ALU.max, negate=True))
                    dve.sem_inc(nm_ready, 1)

                def values(m):
                    b = m % 4
                    if m >= 1:
                        dve.wait_ge(turned_o, START + m)
                    s(dve.tensor_scalar(by_head(og[:, 1, :]), bc_last(nm[:, m % 2, :], HD), -1.0, None, ALU.mult))
                    dve.wait_ge(expd, START + m + 1)
                    s(dve.tensor_copy(by_head(og[:, 2, :]), bc_last(l[:, m % 2, :], HD)))
                    dve.wait_ge(gated, START + m + 1)
                    dve.wait_ge(o_made, START + m + 1)
                    s(dve.tensor_tensor(og[:, 0, :], po[:, 0:P], z[:, b, 3, :], ALU.mult))
                    dve.sem_inc(og_ready, 1)

                s(dve.memset(kT[:, :, :], 0.0))
                s(dve.memset(vp[:, :, :], 0.0))
                dve.sem_inc(zeroed, 1)
                dve.wait_ge(const_in, START + 3 * DMA)
                trips(scores, values)
                dve.wait_ge(placed, START + NM)
                s(dve.tensor_tensor(mx[:, :], MT[:, 0, :], MT[:, 1, :], ALU.max))
                s(dve.tensor_tensor(mx[:, :], mx[:, :], MT[:, 2, :], ALU.max))
                for q in range(NG):
                    s(dve.tensor_tensor(MT[:, q, :], MT[:, q, :], mx[:, :], ALU.subtract))
                    dve.sem_inc(M_ready, 1)
                for q in range(NG):
                    dve.wait_ge(E_ready, START + q + 1)
                    s(dve.tensor_tensor(LT[:, q, :], LT[:, q, :], MT[:, q, :], ALU.mult))
                s(dve.tensor_tensor(sm[:, :], LT[:, 0, :], LT[:, 1, :], ALU.add))
                s(dve.tensor_tensor(sm[:, :], sm[:, :], LT[:, 2, :], ALU.add))
                s(dve.reciprocal(sm[:, :], sm[:, :]))
                for q in range(NG):
                    s(dve.tensor_tensor(MT[:, q, :], MT[:, q, :], sm[:, :], ALU.mult))
                    s(dve.tensor_tensor(yT[:, 5 + q, :], yT[:, 5 + q, :], MT[:, q, :], ALU.mult))

            @block.scalar
            def _(act):
                def scores(m):
                    act.wait_ge(turned_qk, START + m + 1)
                    act.activation(qT[:, m % 2, :], pq[:, 2 * (m % 2), :], ACT.Copy)
                    act.activation(kT[:, m % 2, :], pq[:, 2 * (m % 2) + 1, :], ACT.Copy).then_inc(qk_ready, 1)
                    act.wait_ge(in_[m % 4], START + loads_by[m] * DMA)
                    act.activation(z[:, m % 4, 3, :], z[:, m % 4, 3, :], ACT.Silu).then_inc(gated, 1)

                def values(m):
                    gi, n = tiles_[m]
                    act.wait_ge(nm_ready, START + m + 1)
                    for h in range(2):
                        ins = act.activation(att[:, m % 2, h, :], att[:, m % 2, h, :], ACT.Exp, bias=nm[:, m % 2, h:h + 1],
                                             accum_out=l[:, m % 2, h:h + 1])
                    ins.then_inc(expd, 1)
                    act.wait_ge(turned_p, START + m + 1)
                    act.activation(pT[:, :, :], pt[:, :, :], ACT.Copy).then_inc(pT_ready, 1)
                    act.wait_ge(turned_o, START + m + 1)
                    place = dil_cols(gi, n)
                    for q, dst in enumerate((yT[:, 5 + gi, :], MT[:, gi, :], LT[:, gi, :])):
                        dst = place(dst)
                        ins = act.activation(dst, pz[:, q, :].rearrange("p (a t) -> p a t", a=dst.shape[1]), ACT.Copy)
                    ins.then_inc(placed, 1)

                act.wait_ge(zeroed, START + 1)
                trips(scores, values)
                for q in range(NG):
                    act.wait_ge(M_ready, START + q + 1)
                    act.activation(MT[:, q, :], MT[:, q, :], ACT.Exp).then_inc(E_ready, 1)

            @block.tensor
            def _(pe):
                def scores(m):
                    j = m % 2
                    pe.wait_ge(roped, START + m + 1)
                    for q in range(2):
                        mm = pe.transpose(pq[:, 2 * j + q, :], z[:, m % 4, q, :], ident[:, :])
                    mm.then_inc(turned_qk, 1)
                    pe.wait_ge(qk_ready, START + m + 1)
                    if m >= 1:
                        pe.wait_ge(nm_ready, START + m)
                    for h in range(2):
                        pr = slice(64 * h, 64 * h + 64)
                        pe.matmul(pa[:, h, 0:P], qT[pr, j, :], kT[pr, 1 - j, :], start=True, stop=True)
                        mm = pe.matmul(pa[:, h, P:2 * P], qT[pr, j, :], kT[pr, j, :], start=True, stop=True)
                    mm.then_inc(made, 1)

                def values(m):
                    pe.wait_ge(expd, START + m + 1)
                    for h in range(2):
                        for b in range(2):
                            mm = pe.transpose(pt[:, 2 * h + b, :], att[:, m % 2, h, b * P:(b + 1) * P], ident[:, :])
                    mm.then_inc(turned_p, 1)
                    pe.wait_ge(pT_ready, START + m + 1)
                    for h in range(2):
                        at = slice(h * HD, (h + 1) * HD)
                        pe.matmul(po[:, at], pT[:, 2 * h, :], vp[:, (m - 1) % 3, at], start=True, stop=False)
                        mm = pe.matmul(po[:, at], pT[:, 2 * h + 1, :], vp[:, m % 3, at], start=False, stop=True)
                    mm.then_inc(o_made, 1)
                    pe.wait_ge(og_ready, START + m + 1)
                    if m >= 1:
                        pe.wait_ge(placed, START + m)
                    for q in range(3):
                        mm = pe.transpose(pz[:, q, :], og[:, q, :], ident[:, :])
                    mm.then_inc(turned_o, 1)

                pe.wait_ge(const_in, START + 3 * DMA)
                trips(scores, values)


def turn_rows(nc, A, S, yT):
    NC = 5
    with Phase(nc, "turn") as ph:
        ident = ph.sb("ident", [P, P])
        x = ph.sb("x", [P, 2, NC * P])
        pT = ph.ps("pT", [P, 2, 8, P])
        const_in, in_, turned, placed = ph.sem("const_in"), [ph.sem("in0"), ph.sem("in1")], ph.sem("turned"), [ph.sem("placed0"), ph.sem("placed1")]
        with ph.block() as block:
            @block.sync
            def _(sp):
                sp.dma_start(ident[:, :], A["ident"]).then_inc(const_in, DMA)
                with sp.Fori(0, NT // 2) as i:
                    for j in range(2):
                        sp.wait_ge(placed[j], START + i)
                        sp.dma_start(x[:, j, :], S["y2"][bass.ds((2 * i + j) * P, P), :]).then_inc(in_[j], DMA)

            @block.tensor
            def _(pe):
                pe.wait_ge(const_in, START + DMA)
                with pe.Fori(0, NT // 2) as i:
                    for j in range(2):
                        pe.wait_ge(in_[j], START + (i + 1) * DMA)
                        for q in range(NC):
                            mm = pe.transpose(pT[:, j, q, :], x[:, j, q * P:(q + 1) * P], ident[:, :])
                        mm.then_inc(turned, 1)

            @block.scalar
            def _(act):
                with act.Fori(0, NT // 2) as i:
                    for j in range(2):
                        act.wait_ge(turned, START + 2 * i + j + 1)
                        act.activation(yT[:, 0:NC, bass.ds((2 * i + j) * P, P)], pT[:, j, 0:NC, :], ACT.Copy).then_inc(placed[j], 1)


def add_rows(nc, name, x, t, gate):
    DEEP = 4
    with Phase(nc, name) as ph:
        xs, ts, gs = ph.sb("xs", [P, DEEP, D]), ph.sb("ts", [P, DEEP, D]), ph.sb("gs", [P, DEEP, D])
        in_, sig, step, stored = [ph.sem(f"in{j}") for j in range(DEEP)], ph.sem("sig"), ph.sem("step"), [ph.sem(f"stored{j}") for j in range(DEEP)]
        done = ph.sem("done")
        n_in = 3
        with ph.block() as block:
            @block.sync
            def _(sp):
                with sp.Fori(0, NT // DEEP) as i:
                    for j in range(DEEP):
                        sp.wait_ge(stored[j], START + i * DMA)
                        at = bass.ds((DEEP * i + j) * P, P)
                        sp.dma_start(xs[:, j, :], x[at, :]).then_inc(in_[j], DMA)
                        sp.dma_start(ts[:, j, :], t[at, :]).then_inc(in_[j], DMA)
                        sp.dma_start(gs[:, j, :], gate[at, :]).then_inc(in_[j], DMA)

            @block.vector
            def _(dve):
                with dve.Fori(0, NT // DEEP) as i:
                    for j in range(DEEP):
                        n = DEEP * i + j
                        dve.wait_ge(in_[j], START + (i + 1) * n_in * DMA)
                        dve.wait_ge(sig, START + n + 1)
                        dve.tensor_tensor(ts[:, j, :], ts[:, j, :], gs[:, j, :], ALU.mult).then_inc(step, 1)
                        dve.wait_ge(step, START + n + 1)
                        dve.tensor_tensor(xs[:, j, :], xs[:, j, :], ts[:, j, :], ALU.add).then_inc(done, 1)

            @block.scalar
            def _(act):
                with act.Fori(0, NT // DEEP) as i:
                    for j in range(DEEP):
                        n = DEEP * i + j
                        act.wait_ge(in_[j], START + (i + 1) * n_in * DMA)
                        act.activation(gs[:, j, :], gs[:, j, :], ACT.Sigmoid).then_inc(sig, 1)
                        act.wait_ge(done, START + n + 1)
                        act.dma_start(x[bass.ds(n * P, P), :], xs[:, j, :]).then_inc(stored[j], DMA)
                for j in range(DEEP):
                    act.wait_ge(stored[j], START + NT // DEEP * DMA)


def final_norm(nc, A, x, out):
    with Phase(nc, "final") as ph:
        g = ph.sb("g", [P, D])
        xs, sq = ph.sb("xs", [P, 2, D]), ph.sb("sq", [P, 2, D])
        ss = ph.sb("ss", [P, 2])
        const_in, in_, stored = ph.sem("const_in"), [ph.sem("in0"), ph.sem("in1")], [ph.sem("stored0"), ph.sem("stored1")]
        squares, mean, root, step, done = (ph.sem(n) for n in ("squares", "mean", "root", "step", "done"))
        with ph.block() as block:
            @block.sync
            def _(sp):
                sp.dma_start(g[:, :], rows_to_all(A["final_norm_g_2"])).then_inc(const_in, DMA)
                with sp.Fori(0, NT // 2) as i:
                    for j in range(2):
                        sp.wait_ge(stored[j], START + i * DMA)
                        sp.dma_start(xs[:, j, :], x[bass.ds((2 * i + j) * P, P), :]).then_inc(in_[j], DMA)

            @block.scalar
            def _(act):
                with act.Fori(0, NT // 2) as i:
                    for j in range(2):
                        n = 2 * i + j
                        act.wait_ge(in_[j], START + (i + 1) * DMA)
                        act.activation(sq[:, j, :], xs[:, j, :], ACT.Square, accum_out=ss[:, j:j + 1]).then_inc(squares, 1)
                        act.wait_ge(mean, START + n + 1)
                        act.activation(ss[:, j:j + 1], ss[:, j:j + 1], ACT.Sqrt).then_inc(root, 1)
                        act.wait_ge(done, START + n + 1)
                        act.dma_start(out[bass.ds(n * P, P), :], xs[:, j, :]).then_inc(stored[j], DMA)
                for j in range(2):
                    act.wait_ge(stored[j], START + NT // 2 * DMA)

            @block.vector
            def _(dve):
                dve.wait_ge(const_in, START + DMA)
                with dve.Fori(0, NT // 2) as i:
                    for j in range(2):
                        n = 2 * i + j
                        s = Steps(dve, step, n, 1)
                        dve.wait_ge(squares, START + n + 1)
                        dve.tensor_scalar(ss[:, j:j + 1], ss[:, j:j + 1], 1.0 / D, NORM_EPS, ALU.mult, ALU.add).then_inc(mean, 1)
                        dve.wait_ge(root, START + n + 1)
                        s(dve.reciprocal(ss[:, j:j + 1], ss[:, j:j + 1]))
                        dve.scalar_tensor_tensor(xs[:, j, :], xs[:, j, :], ss[:, j:j + 1], g[:, :], ALU.mult, ALU.mult).then_inc(done, 1)


def layer(nc, A, S, l):
    z2 = S["z2"][1:SEQ + 1, :]
    with ExitStack() as st:
        hT = st.enter_context(nc.sbuf_tensor("hTl", [P, KC, SEQ], F32))
        norm_transpose(nc, "nl", S["x"], NT, hT, 0, A["norm_g_2"][l], None, A, NORM_EPS, False)
        dsa_cols = [(c, min(COL, DIL0 - c)) for c in range(DSA0, DIL0, COL)]
        product(nc, "win2a", hT, NT, 0, A["w_in_2"][l], KC, [(c, w, tiles(z2, slice(c, c + w))) for c, w in dsa_cols], None)
        sb = lambda n, sh: st.enter_context(nc.sbuf_tensor(n, sh, F32))
        B = {"qT": sb("d_qT", [P, 2, SEQ]), "kT": sb("d_kT", [P, SEQ]), "iqT": sb("d_iqT", [P, 2, SEQ]), "ikT": sb("d_ikT", [P, SEQ]),
             "v": sb("d_v", [P, NT, HD]), "iw": sb("d_iw", [P, NT, IDX_H]), "g": sb("d_g", [P, NT, 256]),
             "lo": sb("d_lo", [P, NS]), "hi": sb("d_hi", [P, NS])}
        dsa_prep(nc, A, S, B)
        sc = [sb(f"d_sc{t}", [P, (t + 1) * P]) for t in range(T0, NT)]
        dsa_scores(nc, A, S, B, sc)
        pairs = DSA0 // COL
        product(nc, "win2b", hT, NT, 0, A["w_in_2"][l], KC, [(pairs * COL, DSA0 - pairs * COL, tiles(z2, slice(pairs * COL, DSA0)))],
                (pairs, lambda i, j: i * COL + j * DIL0, lambda i, j: tiles(z2, bass.ds(i * COL + j * DIL0, COL))),
                beside=lambda ph: dsa_search(ph, B, sc))
        dsa_attend(nc, A, S, B, sc)
    rwkv(nc, A, S, l)
    with nc.sbuf_tensor("yTl", [P, KC, SEQ], F32) as yT:
        dilated(nc, A, S, yT)
        turn_rows(nc, A, S, yT)
        product(nc, "wout2", yT, NT, 0, A["w_out_2"][l], KC, [(c, COL, tiles(S["t1"], slice(c, c + COL))) for c in (0, COL)], None)
    with nc.sbuf_tensor("hTp", [P, KC, SEQ], F32) as hT:
        norm_transpose(nc, "np", S["x"], NT, hT, 0, A["ple_norm_g_2"][l], None, A, NORM_EPS, False, addend=S["t1"])
        product(nc, "wgate", hT, NT, 0, A["ple_w_gate_2"][l], KC, [(c, COL, tiles(S["xa"], slice(c, c + COL))) for c in (0, COL)], None)
    with nc.sbuf_tensor("pT", [P, 2, SEQ], F32) as pT:
        load_p(nc, A, pT, l)
        product(nc, "wproj", pT, NT, 0, A["ple_w_proj_2"][l], 2, [(c, COL, tiles(S["t1"], slice(c, c + COL))) for c in (0, COL)], None)
    add_rows(nc, "addp", S["x"], S["t1"], S["xa"])


def load_p(nc, A, pT, l):
    with Phase(nc, "loadp") as ph:
        loaded = ph.sem("loaded")
        with ph.block() as block:
            @block.sync
            def _(sp):
                sp.dma_start(pT[:, :, :], A["pT_2"][l].rearrange("(k p) t -> p k t", p=P)).then_inc(loaded, DMA)
                sp.wait_ge(loaded, START + DMA)


def second_block(nc, A, S, out):
    zero_rows(nc, S, "z2pad", [S["z2"][0:1, :]])
    with nc.Fori(0, LAYERS) as l:
        layer(nc, A, S, l)
    final_norm(nc, A, S["x"], out)


def constants_2():
    f = np.float32
    s, t = np.arange(P)[:, None], np.arange(P)[None, :]
    same = s // CH == t // CH
    c = {"id64": np.tile(np.eye(HD, dtype=f), (2, 1)), "tri64": ((s <= t) & same).astype(f), "blk64": same.astype(f)}
    strict, incl = (s < t) & same, (s <= t) & same
    c["rw_masks"] = np.stack([strict, incl, strict, incl], 1).astype(f)
    pair = (s // 2 == t // 2)
    c["rw_first"] = np.stack([pair & (s > t), pair & (s < t)], 1).astype(f)
    c["rw_levels"] = np.stack([(s // (2 * b) == t // (2 * b)) & (s % (2 * b) < b) & (t % (2 * b) >= b) for b in (2, 4, 8, 16, 32)], 1).astype(f)
    c["causal_ts"] = np.where(t <= s, 0, -BIG).astype(f)
    kj = np.arange(2 * P)[None, :]
    dist = s + P - kj
    band = (dist >= 0) & (dist <= P)
    own = (kj >= P) & (dist >= 0)
    c["dil_masks"] = np.stack([np.where(m, 0, -BIG) for m in (band, own, own & ((kj - P) // 64 == s // 64))], 1).astype(f)

    def table(pos, rot):
        half = rot // 2
        inv = (f(500000.0) ** (-np.arange(half, dtype=f) / f(half))).astype(f)
        ang = pos.astype(f)[..., None] * inv
        return np.stack([np.cos(ang), np.sin(ang)], -2).astype(f)
    pos = np.arange(SEQ).reshape(NT, P)
    c["rope_dsa"] = np.ascontiguousarray(np.concatenate([table(pos, 16), table(pos, 8)], -1).transpose(1, 0, 2, 3))
    orders = []
    for r in RATES:
        if r == 1:
            o = pos
        elif r == 4:
            o = np.stack([(np.arange(P) + (n % 2) * P) * 4 + n // 2 for n in range(NT)])
        else:
            o = np.stack([np.concatenate([np.arange(64) * 16 + 2 * n + m for m in range(2)]) for n in range(NT)])
        orders.append(o)
    c["rope_dil"] = np.ascontiguousarray(table(np.concatenate(orders), 16).transpose(1, 0, 2, 3))
    return c


def scratch_2(nc):
    shapes = {"z2": (SEQ + 1, IN2), "y2": (SEQ, RW + 256)}
    return {k: nc.dram_tensor(f"s_{k}", s, F32, kind="Internal").ap() for k, s in shapes.items()}


def build_program(nc, A, out):
    S = scratch(nc)
    S.update(scratch_2(nc))
    first_block(nc, A, S)
    second_block(nc, A, S, out)


_INS = ("x ctx w_ada b_ada w_in ln_v_g ln_v_b conv_qk b_gates hn_g w_out ln1_g ln1_b w1 w2 b2 ln2_g ln2_b "
        "norm_g_2 w_in_2 tshift_mu_2 rwkv_w0_2 rwkv_w_up_2 rwkv_a0_2 rwkv_a_up_2 rwkv_k_k_2 rwkv_k_a_2 rwkv_r_k_2 "
        "rwkv_ln_g_2 rwkv_ln_b_2 w_out_2 ple_norm_g_2 ple_w_gate_2 ple_w_proj_2 final_norm_g_2").split()


def kernel(**inputs):
    import concourse.bacc as bacc
    from concourse.bass_utils import run_bass_kernel_spmd

    arrays = {n: np.ascontiguousarray(inputs[n]) for n in _INS}
    arrays["pT_2"] = np.ascontiguousarray(np.asarray(inputs["p_2"])[:, 0].transpose(0, 2, 1))
    arrays.update(layouts(inputs))
    arrays.update(constants())
    arrays.update(constants_2())
    nc = bacc.Bacc("TRN2", target_bir_lowering=False, num_devices=1)
    A = {n: nc.dram_tensor(f"in_{n}", a.shape, mybir.dt.from_np(a.dtype), kind="ExternalInput").ap() for n, a in arrays.items()}
    out = nc.dram_tensor("out_y", (SEQ, D), F32, kind="ExternalOutput").ap()
    build_program(nc, A, out)
    r = run_bass_kernel_spmd(nc, [{f"in_{n}": a for n, a in arrays.items()}], core_ids=[0])
    return r.results[0]["out_y"].reshape(1, SEQ, D)
```
